# Optimizing a Trainium2 kernel written in Bass

```python
import math
import jax, jax.numpy as jnp
from jax import lax
import numpy as np

D_MODEL = 1024
BATCH = 1
SEQ = 1024
DEPTH = 1

D_ATT = D_MODEL // 2
D_SSM = D_MODEL - D_ATT
HEAD_DIM = 64
ATT_HEADS = D_ATT // HEAD_DIM
ATT_KV_HEADS = 2
GQA = ATT_HEADS // ATT_KV_HEADS
KV_DIM = ATT_KV_HEADS * HEAD_DIM
L_CMP = 32
CMP_STRIDE = 16
L_SLC = 64
TOP_N = 8
WIN = 256
QBLK = 128
FORCE_SCORE = 1.0e4
NEG_INF = -1.0e30
SSM_HEAD_DIM = 64
SSM_HEADS = D_SSM // SSM_HEAD_DIM
SSM_GROUPS = 2
HEADS_PER_GROUP = SSM_HEADS // SSM_GROUPS
D_STATE = 128
CONV_W = 4
SSD_CHUNK = 128
D_CONV = D_SSM + 2 * SSM_GROUPS * D_STATE
N_EGROUPS = 4
EXPERTS_PER_GROUP = 4
N_EXPERTS = N_EGROUPS * EXPERTS_PER_GROUP
TOP_K_INNER = 2
D_EXPERT = 256
SPLIT_SIZES = (D_ATT, KV_DIM, KV_DIM, KV_DIM, KV_DIM, KV_DIM, KV_DIM, ATT_HEADS * 3, D_SSM, D_CONV, SSM_HEADS)
D_IN = sum(SPLIT_SIZES)
EPS = 1e-6

kernel_name = "nsa_ssd_hymba_hiermoe_trunk"

def rms_norm(x, w):
    xf = x.astype(jnp.float32)
    y = xf * lax.rsqrt(jnp.mean(xf * xf, axis=-1, keepdims=True) + EPS)
    return (y * w.astype(jnp.float32)).astype(x.dtype)

def masked_softmax(s, mask):
    s = jnp.where(mask, s.astype(jnp.float32), NEG_INF)
    p = jax.nn.softmax(s, axis=-1)
    return jnp.where(mask, p, 0.0)

def alibi_slopes(n):
    return np.exp2(-8.0 * (np.arange(n) + 1) / n).astype(np.float32)

def nsa_mixer(q, k_c, v_c, k_s, v_s, k_w, v_w, gates, q_norm_w, k_norm_w, cmp_pe, cmp_w1, cmp_w2):
    Bn, S = q.shape[:2]
    dt = q.dtype
    q = rms_norm(q, q_norm_w)
    k_s = rms_norm(k_s, k_norm_w[1])
    k_w = rms_norm(k_w, k_norm_w[2])

    n_cmp = (S - L_CMP) // CMP_STRIDE + 1
    cmp_idx = np.arange(n_cmp)[:, None] * CMP_STRIDE + np.arange(L_CMP)[None, :]
    cmp_end = jnp.asarray(cmp_idx[:, -1], jnp.int32)

    def compress(kv, pe, w1, w2):
        blk = kv[:, cmp_idx] + pe[None, None, :, None, :]
        blk = blk.transpose(0, 1, 3, 2, 4).reshape(Bn, n_cmp, ATT_KV_HEADS, L_CMP * HEAD_DIM)
        return jax.nn.silu(blk @ w1) @ w2

    k_cmp = rms_norm(compress(k_c, cmp_pe[0], cmp_w1[0], cmp_w2[0]), k_norm_w[0])
    v_cmp = compress(v_c, cmp_pe[1], cmp_w1[1], cmp_w2[1])

    n_slc = S // L_SLC
    s0 = np.arange(n_slc) * L_SLC
    ov = np.clip(np.minimum(cmp_idx[:, -1:] + 1, s0[None] + L_SLC) - np.maximum(cmp_idx[:, :1], s0[None]), 0, None)
    ov = jnp.asarray(ov / L_CMP, jnp.float32)

    k_blk = k_s.reshape(Bn, n_slc, L_SLC, ATT_KV_HEADS, HEAD_DIM).transpose(0, 3, 1, 2, 4)
    v_blk = v_s.reshape(Bn, n_slc, L_SLC, ATT_KV_HEADS, HEAD_DIM).transpose(0, 3, 1, 2, 4)
    k_w_pad = jnp.pad(k_w, ((0, 0), (WIN, 0), (0, 0), (0, 0)))
    v_w_pad = jnp.pad(v_w, ((0, 0), (WIN, 0), (0, 0), (0, 0)))
    gate = jax.nn.sigmoid(gates.astype(jnp.float32)).astype(dt)
    slopes = alibi_slopes(ATT_HEADS).reshape(ATT_KV_HEADS, GQA)
    k_sel = min(TOP_N, n_slc)
    scale = HEAD_DIM ** -0.5
    qg = q.reshape(Bn, S, ATT_KV_HEADS, GQA, HEAD_DIM)
    gather_blocks = jax.vmap(jax.vmap(lambda a, i: a[i]))

    def block(c):
        q0 = c * QBLK
        t = q0 + jnp.arange(QBLK)
        qc = lax.dynamic_slice_in_dim(qg, q0, QBLK, 1) * scale

        s = jnp.einsum('bqkgd,bnkd->bkgqn', qc, k_cmp)
        dist = (t[:, None] - cmp_end[None, :]).astype(jnp.float32)
        s = s.astype(jnp.float32) - slopes[:, :, None, None] * dist
        p_cmp = masked_softmax(s, dist >= 0)
        o_cmp = jnp.einsum('bkgqn,bnkd->bqkgd', p_cmp.astype(dt), v_cmp)

        imp = jnp.einsum('bkgqn,nj->bkqj', p_cmp, ov)
        j = jnp.arange(n_slc)[None, :]
        cur = (t // L_SLC)[:, None]
        valid = j <= cur
        forced = (j == 0) | (j == cur) | (j == cur - 1)
        score = jnp.where(forced, FORCE_SCORE, jnp.where(valid, imp, -1.0))
        _, idx = lax.top_k(score, k_sel)
        ks = gather_blocks(k_blk, idx).reshape(Bn, ATT_KV_HEADS, QBLK, k_sel * L_SLC, HEAD_DIM)
        vs = gather_blocks(v_blk, idx).reshape(Bn, ATT_KV_HEADS, QBLK, k_sel * L_SLC, HEAD_DIM)
        pos = (idx[..., None] * L_SLC + jnp.arange(L_SLC)).reshape(Bn, ATT_KV_HEADS, QBLK, k_sel * L_SLC)
        dist = (t[:, None] - pos).astype(jnp.float32)
        s = jnp.einsum('bqkgd,bkqnd->bkgqn', qc, ks).astype(jnp.float32) \
            - slopes[None, :, :, None, None] * dist[:, :, None]
        p = masked_softmax(s, (dist >= 0)[:, :, None])
        o_slc = jnp.einsum('bkgqn,bkqnd->bqkgd', p.astype(dt), vs)

        kw = lax.dynamic_slice_in_dim(k_w_pad, q0, WIN + QBLK, 1)
        vw = lax.dynamic_slice_in_dim(v_w_pad, q0, WIN + QBLK, 1)
        spos = q0 - WIN + jnp.arange(WIN + QBLK)
        dist = (t[:, None] - spos[None, :]).astype(jnp.float32)
        mask = (dist >= 0) & (dist < WIN) & (spos[None, :] >= 0)
        s = jnp.einsum('bqkgd,bskd->bkgqs', qc, kw).astype(jnp.float32) - slopes[:, :, None, None] * dist
        p = masked_softmax(s, mask)
        o_win = jnp.einsum('bkgqs,bskd->bqkgd', p.astype(dt), vw)

        gc = lax.dynamic_slice_in_dim(gate, q0, QBLK, 1).reshape(Bn, QBLK, ATT_KV_HEADS, GQA, 3)
        o = gc[..., 0:1] * o_cmp + gc[..., 1:2] * o_slc + gc[..., 2:3] * o_win
        return o.reshape(Bn, QBLK, D_ATT)

    out = lax.map(block, jnp.arange(S // QBLK))
    return out.transpose(1, 0, 2, 3).reshape(Bn, S, D_ATT)

def segsum(a):
    T = a.shape[-1]
    x = jnp.broadcast_to(a[..., None], a.shape + (T,))
    x = jnp.where(np.tril(np.ones((T, T), bool), -1), x, 0.0)
    x = jnp.cumsum(x, axis=-2)
    return jnp.where(np.tril(np.ones((T, T), bool)), x, -jnp.inf)

def ssd_chunked(xs, dt, A, Bm, Cm):
    Bn, S, H, P = xs.shape
    nc = S // SSD_CHUNK
    f32 = jnp.float32
    X = (xs.astype(f32) * dt[..., None]).reshape(Bn, nc, SSD_CHUNK, SSM_GROUPS, HEADS_PER_GROUP, P)
    a = (dt * A).reshape(Bn, nc, SSD_CHUNK, SSM_GROUPS, HEADS_PER_GROUP).transpose(0, 3, 4, 1, 2)
    Bc = Bm.astype(f32).reshape(Bn, nc, SSD_CHUNK, SSM_GROUPS, D_STATE)
    Cc = Cm.astype(f32).reshape(Bn, nc, SSD_CHUNK, SSM_GROUPS, D_STATE)
    a_cs = jnp.cumsum(a, axis=-1)
    Lmat = jnp.exp(segsum(a))
    CB = jnp.einsum('bclgn,bcsgn->bgcls', Cc, Bc)
    y_diag = jnp.einsum('bgrcls,bcsgrp->bclgrp', CB[:, :, None] * Lmat, X)
    decay = jnp.exp(a_cs[..., -1:] - a_cs)
    states = jnp.einsum('bclgn,bgrcl,bclgrp->bcgrpn', Bc, decay, X)
    chunk_a = jnp.pad(a_cs[..., -1], ((0, 0), (0, 0), (0, 0), (1, 0)))
    dchunk = jnp.exp(segsum(chunk_a))
    states = jnp.concatenate([jnp.zeros_like(states[:, :1]), states], axis=1)
    states_in = jnp.einsum('bgrzc,bcgrpn->bzgrpn', dchunk, states)[:, :-1]
    y_off = jnp.einsum('bclgn,bcgrpn,bgrcl->bclgrp', Cc, states_in, jnp.exp(a_cs))
    return (y_diag + y_off).reshape(Bn, S, H, P)

def mamba2_mixer(z, xBC, dt_raw, conv_w, conv_b, dt_bias, A_log, D_skip, norm_w):
    Bn, S, _ = z.shape
    dtp = z.dtype
    xBC = lax.conv_general_dilated(xBC, conv_w[:, None, :], window_strides=(1,), padding=((CONV_W - 1, 0),),
                                   dimension_numbers=('NWC', 'WIO', 'NWC'), feature_group_count=D_CONV)
    xBC = jax.nn.silu(xBC + conv_b)
    xs = xBC[..., :D_SSM].reshape(Bn, S, SSM_HEADS, SSM_HEAD_DIM)
    Bm = xBC[..., D_SSM:D_SSM + SSM_GROUPS * D_STATE].reshape(Bn, S, SSM_GROUPS, D_STATE)
    Cm = xBC[..., D_SSM + SSM_GROUPS * D_STATE:].reshape(Bn, S, SSM_GROUPS, D_STATE)
    dt = jax.nn.softplus((dt_raw + dt_bias).astype(jnp.float32))
    A = -jnp.exp(A_log.astype(jnp.float32))
    y = ssd_chunked(xs, dt, A, Bm, Cm)
    y = y + D_skip.astype(jnp.float32)[:, None] * xs.astype(jnp.float32)
    yz = (y.reshape(Bn, S, D_SSM) * jax.nn.silu(z.astype(jnp.float32))).reshape(Bn, S, SSM_GROUPS, D_SSM // SSM_GROUPS)
    yz = yz * lax.rsqrt(jnp.mean(yz * yz, axis=-1, keepdims=True) + EPS)
    return (yz.reshape(Bn, S, D_SSM) * norm_w.astype(jnp.float32)).astype(dtp)

def hier_moe(u, rg_w, rg_b, re_w, re_b, w_gate, w_up, w_down):
    Bn, S, Dm = u.shape
    t = u.reshape(-1, Dm)
    n_tok = t.shape[0]
    g_prob = jax.nn.softmax((t @ rg_w + rg_b).astype(jnp.float32), axis=-1)
    g_p, g_idx = lax.top_k(g_prob, 1)
    e_logit = (t @ re_w + re_b).astype(jnp.float32).reshape(n_tok, N_EGROUPS, EXPERTS_PER_GROUP)
    e_logit = e_logit[jnp.arange(n_tok), g_idx[:, 0]]
    e_l, e_idx = lax.top_k(e_logit, TOP_K_INNER)
    w = jax.nn.softmax(e_l, axis=-1) * g_p
    eid = g_idx * EXPERTS_PER_GROUP + e_idx
    comb = jnp.sum(jax.nn.one_hot(eid, N_EXPERTS, dtype=jnp.float32) * w[..., None], axis=1).astype(u.dtype)
    out = jnp.zeros_like(t)
    for gi in range(N_EGROUPS):
        sl = slice(gi * EXPERTS_PER_GROUP, (gi + 1) * EXPERTS_PER_GROUP)
        hdn = jax.nn.silu(jnp.einsum('nd,edf->nef', t, w_gate[sl])) * jnp.einsum('nd,edf->nef', t, w_up[sl])
        out = out + jnp.einsum('nef,efd->nd', hdn * comb[:, sl, None], w_down[sl])
    return out.reshape(Bn, S, Dm)

def setup_inputs(seed: int = 0) -> dict:
    key = jax.random.key(seed)
    ks = jax.random.split(key, 32)
    f32 = jnp.float32

    def nrm(k, shape, scale):
        return jax.random.normal(k, shape, f32) * scale

    def gain(k, shape):
        return 1.0 + 0.02 * jax.random.normal(k, shape, f32)

    dt0 = jnp.exp(jax.random.uniform(ks[12], (DEPTH, SSM_HEADS), f32, math.log(1e-3), math.log(1e-1)))
    return {
        "x": nrm(ks[0], (BATCH, SEQ, D_MODEL), 1.0),
        "attn_norm_w": gain(ks[1], (DEPTH, D_MODEL)),
        "w_in": nrm(ks[2], (DEPTH, D_MODEL, D_IN), D_MODEL ** -0.5),
        "q_norm_w": gain(ks[3], (DEPTH, HEAD_DIM)),
        "k_norm_w": gain(ks[4], (DEPTH, 3, HEAD_DIM)),
        "cmp_pe": nrm(ks[5], (DEPTH, 2, L_CMP, HEAD_DIM), 0.1),
        "cmp_w1": nrm(ks[6], (DEPTH, 2, L_CMP * HEAD_DIM, HEAD_DIM), (L_CMP * HEAD_DIM) ** -0.5),
        "cmp_w2": nrm(ks[7], (DEPTH, 2, HEAD_DIM, HEAD_DIM), HEAD_DIM ** -0.5),
        "attn_out_norm_w": gain(ks[8], (DEPTH, D_ATT)),
        "conv_w": nrm(ks[9], (DEPTH, CONV_W, D_CONV), CONV_W ** -0.5),
        "conv_b": nrm(ks[10], (DEPTH, D_CONV), 0.01),
        "dt_bias": dt0 + jnp.log(-jnp.expm1(-dt0)),
        "A_log": jnp.log(jax.random.uniform(ks[13], (DEPTH, SSM_HEADS), f32, 1.0, 16.0)),
        "D_skip": 1.0 + 0.1 * jax.random.normal(ks[14], (DEPTH, SSM_HEADS), f32),
        "ssm_norm_w": gain(ks[15], (DEPTH, D_SSM)),
        "w_out": nrm(ks[16], (DEPTH, D_ATT + D_SSM, D_MODEL), (D_ATT + D_SSM) ** -0.5),
        "ffn_norm_w": gain(ks[17], (DEPTH, D_MODEL)),
        "router_g_w": nrm(ks[18], (DEPTH, D_MODEL, N_EGROUPS), D_MODEL ** -0.5),
        "router_g_b": nrm(ks[19], (DEPTH, N_EGROUPS), 0.01),
        "router_e_w": nrm(ks[20], (DEPTH, D_MODEL, N_EXPERTS), D_MODEL ** -0.5),
        "router_e_b": nrm(ks[21], (DEPTH, N_EXPERTS), 0.01),
        "w_gate": nrm(ks[22], (DEPTH, N_EXPERTS, D_MODEL, D_EXPERT), D_MODEL ** -0.5),
        "w_up": nrm(ks[23], (DEPTH, N_EXPERTS, D_MODEL, D_EXPERT), D_MODEL ** -0.5),
        "w_down": nrm(ks[24], (DEPTH, N_EXPERTS, D_EXPERT, D_MODEL), D_EXPERT ** -0.5),
    }

def reference(x, attn_norm_w, w_in, q_norm_w, k_norm_w, cmp_pe, cmp_w1, cmp_w2, attn_out_norm_w,
              conv_w, conv_b, dt_bias, A_log, D_skip, ssm_norm_w, w_out, ffn_norm_w,
              router_g_w, router_g_b, router_e_w, router_e_b, w_gate, w_up, w_down):
    Bn, S = x.shape[:2]
    split_points = [int(v) for v in np.cumsum(SPLIT_SIZES)[:-1]]

    def heads(a, n):
        return a.reshape(Bn, S, n, HEAD_DIM)

    h = x
    for l in range(DEPTH):
        u = rms_norm(h, attn_norm_w[l])
        proj = u @ w_in[l]
        q, kc, vc, ksl, vsl, kw, vw, g, z, xBC, dt_raw = jnp.split(proj, split_points, axis=-1)
        o_att = nsa_mixer(heads(q, ATT_HEADS), heads(kc, ATT_KV_HEADS), heads(vc, ATT_KV_HEADS),
                          heads(ksl, ATT_KV_HEADS), heads(vsl, ATT_KV_HEADS), heads(kw, ATT_KV_HEADS),
                          heads(vw, ATT_KV_HEADS), g.reshape(Bn, S, ATT_HEADS, 3),
                          q_norm_w[l], k_norm_w[l], cmp_pe[l], cmp_w1[l], cmp_w2[l])
        o_att = rms_norm(o_att, attn_out_norm_w[l])
        o_ssm = mamba2_mixer(z, xBC, dt_raw, conv_w[l], conv_b[l], dt_bias[l], A_log[l], D_skip[l], ssm_norm_w[l])
        h = h + jnp.concatenate([o_att, o_ssm], axis=-1) @ w_out[l]
        h = h + hier_moe(rms_norm(h, ffn_norm_w[l]), router_g_w[l], router_g_b[l], router_e_w[l], router_e_b[l],
                         w_gate[l], w_up[l], w_down[l])
    return h


_drawn_inputs = setup_inputs


def setup_inputs(seed=0):
    import zlib

    import numpy as np

    out = dict(_drawn_inputs(seed))
    spreads = {}
    factors = {'q_norm_w': 3.866,
     'k_norm_w': 4.181,
     'attn_out_norm_w': 3.632,
     'conv_b': 4.652,
     'ssm_norm_w': 3.515,
     'ffn_norm_w': 3.356,
     'router_g_b': 7.573,
     'router_e_b': 8.0}
    for name, (base, spread) in spreads.items():
        noise = np.random.default_rng([zlib.crc32(name.encode()), seed]).standard_normal(out[name].shape)
        drawn = base * np.exp(spread * noise) if base else spread * noise
        out[name] = __import__('jax').numpy.asarray(drawn.astype(out[name].dtype))
    for name, factor in factors.items():
        out[name] = (out[name] * factor).astype(out[name].dtype)
    return out
```

```python
from contextlib import ExitStack

import concourse.bass as bass
from concourse import mybir

F32 = mybir.dt.float32
BF16 = mybir.dt.bfloat16
I32 = mybir.dt.int32
ACT = mybir.ActivationFunctionType
ALU = mybir.AluOpType
AX = mybir.AxisListType

P = 128
D = 1024
S = 1024
NT = S // P
KD = D // P
HD = 64
NH = 8
NG = 2
GQ = NH // NG
BANK = 512
N_CMP = 63
N_BLK = 16
L_CMP = 32
CSTR = 16
TOP_N = 8
D_SSM = 512
D_CONV = 1024
N_STATE = 128
SH = 8
EPS = 1e-6
NEG = -1.0e30
KR = 64 + 2 * N_BLK + GQ + 1
ROW_SEL, ROW_ALIBI, ROW_MAX, ROW_SLOPE = 64, 80, 96, 100
N_EXP = 16
D_EXP = 256
PAIRS = 2 * S
SLOTS = PAIRS // P + N_EXP - 1
NGATE = 24
TABLE = 32
EDGES = TABLE + 1
RING = 3
GU_COLS, D_COLS = KD * 2 * D_EXP, (D_EXP // P) * D

COL_Q = 0
COL_KV = 512
COL_GATE = COL_KV + 6 * 128
COL_Z = COL_GATE + NGATE
COL_X = COL_Z + D_SSM
COL_DT = COL_X + D_CONV
D_IN = COL_DT + SH
KVB = 256 + NGATE + SH


def shape_constants():
    import numpy as np

    t = np.arange(S)
    loc = np.arange(P)
    slopes = np.exp2(-8.0 * (np.arange(NH) + 1) / NH).astype(np.float32)
    c = {}
    c["ident"] = np.eye(P, dtype=np.float32)
    def key_rows(pos, live):
        hot = (pos[None] // HD == np.arange(N_BLK)[:, None]).astype(np.float32)
        sel = hot * live
        return np.concatenate([sel, hot, np.ones((GQ, len(pos))), (pos % HD)[None]]).astype(np.float32)
    c["key_rows_sel"] = key_rows(t, 1.0)
    c["key_rows_win"] = key_rows(t, 0.0)
    c["key_rows_cmp"] = key_rows(np.arange(N_CMP) * CSTR + L_CMP - 1, 0.0)
    q = np.zeros((NT, N_BLK, NH, P), np.float32)
    for n in range(NT):
        d = (n * P + loc)[None, :] - HD * np.arange(N_BLK)[:, None]
        q[n] = -slopes[None, :, None] * d[:, None, :]
    c["alibi_rows"] = q
    c["slope_row"] = np.repeat(slopes, P)[None].astype(np.float32)
    c["head_delta"] = np.repeat(np.eye(GQ, dtype=np.float32), P, axis=1)
    m = np.zeros((4, P, P), np.float32)
    m[0] = np.where(loc[None, :] > loc[:, None], NEG, 0)
    m[1] = m[0].T
    m[2] = np.where(loc[None, :] <= loc[:, None], NEG, 0)
    m[3] = m[2].T
    c["masks"] = m.transpose(1, 0, 2).copy()
    end = np.arange(N_CMP) * CSTR + L_CMP - 1
    mc = np.where(end[None, :] > t[:, None], NEG, 0).astype(np.float32).reshape(NT, P, N_CMP)
    c["mask_cmp"] = mc.transpose(1, 0, 2).copy()
    c["mask_cmpT"] = mc.transpose(2, 0, 1).copy()
    s0 = np.arange(N_BLK) * HD
    st = np.arange(N_CMP) * CSTR
    ov = np.clip(np.minimum(st[:, None] + L_CMP, s0[None] + HD) - np.maximum(st[:, None], s0[None]), 0, None)
    c["v_cmp_tail"] = np.concatenate([np.ones((N_CMP, 1)), ov / L_CMP], axis=1).astype(np.float32)
    j = np.arange(N_BLK)[None, :]
    cur = (t // HD)[:, None]
    forced = (j == 0) | (j == cur) | (j == cur - 1)
    valid = j <= cur
    rows = np.stack([valid & ~forced, np.where(forced, 1.0e4, np.where(valid, 0.0, -1.0))]).astype(np.float32)
    c["score_rows"] = rows.reshape(2, NT, P, N_BLK).transpose(2, 0, 1, 3).copy()
    i = np.arange(N_BLK)
    c["before"] = (i[None, :] < i[:, None]).astype(np.float32).reshape(-1)
    c["tri"] = np.triu(np.ones((P, P), np.float32))
    c["tri_strict"] = np.triu(np.ones((P, P), np.float32), 1)
    c["iota"] = np.tile(np.arange(P, dtype=np.float32), (P, 1))
    c["token"] = (np.arange(NT)[None, :] * P + loc[:, None]).astype(np.float32)
    c["slot_edges"] = np.tile(np.arange(EDGES, dtype=np.float32) * P, (P, 1))
    return c


class Names:

    def __init__(self, nc, stack):
        self.nc, self.stack = nc, stack

    def sb(self, name, shape, dt=F32):
        return self.stack.enter_context(self.nc.sbuf_tensor(name, shape, dt))

    def ps(self, name, shape, dt=F32):
        return self.stack.enter_context(self.nc.psum_tensor(name, shape, dt))

    def sem(self, name):
        return self.stack.enter_context(self.nc.semaphore(name))


class Order:

    def __init__(self, engine, sem):
        self.engine, self.sem, self.n = engine, sem, 0

    def mark(self, ins):
        self.n += 1
        ins.then_inc(self.sem, 1)

    def wait(self):
        self.engine.wait_ge(self.sem, self.n)

    def done(self, ins):
        self.mark(ins)
        self.wait()


def build(nc, A, C, out, last="combine"):
    stack = ExitStack()
    with stack:
        N = Names(nc, stack)
        M = {}
        setup_memory(nc, N, M, A, C)
        stages = [("project", project), ("attend", attend), ("ssd", ssd), ("merge", merge),
                  ("experts", experts), ("combine", combine)]
        for name, stage in stages:
            stage(nc, N, M, A, C, out)
            if name == last:
                break


def setup_memory(nc, N, M, A, C):
    sb = N.sb
    M["ident"] = sb("ident", [P, P])
    M["identb"] = sb("identb", [P, P], BF16)
    M["masksb"] = sb("masksb", [P, 4, P], BF16)
    M["vec_rows"] = sb("vec_rows", [64, P])
    M["vecT"] = sb("vecT", [P, 64])
    M["qk_rows"] = sb("qk_rows", [4, HD])
    M["qkT"] = sb("qkT", [HD, 4])
    M["small"] = sb("small", [P, 512])
    M["eps"] = sb("eps", [P, 1])
    M["head_rows"] = sb("head_rows", [P, 3, SH])
    M["tri"] = sb("tri", [P, P])
    M["gate_dt"] = sb("gate_dt", [P, NT, 32])
    M["big_u"] = sb("big_u", [P, KD * S])
    M["big_w"] = sb("big_w", [P, 2 * KD * BANK])
    M["conv"] = sb("conv", [P, NT, S + 3])
    ring = sb("ring_gate_up", [P, 3 * 4096])
    M["ring_gu"] = ring
    M["z"] = ring[:, 0:4096].rearrange("p (c n) -> p c n", c=NT)
    M["kvcT"] = ring[:, 4096:8192].rearrange("p (j n) -> p j n", j=4)
    M["qn"] = ring[:, 8192:12288].rearrange("p (c n) -> p c n", c=NT)
    M["o_att"] = sb("o_att", [P, NT, 512])
    ring = sb("ring_down", [P, 2 * NG * S + 2 * NT * NG * (HD + 1)])
    M["ring_d"] = ring
    M["k_sel"] = ring[:, 0:2048].rearrange("p (g n) -> p g n", g=NG)
    M["k_win"] = ring[:, 2048:4096].rearrange("p (g n) -> p g n", g=NG)
    M["v_sel"] = ring[:, 4096:5136].rearrange("p (c g n) -> p c g n", c=NT, g=NG)
    M["v_win"] = ring[:, 5136:6176].rearrange("p (c g n) -> p c g n", c=NT, g=NG)
    M["misc"] = sb("misc", [P, 3 * 1024])
    M["ps"] = N.ps("ps", [P, 8, BANK])
    M["s_w_out"] = N.sem("w_out_loaded")
    M["s_expert"] = [N.sem(f"expert_loaded{r}") for r in range(RING)]
    M["hn_dram"] = nc.dram_tensor("hn_dram", (S, D), F32, kind="Internal").ap()
    M["y_dram"] = nc.dram_tensor("y_dram", (SLOTS * P, D), F32, kind="Internal").ap()
    plan = M["misc"][:, 2048:3072]
    M["tok_table"] = plan[:, 0:TABLE].bitcast(I32)
    M["w_table"] = plan[:, 32:64]
    M["slot_pos"] = plan[:, 64:80].bitcast(I32)
    M["slot_expert"] = plan[0:1, 80:112].bitcast(I32)
    M["expert_end"] = plan[0:1, 112:128].bitcast(I32)
    M["tok_idx"] = plan[:, 128:130].bitcast(I32)
    M["Q"] = M["misc"][:, :].rearrange("p (r g n) -> p r g n", r=3, g=NG)
    M["s_alibi"] = [N.sem("alibi_loaded0"), N.sem("alibi_loaded1")]
    w = M["big_w"]
    at = [0]

    def part(name, n, dt=F32, p=P):
        cols = n if dt == F32 else (n + 1) // 2
        view = w[0:p, at[0]:at[0] + cols]
        at[0] += cols
        M[name] = view if dt == F32 else view.bitcast(dt)

    part("k_cmp", NG * 64)
    part("v_cmp", NG * 82)
    part("score_rows", 2 * NT * N_BLK)
    part("before", N_BLK * N_BLK)
    part("sg", NT * NGATE)
    part("mask_cmp", NT * 64, BF16)
    part("mask_cmpT", NT * P, BF16)
    part("hid", 2 * NG * 64)
    part("peT", 32)
    part("cmp_w2", 2 * HD)
    part("pe_rows", P)
    part("pe_bias", 2)
    part("head_delta", GQ * P)
    part("o_tmp", GQ * HD)
    part("sel_tmp", 896)
    part("sel01", N_BLK, BF16)
    part("att_small", 64)
    assert at[0] <= KD * BANK
    stage = M["o_att"][:, :, :].rearrange("p c n -> p (c n)")
    M["cmp_w1"] = stage[:, 0:2048].rearrange("p (v l e) -> p v l e", v=2, l=16)
    M["stage_masks"] = stage[:, 2048:2560]
    M["stage_cmp"] = stage[:, 2560:2560 + NT * N_CMP]
    M["stage_cmpT"] = stage[0:N_CMP, 3072:4096]
    M["V_ATT"], M["V_CONVW"], M["V_CONVB"], M["V_AON"], M["V_SSM"], M["V_FFN"] = 0, 8, 40, 48, 52, 56


def load_alibi(sp, M, C, u):
    c, g = u // NG, u % NG
    for br in range(3):
        sp.dma_start(M["Q"][ROW_ALIBI:ROW_MAX, br, g, :],
                     C["alibi_rows"][c, :, g * GQ:(g + 1) * GQ, :].rearrange("j h q -> j (h q)")).then_inc(M["s_alibi"][g], 16)


def project(nc, N, M, A, C, out):
    sem = N.sem
    x_in = M["misc"][:, 0:2048].rearrange("p (b n) -> p b n", b=2)
    xn1 = M["misc"][:, 2048:3072]
    uT = M["big_u"][:, :].rearrange("p (k t) -> p k t", k=KD)
    wbuf = M["big_w"][:, :].rearrange("p (b k n) -> p b k n", b=2, k=KD)
    conv, z, qn = M["conv"], M["z"], M["qn"]
    square = conv[:, 6, 3:3 + BANK]
    junk = conv[:, 7, 3:3 + D]
    kc_nat = M["o_att"]
    ks_nat = conv[:, 5, 3:3 + 256]
    acc = M["misc"][:, 0:2048].rearrange("p (b n) -> p b n", b=2)
    small = M["small"]
    ss_x, rs_x = small[:, 0:8], small[:, 8:16]
    ss_q, rs_q = small[:, 16:80], small[:, 80:144]
    ss_k, rs_k = small[:, 144:176], small[:, 176:208]
    ps, ident, vecT, qkT = M["ps"], M["ident"], M["vecT"], M["qkT"]

    s_const, s_rows = sem("const_loaded"), sem("rows_loaded")
    s_x = [sem("x_loaded0"), sem("x_loaded1")]
    s_w = [sem("w_loaded0"), sem("w_loaded1")]
    s_krows = sem("key_rows_loaded")
    x_stat = sem("x_rstd_ready")
    xn_ready = sem("xn_ready")
    t_full = sem("transposes_full")
    t_free = sem("transposes_evacuated")
    m_full = sem("product_full")
    q_ready = sem("q_normed")
    m_free_act = sem("product_copied")
    vec_full, vec_done = sem("vectors_transposed"), sem("vectors_copied")
    sq_ready, ss_ready, rs_ready = sem("squares_ready"), sem("square_sums_ready"), sem("rstd_ready")
    kn_ready = sem("k_normed")
    conv_in, conv_out, conv_silu = sem("conv_in_ready"), sem("conv_sum_ready"), sem("conv_silu_done")
    ord_act, ord_dve, ord_pool = sem("scalar_order1"), sem("vector_order1"), sem("pool_order1")
    pads = sem("pads_set")
    q_zeroed, s_slopes = sem("query_rows_zeroed"), sem("slopes_loaded")
    s_cmp, s_stage, s_small = sem("cmp_w1_loaded"), sem("masks_loaded"), sem("small_loaded")
    c_full, c_read, c_hid = sem("compress_full"), sem("compress_read"), sem("compress_hidden_ready")
    c_sq, c_ss, c_rs, c_kn = sem("cmp_squares"), sem("cmp_sums"), sem("cmp_rstd"), sem("cmp_k_normed")
    kvcT = M["kvcT"]
    hid = M["hid"][0:HD, :].rearrange("p (v g n) -> p v g n", v=2, g=NG)
    w2 = M["cmp_w2"][0:HD, :].rearrange("p (v e) -> p v e", v=2)
    k_nat = M["sel_tmp"][0:N_CMP, 0:P].rearrange("p (g d) -> p g d", g=NG)
    k_sq = M["sel_tmp"][0:N_CMP, P:2 * P]
    ss_c, rs_c = small[0:N_CMP, 208:210], small[0:N_CMP, 210:212]
    w_in = A["w_in"][0].rearrange("(k p) n -> p k n", p=P)
    NCH = 6
    Q_, KVA, KVB, X0, X1, Z_ = range(NCH)
    T_X, T_KV = 2 * NT, 2 * NT

    with nc.Block() as block:
        @block.sync
        def _(sp):
            def load_x(c):
                if c >= 2:
                    sp.wait_ge(xn_ready, c - 1)
                sp.dma_start(x_in[:, c % 2, :], A["x"][0, c * P:(c + 1) * P, :]).then_inc(s_x[c % 2], 16)

            def load_w(n):
                b = n % 2
                if n >= 2:
                    sp.wait_ge(m_full, NT * (n - 1))
                if n == KVB:
                    sp.dma_start(wbuf[:, b, :, 0:280],
                                 w_in[:, :, COL_KV + 512:COL_Z]).then_inc(s_w[b], 16)
                    sp.dma_start(wbuf[:, b, :, 280:288], w_in[:, :, COL_DT:D_IN]).then_inc(s_w[b], 16)
                    return
                col = {Q_: COL_Q, KVA: COL_KV, X0: COL_X, X1: COL_X + BANK, Z_: COL_Z}[n]
                for h in range(2):
                    sp.dma_start(wbuf[:, b, 4 * h:4 * h + 4, :],
                                 w_in[:, 4 * h:4 * h + 4, col:col + BANK]).then_inc(s_w[b], 16)

            load_x(0)
            sp.dma_start(ident[:, :], C["ident"]).then_inc(s_const, 16)
            r = M["vec_rows"]
            sp.dma_start(r[0:8, :], A["attn_norm_w"].rearrange("a (m p) -> (a m) p", p=P)).then_inc(s_rows, 16)
            sp.dma_start(r[8:40, :], A["conv_w"][0].rearrange("i (m p) -> (i m) p", p=P)).then_inc(s_rows, 16)
            sp.dma_start(r[40:48, :], A["conv_b"].rearrange("a (m p) -> (a m) p", p=P)).then_inc(s_rows, 16)
            sp.dma_start(r[48:52, :], A["attn_out_norm_w"].rearrange("a (m p) -> (a m) p", p=P)).then_inc(s_rows, 16)
            sp.dma_start(r[52:56, :], A["ssm_norm_w"].rearrange("a (m p) -> (a m) p", p=P)).then_inc(s_rows, 16)
            sp.dma_start(r[56:64, :], A["ffn_norm_w"].rearrange("a (m p) -> (a m) p", p=P)).then_inc(s_rows, 16)
            sp.dma_start(M["qk_rows"][0:1, :], A["q_norm_w"]).then_inc(s_rows, 16)
            sp.dma_start(M["qk_rows"][1:4, :], A["k_norm_w"][0]).then_inc(s_rows, 16)
            load_x(1)
            load_w(Q_)
            load_w(KVA)
            for c in range(2, NT):
                load_x(c)
            for i, name in enumerate(("dt_bias", "A_log", "D_skip")):
                sp.dma_start(M["head_rows"][:, i, :], A[name][0].partition_broadcast(P)).then_inc(s_krows, 16)
            sp.dma_start(M["tri"][:, :], C["tri"]).then_inc(s_krows, 16)
            for g in range(NG):
                sp.dma_start(M["k_sel"][64:KR, g, :], C["key_rows_sel"]).then_inc(s_krows, 16)
                sp.dma_start(M["k_win"][64:KR, g, :], C["key_rows_win"]).then_inc(s_krows, 16)
            load_w(KVB)
            load_w(X0)
            sp.wait_ge(t_free, T_X + 2 * NT)
            for v in range(2):
                sp.dma_start(M["cmp_w1"][:, v], A["cmp_w1"][0, v].rearrange("(l p) e -> p l e", p=P)).then_inc(s_cmp, 16)
            sp.dma_start(M["stage_masks"], C["masks"].rearrange("p a b -> p (a b)")).then_inc(s_stage, 16)
            sp.dma_start(M["stage_cmp"], C["mask_cmp"].rearrange("p a b -> p (a b)")).then_inc(s_stage, 16)
            sp.dma_start(M["stage_cmpT"], C["mask_cmpT"].rearrange("p a b -> p (a b)")).then_inc(s_stage, 16)
            sp.dma_start(M["kvcT"][64:P, :, 0:S - 1], M["kvcT"][0:HD, :, 1:S]).then_inc(s_cmp, 16)
            load_w(X1)
            load_w(Z_)
            sp.wait_ge(m_full, NT * Z_)
            sp.dma_start(M["cmp_w2"][0:HD, :].rearrange("p (v e) -> p v e", v=2),
                         A["cmp_w2"][0].rearrange("v d e -> d v e")).then_inc(s_small, 16)
            sp.dma_start(M["pe_rows"][0:32, :], A["cmp_pe"][0].rearrange("v (l i) d -> (v l) (i d)", i=2)).then_inc(s_small, 16)
            vc = M["v_cmp"].rearrange("p (g n) -> p g n", g=NG)
            for g in range(NG):
                sp.dma_start(M["k_cmp"].rearrange("p (g n) -> p g n", g=NG)[64:KR, g, 0:N_CMP],
                             C["key_rows_cmp"]).then_inc(s_small, 16)
                sp.dma_start(vc[0:N_CMP, g, HD:HD + 17], C["v_cmp_tail"]).then_inc(s_small, 16)
            sp.dma_start(M["score_rows"], C["score_rows"].rearrange("p a b c -> p (a b c)")).then_inc(s_small, 16)
            sp.dma_start(M["before"], C["before"].partition_broadcast(P)).then_inc(s_small, 16)
            sp.dma_start(M["head_delta"][0:GQ, :], C["head_delta"]).then_inc(s_small, 16)
            sp.wait_ge(q_zeroed, 1)
            for g in range(NG):
                for br in range(3):
                    sp.dma_start(M["Q"][ROW_SLOPE:ROW_SLOPE + 1, br, g, :],
                                 C["slope_row"][:, g * BANK:(g + 1) * BANK]).then_inc(s_slopes, 16)
                load_alibi(sp, M, C, g)
            sp.wait_ge(s_slopes, 96)
            sp.wait_ge(s_krows, 128)
            sp.wait_ge(s_stage, 48)
            sp.wait_ge(s_small, 9 * 16)

        @block.tensor
        def _(pe):
            state = {"t": 0, "m": 0}

            def t_bank(n_ops):
                t = state["t"]
                if t >= 4:
                    pe.wait_ge(t_free, t - 3)
                state["t"] += 1
                return t % 4

            def m_bank():
                m = state["m"]
                if m >= 4 + 3 * NT:
                    pe.wait_ge(m_free_act, m - 3 - 3 * NT)
                elif m >= 4 + NT:
                    pe.wait_ge(kn_ready, m - 3 - NT)
                elif m >= 4:
                    pe.wait_ge(q_ready, m - 3)
                state["m"] += 1
                return 4 + m % 4

            def transpose_x(c):
                pe.wait_ge(xn_ready, c + 1)
                for j in range(2):
                    b = t_bank(4)
                    for i in range(4):
                        k = 4 * j + i
                        last = nc.tensor.transpose(ps[:, b, i * P:(i + 1) * P], xn1[:, k * P:(k + 1) * P], ident[:, :])
                    last.then_inc(t_full, 1)

            def chunk_loaded(n):
                pe.wait_ge(s_w[n % 2], 32 * (n // 2 + 1))

            def product_natural(n, c, width):
                b = m_bank()
                for k in range(KD):
                    last = nc.tensor.matmul(ps[:, b, 0:width], uT[:, k, c * P:(c + 1) * P], wbuf[:, n % 2, k, 0:width],
                                            start=(k == 0), stop=(k == KD - 1))
                last.then_inc(m_full, 1)
                return last

            def product_channels(n, m, half):
                b = m_bank()
                for k in range(KD):
                    last = nc.tensor.matmul(ps[:, b, :], wbuf[:, n % 2, k, m * P:(m + 1) * P],
                                            uT[:, k, half * BANK:(half + 1) * BANK], start=(k == 0), stop=(k == KD - 1))
                last.then_inc(m_full, 1)

            pe.wait_ge(s_const, 16)
            pe.wait_ge(s_rows, 8 * 16)
            nc.tensor.transpose(ps[:, 4, 0:64], M["vec_rows"][:, :], ident[0:64, 0:64])
            nc.tensor.transpose(ps[0:HD, 4, 64:68], M["qk_rows"][:, :], ident[0:4, 0:4]).then_inc(vec_full, 1)
            transpose_x(0)
            pe.wait_ge(vec_done, 1)
            chunk_loaded(Q_)
            for c in range(NT):
                if c + 1 < NT:
                    transpose_x(c + 1)
                pe.wait_ge(t_free, 2 * (c + 1))
                product_natural(Q_, c, BANK)
            def transpose_kv(i):
                c = i % NT
                pe.wait_ge(kn_ready, i + 1)
                if i < NT:
                    b = t_bank(4)
                    for j in range(4):
                        last = nc.tensor.transpose(ps[0:HD, b, j * P:(j + 1) * P],
                                                   kc_nat[:, i, j * HD:(j + 1) * HD], ident[:, :])
                    last.then_inc(t_full, 1)
                b = t_bank(2)
                for g in range(NG):
                    last = nc.tensor.transpose(ps[0:HD, b, g * P:(g + 1) * P],
                                               ks_nat[:, (i % 2) * P + g * HD:(i % 2) * P + (g + 1) * HD], ident[:, :])
                last.then_inc(t_full, 1)

            for i in range(2 * NT):
                n = KVA if i < NT else KVB
                if i % NT == 0:
                    chunk_loaded(n)
                product_natural(n, i % NT, BANK if n == KVA else 288)
                if i >= 1:
                    transpose_kv(i - 1)
            for n in (X0, X1):
                chunk_loaded(n)
                for m in range(4):
                    for half in range(2):
                        product_channels(n, m, half)
                        if n == X0 and m == 0 and half == 0:
                            transpose_kv(2 * NT - 1)
            chunk_loaded(Z_)
            for c in range(NT):
                product_natural(Z_, c, BANK)
                if c == 0:
                    pe.wait_ge(t_free, T_X + 3 * NT)
                    pe.wait_ge(s_small, 9 * 16)
                    nc.tensor.transpose(ps[:, 0, 0:32], M["pe_rows"][0:32, :], ident[0:32, 0:32]).then_inc(c_full, 1)
                if c == 1:
                    pe.wait_ge(s_cmp, 48)
                    pe.wait_ge(c_read, 1)
                    for v in range(2):
                        for l in range(16):
                            nc.tensor.matmul(ps[0:HD, 1, v * P:v * P + NG * N_CMP].rearrange("e (g n) -> e g n", g=NG),
                                             M["cmp_w1"][:, v, l, :],
                                             kvcT[:, 2 * v:2 * v + 2, 2 * l:2 * l + CSTR * (N_CMP - 1) + 1:CSTR],
                                             start=(l == 0), stop=(l == 15))
                    for v in range(2):
                        for l in range(16):
                            last = nc.tensor.matmul(ps[0:HD, 2, v:v + 1], M["cmp_w1"][:, v, l, :],
                                                    M["peT"][:, v * 16 + l:v * 16 + l + 1], start=(l == 0), stop=(l == 15))
                    last.then_inc(c_full, 1)
                if c == 3:
                    pe.wait_ge(c_hid, 2)
                    for v in range(2):
                        for g in range(NG):
                            last = nc.tensor.matmul(ps[0:N_CMP, 0, (2 * v + g) * HD:(2 * v + g + 1) * HD],
                                                    hid[:, v, g, 0:N_CMP], w2[:, v, :], start=True, stop=True)
                    last.then_inc(c_full, 1)
                if c == 5:
                    pe.wait_ge(c_kn, 1)
                    for g in range(NG):
                        last = nc.tensor.transpose(ps[0:HD, 1, g * 64:g * 64 + N_CMP], k_nat[:, g, :],
                                                   ident[0:N_CMP, 0:N_CMP])
                    last.then_inc(c_full, 1)

        @block.scalar
        def _(act):
            o = Order(act, ord_act)
            nc.scalar.preload_act_table_set("natural_log_exp_and_others")

            def rstd(ss, rs, n):
                o.done(nc.scalar.activation(rs, ss, ACT.Ln, scale=1.0 / n, bias=M["eps"][:, 0:1]))
                return nc.scalar.activation(rs, rs, ACT.Exp, scale=-0.5)

            def x_stats(c):
                act.wait_ge(s_x[c % 2], 16 * (c // 2 + 1))
                o.done(nc.scalar.activation(junk, x_in[:, c % 2, :], ACT.Square, accum_out=ss_x[:, c:c + 1]))
                rstd(ss_x[:, c:c + 1], rs_x[:, c:c + 1], D).then_inc(x_stat, 1)

            def q_stats(c):
                act.wait_ge(m_full, c + 1)
                nc.scalar.activation(square, ps[:, 4 + c % 4, :], ACT.Square).then_inc(sq_ready, 1)
                act.wait_ge(ss_ready, c + 1)
                rstd(ss_q[:, 8 * c:8 * c + 8], rs_q[:, 8 * c:8 * c + 8], HD).then_inc(rs_ready, 1)

            def kv_part(i):
                c, b = i % NT, 4 + i % 4
                act.wait_ge(m_full, NT + i + 1)
                if i < NT:
                    nc.scalar.activation(square[:, 0:P], ps[:, b, 256:384], ACT.Square).then_inc(sq_ready, 1)
                    o.mark(nc.scalar.activation(kc_nat[:, c, 0:256], ps[:, b, 0:256], ACT.Copy))
                    o.mark(nc.scalar.activation(M["v_sel"][:, c, :, 0:HD],
                                                ps[:, b, 384:512].rearrange("p (g d) -> p g d", g=NG), ACT.Copy))
                else:
                    nc.scalar.activation(square[:, 0:P], ps[:, b, 0:P], ACT.Square).then_inc(sq_ready, 1)
                    o.mark(nc.scalar.activation(M["v_win"][:, c, :, 0:HD],
                                                ps[:, b, P:2 * P].rearrange("p (g d) -> p g d", g=NG), ACT.Copy))
                    o.mark(nc.scalar.activation(M["gate_dt"][:, c, :], ps[:, b, 256:288], ACT.Copy))
                act.wait_ge(ss_ready, NT + i + 1)
                rstd(ss_k[:, 2 * i:2 * i + 2], rs_k[:, 2 * i:2 * i + 2], HD).then_inc(rs_ready, 1)

            act.wait_ge(pads, 1)
            x_stats(0)
            x_stats(1)
            for c in range(NT):
                if c + 2 < NT:
                    x_stats(c + 2)
                q_stats(c)
            for i in range(2 * NT):
                kv_part(i)
            nc.scalar.preload_act_table(ACT.Silu)

            def silu(m):
                act.wait_ge(conv_out, m + 1)
                nc.scalar.activation(conv[:, m, 3:3 + S], acc[:, m % 2, :], ACT.Silu).then_inc(conv_silu, 1)

            for m in range(KD):
                for half in range(2):
                    j = 2 * m + half
                    act.wait_ge(m_full, 3 * NT + j + 1)
                    if j == 0:
                        act.wait_ge(kn_ready, 2 * NT)
                    if m == 5 and half == 0:
                        act.wait_ge(t_free, T_X + 2 * NT + NT)
                    a = nc.scalar.activation(conv[:, m, 3 + half * BANK:3 + (half + 1) * BANK], ps[:, 4 + j % 4, :],
                                             ACT.Copy)
                    a.then_inc(m_free_act, 1)
                if m >= 1:
                    silu(m - 1)
            silu(KD - 1)
            for c in range(NT):
                act.wait_ge(m_full, 5 * NT + c + 1)
                nc.scalar.activation(z[:, c, :], ps[:, 4 + c % 4, :], ACT.Silu).then_inc(m_free_act, 1)
                if c == 1:
                    act.wait_ge(c_read, 2)
                    for v in range(2):
                        nc.scalar.activation(hid[:, v, :, 0:N_CMP],
                                             ps[0:HD, 1, v * P:v * P + NG * N_CMP].rearrange("e (g n) -> e g n", g=NG),
                                             ACT.Silu, bias=M["pe_bias"][0:HD, v:v + 1]).then_inc(c_hid, 1)
                if c == 3:
                    act.wait_ge(c_read, 3)
                    nc.scalar.activation(k_sq, ps[0:N_CMP, 0, 0:P], ACT.Square).then_inc(c_sq, 1)
                    act.wait_ge(c_ss, 1)
                    o.done(nc.scalar.activation(rs_c, ss_c, ACT.Ln, scale=1.0 / HD, bias=M["eps"][0:N_CMP, 0:1]))
                    nc.scalar.activation(rs_c, rs_c, ACT.Exp, scale=-0.5).then_inc(c_rs, 1)

        @block.gpsimd
        def _(pool):
            nc.gpsimd.memset(M["eps"][:, :], EPS).then_inc(pads, 1)
            nc.gpsimd.memset(conv[:, :, 0:3], 0.0).then_inc(pads, 1)
            nc.gpsimd.memset(M["v_sel"][:, :, :, HD:HD + 1], 1.0).then_inc(pads, 1)
            nc.gpsimd.memset(M["v_win"][:, :, :, HD:HD + 1], 1.0).then_inc(pads, 1)
            pool.wait_ge(conv_silu, KD)
            nc.gpsimd.memset(M["misc"][64:P, :], 0.0).then_inc(q_zeroed, 1)

        @block.vector
        def _(dve):
            o = Order(dve, ord_dve)
            V_ATT, V_CONVW, V_CONVB = M["V_ATT"], M["V_CONVW"], M["V_CONVB"]
            state = {"t": 0}

            def normalise_x(c):
                dve.wait_ge(x_stat, c + 1)
                if c >= 1:
                    dve.wait_ge(t_full, 2 * c)
                nc.vector.tensor_scalar(xn1, x_in[:, c % 2, :], rs_x[:, c:c + 1], None, ALU.mult).then_inc(xn_ready, 1)

            def next_t():
                state["t"] += 1
                dve.wait_ge(t_full, state["t"])
                return (state["t"] - 1) % 4

            def evacuate_u(c):
                for j in range(2):
                    b = next_t()
                    nc.vector.tensor_tensor(uT[:, 4 * j:4 * j + 4, c * P:(c + 1) * P],
                                            ps[:, b, :].rearrange("p (k t) -> p k t", k=4),
                                            vecT[:, V_ATT + 4 * j:V_ATT + 4 * j + 4].unsqueeze(2).broadcast_to([P, 4, P]),
                                            ALU.mult).then_inc(t_free, 1)

            def q_norm(c):
                dve.wait_ge(sq_ready, c + 1)
                nc.vector.tensor_reduce(ss_q[:, 8 * c:8 * c + 8], square.rearrange("p (h d) -> p h d", h=NH),
                                        AX.X, ALU.add).then_inc(ss_ready, 1)
                dve.wait_ge(rs_ready, c + 1)
                nc.vector.tensor_tensor(qn[:, c, :].rearrange("p (h d) -> p h d", h=NH),
                                        ps[:, 4 + c % 4, :].rearrange("p (h d) -> p h d", h=NH),
                                        rs_q[:, 8 * c:8 * c + 8].unsqueeze(2).broadcast_to([P, NH, HD]),
                                        ALU.mult).then_inc(q_ready, 1)

            dve.wait_ge(vec_full, 1)
            o.mark(nc.vector.tensor_copy(vecT[:, :], ps[:, 4, 0:64]))
            o.done(nc.vector.tensor_copy(qkT[:, :], ps[0:HD, 4, 64:68]))
            nc.vector.tensor_scalar(qkT[:, 0:1], qkT[:, 0:1], HD ** -0.5, None, ALU.mult).then_inc(vec_done, 1)
            dve.wait_ge(vec_done, 1)
            normalise_x(0)
            for c in range(NT):
                if c + 1 < NT:
                    normalise_x(c + 1)
                evacuate_u(c)
                if c >= 1:
                    q_norm(c - 1)
            q_norm(NT - 1)

            def k_norm(i):
                b = 4 + i % 4
                dve.wait_ge(sq_ready, NT + i + 1)
                nc.vector.tensor_reduce(ss_k[:, 2 * i:2 * i + 2], square[:, 0:P].rearrange("p (h d) -> p h d", h=NG),
                                        AX.X, ALU.add).then_inc(ss_ready, 1)
                dve.wait_ge(rs_ready, NT + i + 1)
                col = 256 if i < NT else 0
                if i >= 2:
                    dve.wait_ge(t_full, T_X + (2 * (i - 1) if i - 1 <= NT else 2 * NT + (i - 1 - NT)))
                nc.vector.tensor_tensor(ks_nat[:, (i % 2) * P:(i % 2) * P + P].rearrange("p (h d) -> p h d", h=NG),
                                        ps[:, b, col:col + P].rearrange("p (h d) -> p h d", h=NG),
                                        rs_k[:, 2 * i:2 * i + 2].unsqueeze(2).broadcast_to([P, NG, HD]),
                                        ALU.mult).then_inc(kn_ready, 1)

            def evacuate_kv(i):
                c = i % NT
                if i < NT:
                    b = next_t()
                    nc.vector.tensor_copy(M["kvcT"][0:HD, :, c * P:(c + 1) * P],
                                          ps[0:HD, b, :].rearrange("p (j t) -> p j t", j=4)).then_inc(t_free, 1)
                b = next_t()
                dst, w = (M["k_sel"], 2) if i < NT else (M["k_win"], 3)
                nc.vector.tensor_scalar(dst[0:HD, :, c * P:(c + 1) * P],
                                        ps[0:HD, b, 0:2 * P].rearrange("p (g t) -> p g t", g=NG),
                                        qkT[:, w:w + 1], None, ALU.mult).then_inc(t_free, 1)

            for i in range(2 * NT):
                k_norm(i)
                if i >= 1:
                    evacuate_kv(i - 1)
            evacuate_kv(2 * NT - 1)
            dve.wait_ge(pads, 4)
            for m in range(KD):
                dve.wait_ge(m_free_act, 2 * m + 2)
                if m >= 2:
                    dve.wait_ge(conv_silu, m - 1)
                a = acc[:, m % 2, :]
                w = lambda i: vecT[:, V_CONVW + 8 * i + m:V_CONVW + 8 * i + m + 1]
                o.done(nc.vector.tensor_scalar(a, conv[:, m, 3:3 + S], w(3), vecT[:, V_CONVB + m:V_CONVB + m + 1],
                                               ALU.mult, ALU.add))
                for i in (2, 1):
                    o.done(nc.vector.scalar_tensor_tensor(a, conv[:, m, i:i + S], w(i), a, ALU.mult, ALU.add))
                nc.vector.scalar_tensor_tensor(a, conv[:, m, 0:S], w(0), a, ALU.mult, ALU.add).then_inc(conv_out, 1)
            dve.wait_ge(c_full, 1)
            nc.vector.tensor_copy(M["peT"], ps[:, 0, 0:32]).then_inc(c_read, 1)
            dve.wait_ge(c_full, 2)
            nc.vector.tensor_copy(M["pe_bias"][0:HD, :], ps[0:HD, 2, 0:2]).then_inc(c_read, 1)
            dve.wait_ge(c_full, 3)
            nc.vector.tensor_copy(M["v_cmp"][0:N_CMP, :].rearrange("p (g n) -> p g n", g=NG)[:, :, 0:HD],
                                  ps[0:N_CMP, 0, P:2 * P].rearrange("p (g d) -> p g d", g=NG)).then_inc(c_read, 1)
            dve.wait_ge(c_sq, 1)
            nc.vector.tensor_reduce(ss_c, k_sq.rearrange("p (g d) -> p g d", g=NG), AX.X, ALU.add).then_inc(c_ss, 1)
            dve.wait_ge(c_rs, 1)
            nc.vector.tensor_tensor(k_nat, ps[0:N_CMP, 0, 0:P].rearrange("p (g d) -> p g d", g=NG),
                                    rs_c.unsqueeze(2).broadcast_to([N_CMP, NG, HD]), ALU.mult).then_inc(c_kn, 1)
            dve.wait_ge(c_full, 4)
            nc.vector.tensor_scalar(M["k_cmp"].rearrange("p (g n) -> p g n", g=NG)[0:HD, :, 0:N_CMP],
                                    ps[0:HD, 1, 0:P].rearrange("p (g n) -> p g n", g=NG)[:, :, 0:N_CMP],
                                    qkT[:, 1:2], None, ALU.mult)


CMP, WIN, SEL = range(3)


def attend_order():
    steps = []
    for u in range(-1, NT * NG):
        new, old = u + 1 < NT * NG, u >= 0
        if old:
            steps += [("scoresT", WIN, u), ("values", WIN, u)]
            if u // NG >= NT // 2:
                steps += [("selT", SEL, u)]
            steps += [("scores", SEL, u)]
        if new:
            steps += [("queriesT", CMP, u + 1)]
        if old:
            steps += [("maxT", SEL, u)]
        if new:
            steps += [("scores", CMP, u + 1)]
        if old:
            steps += [("scoresT", SEL, u)]
        if new:
            steps += [("maxT", CMP, u + 1), ("scores", WIN, u + 1)]
        if old:
            steps += [("values", SEL, u)]
        if new:
            steps += [("scoresT", CMP, u + 1), ("maxT", WIN, u + 1), ("values", CMP, u + 1)]
    return steps


def cmp_keys(c):
    return (c * P + P - L_CMP) // CSTR + 1


def key_blocks(br, c):
    return {CMP: [0], WIN: list(range(max(0, c - 2), c + 1)), SEL: list(range(c + 1))}[br]


def score_slots(br, c):
    return {CMP: [[0, 1, 2, 3]], WIN: [[0, 1], [2, 3]],
            SEL: [[0, 1], [2, 3]] if c < NT // 2 else [[0], [1], [2], [3]]}[br]


def attend(nc, N, M, A, C, out):
    sem = N.sem
    ps, ident, identb, qkT, Q, qn = M["ps"], M["ident"], M["identb"], M["qkT"], M["Q"], M["qn"]
    masksb = M["masksb"]
    mask_cmp = M["mask_cmp"].rearrange("p (c n) -> p c n", c=NT)
    mask_cmpT = M["mask_cmpT"].rearrange("p (c n) -> p c n", c=NT)
    k_cmp = M["k_cmp"].rearrange("p (g n) -> p g n", g=NG)
    v_cmp = M["v_cmp"].rearrange("p (g n) -> p g n", g=NG)
    keys = {WIN: M["k_win"], SEL: M["k_sel"]}
    vals = {WIN: M["v_win"], SEL: M["v_sel"]}
    pT = {CMP: M["kvcT"][:, 0, 0:BANK].unsqueeze(1),
          WIN: M["kvcT"][:, 1:3, :].rearrange("p a n -> p (a n)")[:, 0:3 * BANK].rearrange("p (b n) -> p b n", b=3),
          SEL: M["big_u"][:, 0:NT * BANK].rearrange("p (b n) -> p b n", b=NT)}
    sg = M["sg"].rearrange("p (c h r) -> p c h r", c=NT, h=NH)
    o_att = M["o_att"]
    o_tmp = M["o_tmp"].rearrange("p (h d) -> p h d", h=GQ)
    t = M["sel_tmp"]
    imp_h, imp, score = t[:, 0:64], t[:, 64:80], t[:, 80:96]
    gt, eq, rank = t[:, 96:352], t[:, 352:608], t[:, 608:624]
    before = M["before"].rearrange("p (j i) -> p j i", j=N_BLK)
    score_rows = M["score_rows"].rearrange("p (a c j) -> p a c j", a=2, c=NT)
    neg = M["att_small"][:, 0:12].rearrange("p (r h) -> p r h", r=3)
    den, coef = M["att_small"][:, 12:24].rearrange("p (r h) -> p r h", r=3), M["att_small"][:, 24:36].rearrange("p (r h) -> p r h", r=3)
    head_delta = M["head_delta"][0:GQ, :]

    consts = sem("masks_cast")
    q_full, q_cmp_rows, q_rows = sem("queries_transposed"), sem("query_rows_cmp"), sem("query_rows_both")
    slot_full, slot_read = sem("scores_full"), sem("scores_read")
    max_ready, max_full, max_rows = sem("maxima_ready"), sem("maxima_transposed"), sem("maxima_rows")
    st_full, exp_done = sem("scoresT_full"), sem("exp_done")
    o_full, o_read = sem("values_full"), sem("values_read")
    sel_ready, sel_full, sel_rows = sem("selection_ready"), sem("selection_transposed"), sem("selection_rows")
    zeroed = sem("maxima_rows_zeroed")
    ord_dve, ord_act = sem("vector_order2"), sem("scalar_order2")
    gates_exp, gates_done = sem("gates_exp"), sem("gates_done")

    steps = attend_order()
    slots_before, st_before, o_before, max_before, sel_before = {}, {}, {}, {}, {}
    a = b = v = m = z = 0
    for kind, br, u in steps:
        c = u // NG
        if kind == "scores":
            slots_before[br, u] = a
            a += len(score_slots(br, c))
        elif kind == "scoresT":
            st_before[br, u] = b
            b += len(key_blocks(br, c))
        elif kind == "values":
            o_before[br, u] = v
            v += 1
        elif kind == "maxT":
            max_before[br, u] = m
            m += 1
        elif kind == "selT":
            sel_before[u] = z
            z += 1

    with nc.Block() as block:
        @block.sync
        def _(sp):
            for u in range(NT * NG - NG):
                sp.wait_ge(st_full, st_before[SEL, u] + u // NG + 1)
                load_alibi(sp, M, C, u + NG)

        @block.gpsimd
        def _(pool):
            for u in range(NT * NG - NG):
                pool.wait_ge(st_full, st_before[SEL, u] + u // NG + 1)
                nc.gpsimd.memset(Q[ROW_MAX:ROW_MAX + GQ, :, u % NG, :], 0.0).then_inc(zeroed, 1)

        @block.tensor
        def _(pe):
            state = {"x": (0, 0)}

            def x_bank_free():
                nm, ns = state["x"]
                if nm:
                    pe.wait_ge(max_rows, nm)
                if ns:
                    pe.wait_ge(sel_rows, ns)

            def queriesT(u):
                c, g = u // NG, u % NG
                if u >= 1:
                    pe.wait_ge(o_read, o_before[WIN, u - 1] + 1)
                for h in range(GQ):
                    n = (g * GQ + h) * HD
                    last = nc.tensor.transpose(ps[0:HD, 6, h * P:(h + 1) * P], qn[:, c, n:n + HD], ident[:, :])
                last.then_inc(q_full, 1)

            def scores(br, u):
                c, g = u // NG, u % NG
                if br == CMP:
                    pe.wait_ge(q_cmp_rows, u + 1)
                    pe.wait_ge(M["s_alibi"][g], 48 * (c + 1))
                    if u >= NG:
                        pe.wait_ge(zeroed, u - 1)
                elif br == WIN:
                    pe.wait_ge(q_rows, u + 1)
                elif c >= NT // 2:
                    pe.wait_ge(sel_rows, sel_before[u] + 1)
                for i, heads in enumerate(score_slots(br, c)):
                    k = slots_before[br, u] + i
                    if k >= 2:
                        pe.wait_ge(slot_read, k - 1)
                    for j, h in enumerate(heads):
                        lhsT = Q[0:KR, br, g, h * P:(h + 1) * P]
                        if br == CMP:
                            n = cmp_keys(c)
                            o = ps[:, 2 * (k % 2), h * 64:h * 64 + n]
                            nc.tensor.matmul(o, lhsT, k_cmp[0:KR, g, 0:n], start=True, stop=False)
                            last = nc.tensor.matmul(o, identb[:, :], mask_cmp[:, c, 0:n], start=False, stop=True)
                            continue
                        blocks = key_blocks(br, c)
                        k0 = blocks[0] * P
                        for part in range(0, len(blocks), 4):
                            inner = blocks[part:part + 4]
                            bank = 2 * (k % 2) + (j if len(heads) > 1 else part // 4)
                            n = len(inner) * P
                            diag = inner[-1] == c
                            far = br == WIN and inner[0] == c - 2
                            s0 = k0 + part * P
                            last = nc.tensor.matmul(ps[:, bank, 0:n], lhsT, keys[br][0:KR, g, s0:s0 + n],
                                                    start=True, stop=not (diag or far))
                            if far:
                                nc.tensor.matmul(ps[:, bank, 0:P], identb[:, :], masksb[:, 2, :], start=False, stop=False)
                            if diag:
                                last = nc.tensor.matmul(ps[:, bank, n - P:n], identb[:, :], masksb[:, 0, :],
                                                        start=False, stop=True)
                    last.then_inc(slot_full, 1)

            def maxT(br, u):
                n = max_before[br, u]
                pe.wait_ge(max_ready, n + 1)
                x_bank_free()
                nc.tensor.transpose(ps[0:GQ, 7, 0:P], neg[:, br, :], ident[:, :]).then_inc(max_full, 1)
                state["x"] = (n + 1, state["x"][1])

            def selT(u):
                n = sel_before[u]
                pe.wait_ge(sel_ready, n + 1)
                x_bank_free()
                nc.tensor.matmul(ps[64:64 + N_BLK, 7, 0:P], M["sel01"], identb[:, :], start=True, stop=True)\
                    .then_inc(sel_full, 1)
                state["x"] = (state["x"][0], n + 1)

            def scoresT(br, u):
                c, g = u // NG, u % NG
                pe.wait_ge(max_rows, max_before[br, u] + 1)
                for i, b in enumerate(key_blocks(br, c)):
                    k = st_before[br, u] + i
                    if k >= 2:
                        pe.wait_ge(exp_done, k - 1)
                    rhs = Q[0:KR, br, g, :]
                    if br == CMP:
                        n = cmp_keys(c)
                        o = ps[0:n, 4 + k % 2, :]
                        nc.tensor.matmul(o, k_cmp[0:KR, g, 0:n], rhs, start=True, stop=False)
                        last = nc.tensor.matmul(o, identb[0:N_CMP, 0:n],
                                                mask_cmpT[0:N_CMP, c, :].unsqueeze(1).broadcast_to([N_CMP, GQ, P]),
                                                start=False, stop=True)
                    else:
                        o = ps[:, 4 + k % 2, :]
                        mask = 1 if b == c else 3 if br == WIN and b == c - 2 else None
                        last = nc.tensor.matmul(o, keys[br][0:KR, g, b * P:(b + 1) * P], rhs,
                                                start=True, stop=mask is None)
                        if mask is not None:
                            last = nc.tensor.matmul(o, identb[:, :],
                                                    masksb[:, mask, :].unsqueeze(1).broadcast_to([P, GQ, P]),
                                                    start=False, stop=True)
                    last.then_inc(st_full, 1)

            def values(br, u):
                c, g = u // NG, u % NG
                n = o_before[br, u]
                blocks = key_blocks(br, c)
                if n >= 1:
                    pe.wait_ge(o_read, n)
                if br == SEL and u + 1 < NT * NG:
                    pe.wait_ge(q_rows, u + 2)
                if br == CMP and u == 0:
                    pe.wait_ge(q_rows, 1)
                pe.wait_ge(exp_done, st_before[br, u] + len(blocks))
                w = HD + 17 if br == CMP else HD + 1
                for h in range(GQ):
                    o = ps[:, 6, h * w:(h + 1) * w]
                    for i, b in enumerate(blocks):
                        if br == CMP:
                            kk = cmp_keys(c)
                            last = nc.tensor.matmul(o, pT[CMP][0:kk, 0, h * P:(h + 1) * P], v_cmp[0:kk, g, 0:w],
                                                    start=True, stop=True)
                        else:
                            last = nc.tensor.matmul(o, pT[br][:, i, h * P:(h + 1) * P], vals[br][:, b, g, :],
                                                    start=(i == 0), stop=(i == len(blocks) - 1))
                last.then_inc(o_full, 1)

            pe.wait_ge(consts, 4)
            for kind, br, u in steps:
                if kind == "queriesT":
                    queriesT(u)
                elif kind == "scores":
                    scores(br, u)
                elif kind == "maxT":
                    maxT(br, u)
                elif kind == "selT":
                    selT(u)
                elif kind == "scoresT":
                    scoresT(br, u)
                else:
                    values(br, u)

        @block.scalar
        def _(act):
            nc.scalar.preload_act_table_set("natural_log_exp_and_others")
            nc.scalar.activation(M["sg"].rearrange("p (c n) -> p c n", c=NT), M["gate_dt"][:, :, 0:NGATE], ACT.Exp,
                                 scale=-1.0).then_inc(gates_exp, 1)
            for kind, br, u in steps:
                c, g = u // NG, u % NG
                if kind == "queriesT":
                    act.wait_ge(q_cmp_rows, u + 1)
                    nc.scalar.activation(Q[0:HD, 1:3, g, :], ps[0:HD, 6, :].unsqueeze(1).broadcast_to([HD, 2, BANK]),
                                         ACT.Copy, scale=qkT[:, 0:1]).then_inc(q_rows, 1)
                elif kind == "scoresT":
                    for i, b in enumerate(key_blocks(br, c)):
                        k = st_before[br, u] + i
                        n = cmp_keys(c) if br == CMP else P
                        act.wait_ge(st_full, k + 1)
                        nc.scalar.activation(pT[br][0:n, i, :], ps[0:n, 4 + k % 2, :], ACT.Exp).then_inc(exp_done, 1)

        @block.vector
        def _(dve):
            o = Order(dve, ord_dve)
            nc.vector.tensor_copy(masksb[:, :, :].rearrange("p a b -> p (a b)"), M["stage_masks"]).then_inc(consts, 1)
            nc.vector.tensor_copy(mask_cmp[:, :, 0:N_CMP],
                                  M["stage_cmp"].rearrange("p (c n) -> p c n", c=NT)).then_inc(consts, 1)
            nc.vector.tensor_copy(mask_cmpT[0:N_CMP, :, :].rearrange("p c n -> p (c n)"), M["stage_cmpT"]).then_inc(consts, 1)
            nc.vector.tensor_copy(identb[:, :], ident[:, :]).then_inc(consts, 1)
            dve.wait_ge(consts, 4)
            dve.wait_ge(gates_exp, 1)
            o.done(nc.vector.tensor_scalar(M["sg"], M["sg"], 1.0, None, ALU.add))
            o.done(nc.vector.reciprocal(M["sg"], M["sg"]))

            def maxima(br, u):
                c = u // NG
                for i, heads in enumerate(score_slots(br, c)):
                    k = slots_before[br, u] + i
                    dve.wait_ge(slot_full, k + 1)
                    h0, b0 = heads[0], 2 * (k % 2)
                    if br == CMP:
                        src = ps[:, b0, 0:4 * 64].rearrange("p (h n) -> p h n", h=GQ)[:, :, 0:cmp_keys(c)]
                    elif len(heads) == 2:
                        src = ps[:, b0:b0 + 2, 0:len(key_blocks(br, c)) * P]
                    else:
                        src = ps[:, b0:b0 + 2, :].rearrange("p b n -> p (b n)")[:, 0:(c + 1) * P].unsqueeze(1)
                    ins = nc.vector.tensor_reduce(neg[:, br, h0:h0 + len(heads)], src, AX.X, ALU.max, negate=True)
                    ins.then_inc(slot_read, 1)
                dve.wait_ge(slot_read, k + 1)
                nc.vector.tensor_scalar(neg[:, br, :], neg[:, br, :], 1.0e20, None, ALU.min).then_inc(max_ready, 1)

            def maxima_to_rows(br, u):
                dve.wait_ge(max_full, max_before[br, u] + 1)
                nc.vector.tensor_tensor(Q[ROW_MAX:ROW_MAX + GQ, br, u % NG, :].rearrange("p (h q) -> p h q", h=GQ),
                                        ps[0:GQ, 7, 0:P].unsqueeze(1).broadcast_to([GQ, GQ, P]),
                                        head_delta.rearrange("p (h q) -> p h q", h=GQ), ALU.mult).then_inc(max_rows, 1)

            def read_values(br, u):
                c, g = u // NG, u % NG
                dve.wait_ge(o_full, o_before[br, u] + 1)
                w = HD + 17 if br == CMP else HD + 1
                O = ps[:, 6, 0:GQ * w].rearrange("p (h n) -> p h n", h=GQ)
                dst = o_att[:, c, g * GQ * HD:(g + 1) * GQ * HD].rearrange("p (h d) -> p h d", h=GQ)
                gate_at = {CMP: 0, SEL: 1, WIN: 2}[br]
                d, f = den[:, br, :], coef[:, br, :]
                o.done(nc.vector.tensor_scalar(d, O[:, :, HD], 1.0e-30, None, ALU.max))
                o.done(nc.vector.reciprocal(d, d))
                o.done(nc.vector.tensor_tensor(f, d, sg[:, c, g * GQ:(g + 1) * GQ, gate_at], ALU.mult))
                fb = f.unsqueeze(2).broadcast_to([P, GQ, HD])
                if br == CMP:
                    if c >= NT // 2:
                        o.mark(nc.vector.tensor_tensor(imp_h.rearrange("p (h j) -> p h j", h=GQ), O[:, :, HD + 1:w],
                                                       d.unsqueeze(2).broadcast_to([P, GQ, N_BLK]), ALU.mult))
                    o.mark(nc.vector.tensor_tensor(dst, O[:, :, 0:HD], fb, ALU.mult))
                    o.wait()
                    dve.sem_inc(o_read, 1)
                else:
                    nc.vector.tensor_tensor(o_tmp, O[:, :, 0:HD], fb, ALU.mult).then_inc(o_read, 1)
                    dve.wait_ge(o_read, o_before[br, u] + 1)
                    o.done(nc.vector.tensor_tensor(dst, dst, o_tmp, ALU.add))

            def select(u):
                c = u // NG
                o.done(nc.vector.tensor_reduce(imp, imp_h.rearrange("p (h j) -> p j h", h=GQ), AX.X, ALU.add))
                o.done(nc.vector.tensor_tensor(score, imp, score_rows[:, 0, c, :], ALU.mult))
                o.done(nc.vector.tensor_tensor(score, score, score_rows[:, 1, c, :], ALU.add))
                si = score.unsqueeze(1).broadcast_to([P, N_BLK, N_BLK])
                sj = score.unsqueeze(2).broadcast_to([P, N_BLK, N_BLK])
                g3, e3 = gt.rearrange("p (j i) -> p j i", j=N_BLK), eq.rearrange("p (j i) -> p j i", j=N_BLK)
                o.mark(nc.vector.tensor_tensor(g3, si, sj, ALU.is_gt))
                o.done(nc.vector.tensor_tensor(e3, si, sj, ALU.is_equal))
                o.done(nc.vector.tensor_tensor(e3, e3, before, ALU.mult))
                o.done(nc.vector.tensor_tensor(g3, g3, e3, ALU.add))
                o.done(nc.vector.tensor_reduce(rank, g3, AX.X, ALU.add))
                nc.vector.tensor_scalar(M["sel01"], rank, float(TOP_N) - 0.5, None, ALU.is_lt).then_inc(sel_ready, 1)

            def selection_to_rows(u):
                dve.wait_ge(sel_full, sel_before[u] + 1)
                nc.vector.tensor_scalar(Q[ROW_SEL:ROW_SEL + N_BLK, SEL, u % NG, :].rearrange("p (h q) -> p h q", h=GQ),
                                        ps[64:64 + N_BLK, 7, 0:P].unsqueeze(1).broadcast_to([N_BLK, GQ, P]),
                                        -1.0, -NEG, ALU.add, ALU.mult).then_inc(sel_rows, 1)

            for kind, br, u in steps:
                c, g = u // NG, u % NG
                if kind == "queriesT":
                    dve.wait_ge(q_full, u + 1)
                    nc.vector.tensor_scalar(Q[0:HD, CMP, g, :], ps[0:HD, 6, :], qkT[:, 0:1], None, ALU.mult)\
                        .then_inc(q_cmp_rows, 1)
                elif kind == "scores":
                    maxima(br, u)
                elif kind == "maxT":
                    maxima_to_rows(br, u)
                elif kind == "selT":
                    selection_to_rows(u)
                elif kind == "values":
                    read_values(br, u)
                    if br == CMP and c >= NT // 2:
                        select(u)


def ssd(nc, N, M, A, C, out):
    sem = N.sem
    ps, ident, identb, conv, z, tri = M["ps"], M["ident"], M["identb"], M["conv"], M["z"], M["tri"]
    u = M["big_u"]
    x_dt = u[:, 0:1024].rearrange("p (b h d) -> p b h d", b=2, h=SH)
    x_decay = u[:, 1024:2048].rearrange("p (b h d) -> p b h d", b=2, h=SH)
    x_skip = u[:, 2048:3072].rearrange("p (b h d) -> p b h d", b=2, h=SH)
    mT = u[:, 3072:5120].rearrange("p (b h l) -> p b h l", b=2, h=SH)
    decT = u[:, 5120:7168].rearrange("p (b h l) -> p b h l", b=2, h=SH)
    b_nat = u[:, 7168:7680].rearrange("p (b g n) -> p b g n", b=2, g=NG)
    state = u[:, 7680:8192].rearrange("p (h d) -> p h d", h=SH)
    y = M["misc"][:, 0:1024].rearrange("p (b h d) -> p b h d", b=2, h=SH)
    ones = M["misc"][:, 1024:1024 + P]
    junk = M["misc"][:, 2048:2048 + 256]
    sm = M["small"]
    part = lambda i: sm[:, 64 * i:64 * i + 64].rearrange("p (c h) -> p c h", c=NT)
    flat = lambda i: sm[:, 64 * i:64 * i + 64]
    dt, a, neg_cs, decay, e_cs, e_tot, tmp = (part(i) for i in range(7))
    M["ss_ssm"] = sm[:, 448:464]
    o_ssm = M["qn"]
    GW = 4 * HD

    prep_full, prep_done = sem("ssd_constants_full"), sem("ssd_constants_ready")
    dt_sem = sem("dt_steps")
    pre_full = sem("chunk_operands_full")
    x_read, b_read, cb_read, dec_read = sem("x_natural_read"), sem("b_natural_read"), sem("cb_read"), sem("decay_read")
    y_full, y_read = sem("y_full"), sem("y_read")
    st_full, st_ready = sem("new_states_full"), sem("state_ready")
    y_ready, y_squared = sem("y_ready"), sem("y_squared")
    ord_dve, ord_act = sem("vector_order3"), sem("scalar_order3")
    set_up = sem("ssd_set_up")
    X_BANK, CB_BANK, DEC_BANK, YD_BANK, YO_BANK, ST_BANK = 0, 1, 2, 4, 5, 6

    with nc.Block() as block:
        @block.sync
        def _(sp):
            for k in range(KD):
                sp.dma_start(M["big_w"][:, k * D:(k + 1) * D], A["w_out"][0, k * P:(k + 1) * P, :]).then_inc(M["s_w_out"], 16)

        @block.gpsimd
        def _(pool):
            nc.gpsimd.memset(ones, 1.0).then_inc(set_up, 1)
            nc.gpsimd.memset(u[:, 7680:8192], 0.0).then_inc(set_up, 1)

        @block.tensor
        def _(pe):
            pe.wait_ge(set_up, 2)
            pe.wait_ge(dt_sem, 6)
            nc.tensor.matmul(ps[:, 7, 0:64], tri[:, :], flat(1), start=True, stop=True)
            nc.tensor.matmul(ps[:, 7, 64:128], ones, flat(1), start=True, stop=True).then_inc(prep_full, 1)

            def operands(c):
                tok = slice(3 + c * P, 3 + (c + 1) * P)
                if c >= 1:
                    pe.wait_ge(x_read, c)
                for m in range(4):
                    nc.tensor.transpose(ps[:, X_BANK, m * P:(m + 1) * P], conv[:, m, tok], ident[:, :])
                if c >= 1:
                    pe.wait_ge(b_read, c)
                    pe.wait_ge(cb_read, NG * c)
                for g in range(NG):
                    nc.tensor.transpose(ps[:, CB_BANK, g * P:(g + 1) * P], conv[:, 4 + g, tok], ident[:, :])
                for g in range(NG):
                    nc.tensor.matmul(ps[:, CB_BANK, (2 + g) * P:(3 + g) * P], conv[:, 4 + g, tok], conv[:, 6 + g, tok],
                                     start=True, stop=True)
                if c >= 1:
                    pe.wait_ge(dec_read, NG * c)
                for g in range(NG):
                    o = ps[:, DEC_BANK + g, :]
                    nc.tensor.matmul(o, identb[:, :], M["masksb"][:, 1, :].unsqueeze(1).broadcast_to([P, GQ, P]),
                                     start=True, stop=True, skip_group_check=True)
                    for r in range(GQ):
                        last = nc.tensor.matmul(o[:, r * P:(r + 1) * P],
                                                a[:, c, g * GQ + r:g * GQ + r + 1].broadcast_to([P, P]), tri[:, :],
                                                start=False, stop=True, skip_group_check=True)
                last.then_inc(pre_full, 1)

            operands(0)
            for c in range(NT):
                tok = slice(3 + c * P, 3 + (c + 1) * P)
                if c + 1 < NT:
                    operands(c + 1)
                if c >= 1:
                    pe.wait_ge(y_read, c)
                    pe.wait_ge(st_ready, c)
                    for g in range(NG):
                        nc.tensor.matmul(ps[:, YO_BANK, g * GW:(g + 1) * GW], conv[:, 6 + g, tok],
                                         state[:, g * GQ:(g + 1) * GQ, :], start=True, stop=True)
                pe.wait_ge(b_read, c + 1)
                pe.wait_ge(cb_read, NG * (c + 1))
                for h in range(SH):
                    last = nc.tensor.matmul(ps[:, YD_BANK, h * HD:(h + 1) * HD], mT[:, c % 2, h, :], x_dt[:, c % 2, h, :],
                                            start=True, stop=True)
                last.then_inc(y_full, 1)
                if c + 1 < NT:
                    for g in range(NG):
                        last = nc.tensor.matmul(ps[:, ST_BANK, g * GW:(g + 1) * GW], b_nat[:, c % 2, g, :],
                                                x_decay[:, c % 2, g * GQ:(g + 1) * GQ, :], start=True, stop=True)
                    last.then_inc(st_full, 1)

        @block.scalar
        def _(act):
            o = Order(act, ord_act)
            act.wait_ge(dt_sem, 2)
            o.done(nc.scalar.activation(flat(0), flat(6), ACT.Exp, scale=-1.0))
            o.mark(nc.scalar.activation(M["head_rows"][:, 1, :], M["head_rows"][:, 1, :], ACT.Exp))
            o.wait()
            nc.scalar.activation(flat(0), flat(0), ACT.Ln, bias=1.0).then_inc(dt_sem, 1)
            act.wait_ge(dt_sem, 8)
            for i in (3, 4, 5):
                nc.scalar.activation(flat(i), flat(i), ACT.Exp).then_inc(prep_done, 1)

            def square(c):
                act.wait_ge(y_ready, c + 1)
                for g in range(NG):
                    o.done(nc.scalar.activation(junk, o_ssm[:, c, g * GW:(g + 1) * GW], ACT.Square,
                                                accum_out=M["ss_ssm"][:, NG * c + g:NG * c + g + 1]))

            for c in range(NT):
                act.wait_ge(pre_full, c + 1)
                if c >= 2:
                    act.wait_ge(y_full, c - 1)
                    act.wait_ge(st_full, c - 1)
                nc.scalar.activation(b_nat[:, c % 2, :, :], ps[:, CB_BANK, 0:2 * P].rearrange("p (g n) -> p g n", g=NG),
                                     ACT.Copy).then_inc(b_read, 1)
                for g in range(NG):
                    for r in range(GQ):
                        h = g * GQ + r
                        last = nc.scalar.activation(decT[:, c % 2, h, :], ps[:, DEC_BANK + g, r * P:(r + 1) * P], ACT.Exp,
                                                    bias=neg_cs[:, c, h:h + 1])
                    last.then_inc(dec_read, 1)
                if c >= 2:
                    square(c - 2)
            square(NT - 2)
            square(NT - 1)

        @block.vector
        def _(dve):
            o = Order(dve, ord_dve)
            rows = M["head_rows"]
            o.done(nc.vector.tensor_tensor(dt, M["gate_dt"][:, :, NGATE:], rows[:, 0, :].unsqueeze(1).broadcast_to([P, NT, SH]),
                                           ALU.add))
            nc.vector.tensor_scalar(flat(1), flat(0), 0.0, None, ALU.max).then_inc(dt_sem, 1)
            dve.wait_ge(dt_sem, 1)
            nc.vector.scalar_tensor_tensor(flat(6), flat(1), 2.0, flat(0), ALU.mult, ALU.subtract).then_inc(dt_sem, 1)
            dve.wait_ge(dt_sem, 3)
            nc.vector.tensor_tensor(flat(0), flat(0), flat(1), ALU.add).then_inc(dt_sem, 1)
            dve.wait_ge(dt_sem, 4)
            nc.vector.tensor_scalar(flat(6), flat(0), -1.0, None, ALU.mult).then_inc(dt_sem, 1)
            dve.wait_ge(dt_sem, 5)
            nc.vector.tensor_tensor(a, tmp, rows[:, 1, :].unsqueeze(1).broadcast_to([P, NT, SH]), ALU.mult).then_inc(dt_sem, 1)
            dve.wait_ge(prep_full, 1)
            o.mark(nc.vector.tensor_scalar(flat(2), ps[:, 7, 0:64], -1.0, None, ALU.mult))
            o.mark(nc.vector.tensor_copy(flat(4), ps[:, 7, 0:64]))
            o.done(nc.vector.tensor_copy(flat(5), ps[:, 7, 64:128]))
            nc.vector.tensor_tensor(flat(3), flat(5), flat(4), ALU.subtract).then_inc(dt_sem, 1)
            dve.wait_ge(dt_sem, 7)
            nc.vector.tensor_copy(flat(6)[:, 0:1], flat(3)[:, 0:1]).then_inc(dt_sem, 1)

            def heads(v):
                return v.unsqueeze(2).broadcast_to([P, v.shape[1], HD])

            def chunk_in(c):
                dve.wait_ge(pre_full, c + 1)
                b = c % 2
                if c >= 2:
                    dve.wait_ge(y_full, c - 1)
                    dve.wait_ge(st_full, c - 1)
                xs = ps[:, X_BANK, :].rearrange("p (h d) -> p h d", h=SH)
                o.mark(nc.vector.tensor_tensor(x_dt[:, b], xs, heads(dt[:, c, :]), ALU.mult))
                nc.vector.tensor_tensor(x_skip[:, b], xs, heads(rows[:, 2, :]), ALU.mult).then_inc(x_read, 1)
                o.wait()
                o.done(nc.vector.tensor_tensor(x_decay[:, b], x_dt[:, b], heads(decay[:, c, :]), ALU.mult))
                dve.wait_ge(b_read, c + 1)
                for g in range(NG):
                    dve.wait_ge(dec_read, NG * c + g + 1)
                    nc.vector.tensor_tensor(mT[:, b, g * GQ:(g + 1) * GQ, :], decT[:, b, g * GQ:(g + 1) * GQ, :],
                                            ps[:, CB_BANK, (2 + g) * P:(3 + g) * P].unsqueeze(1).broadcast_to([P, GQ, P]),
                                            ALU.mult).then_inc(cb_read, 1)

            def chunk_out(c):
                b = c % 2
                yb = y[:, b]
                dve.wait_ge(y_full, c + 1)
                dve.wait_ge(x_read, c + 1)
                o.done(nc.vector.tensor_tensor(yb, ps[:, YD_BANK, :].rearrange("p (h d) -> p h d", h=SH), x_skip[:, b],
                                               ALU.add))
                if c >= 1:
                    o.done(nc.vector.tensor_tensor(x_skip[:, b], ps[:, YO_BANK, :].rearrange("p (h d) -> p h d", h=SH),
                                                   heads(e_cs[:, c, :]), ALU.mult))
                dve.sem_inc(y_read, 1)
                if c + 1 < NT:
                    o.done(nc.vector.tensor_tensor(state, state, heads(e_tot[:, c, :]), ALU.mult))
                    dve.wait_ge(st_full, c + 1)
                    nc.vector.tensor_tensor(state, state, ps[:, ST_BANK, :].rearrange("p (h d) -> p h d", h=SH),
                                            ALU.add).then_inc(st_ready, 1)
                if c >= 1:
                    o.done(nc.vector.tensor_tensor(yb, yb, x_skip[:, b], ALU.add))
                nc.vector.tensor_tensor(o_ssm[:, c, :].rearrange("p (h d) -> p h d", h=SH), yb,
                                        z[:, c, :].rearrange("p (h d) -> p h d", h=SH), ALU.mult).then_inc(y_ready, 1)

            dve.wait_ge(prep_done, 3)
            dve.wait_ge(set_up, 2)
            chunk_in(0)
            for c in range(NT):
                if c + 1 < NT:
                    chunk_in(c + 1)
                chunk_out(c)


def load_expert(sp, M, A, e, r):
    ws = bass.ds(e, 1)
    gu = M["ring_gu"][:, r * GU_COLS:(r + 1) * GU_COLS].rearrange("p (k n) -> p k n", k=KD)
    dn = M["ring_d"][:, r * D_COLS:(r + 1) * D_COLS].rearrange("p (f n) -> p f n", f=D_EXP // P)
    for i, name in enumerate(("w_gate", "w_up")):
        sp.dma_start(gu[:, :, i * D_EXP:(i + 1) * D_EXP],
                     A[name][0, ws].rearrange("e (k p) n -> p (e k) n", p=P)).then_inc(M["s_expert"][r], 16)
    sp.dma_start(dn, A["w_down"][0, ws].rearrange("e (f p) n -> p (e f) n", p=P)).then_inc(M["s_expert"][r], 16)


def merge(nc, N, M, A, C, out):
    sem = N.sem
    ps, ident, vecT = M["ps"], M["ident"], M["vecT"]
    u = M["big_u"]
    catT = u[:, 0:2048].rearrange("p (b k t) -> p b k t", b=2, k=KD)
    hnT = u[:, 2048:3072].rearrange("p (k t) -> p k t", k=KD)
    hn = u[:, 3072:5120].rearrange("p (b n) -> p b n", b=2)
    at = [5120]

    def cols(n, base=u, at=at):
        at[0] += n
        return base[:, at[0] - n:at[0]]

    NR = 4 + N_EXP
    rw = cols(KD * NR).rearrange("p (k n) -> p k n", k=KD)
    edges, iota, token, tri_strict, before_, bias = cols(EDGES), cols(P), cols(NT), cols(P), cols(256), cols(NR)
    before = before_.rearrange("p (j i) -> p j i", j=N_BLK)
    lg = cols(NT * NR).rearrange("p (c n) -> p c n", c=NT)
    ge = cols(2 * NT * EDGES).rearrange("p (i s) -> p i s", s=EDGES)
    c1, c2, t4 = cols(NT * 16), cols(NT * 16), cols(NT * 16)
    H = [cols(P), cols(P)]
    both, pos, base = cols(P), cols(P), cols((NT + 1) * N_EXP)
    gmax, gp, l1, l2, d21, spare = (cols(NT) for _ in range(6))
    g4, e4, r4, oh_g, oh1, oh2 = (cols(NT * 4).rearrange("p (c n) -> p c n", c=NT) for _ in range(6))
    tiles, start, end_, st128 = (cols(N_EXP) for _ in range(4))
    posk, slot, place, wk = (cols(2 * NT) for _ in range(4))
    assert at[0] <= KD * S
    x_in = M["misc"][:, 0:2048].rearrange("p (b n) -> p b n", b=2)
    hot = M["misc"][:, 0:1024].rearrange("p (i s) -> p i s", s=64)[:, :, 0:TABLE]
    e_cmp = M["misc"][0:1, 1024:1536].rearrange("p (s e) -> p s e", e=N_EXP)
    e_sum = M["misc"][0:1, 1536:1536 + TABLE]
    place_hot = u[:, 0:2048].rearrange("p (i n) -> p i n", n=P)
    values = u[:, 2048:3072].rearrange("p (i n) -> p i n", n=2 * TABLE)
    w_out = M["big_w"][:, :].rearrange("p (k n) -> p k n", k=KD)
    h = M["conv"][:, :, 0:D]
    o_att, o_ssm = M["o_att"], M["qn"]
    junk = M["ring_gu"][:, 4096:4096 + D]
    rs = M["small"]
    ss_att, rs_att, rs_ssm, ss_h, rs_h = rs[:, 464:472], rs[:, 472:480], rs[:, 480:496], rs[:, 496:504], rs[:, 504:512]

    s_x = [sem("x_again_loaded0"), sem("x_again_loaded1")]
    s_route = sem("router_loaded")
    s_hn = [sem("hn_stored0"), sem("hn_stored1")]
    cat_ready, cat_full, cat_evac = sem("cat_scaled"), sem("catT_full"), sem("catT_ready")
    o_full, h_ready, rs_ready, hn_ready = sem("out_full"), sem("h_ready"), sem("h_rstd_ready"), sem("hn_ready")
    hnT_full, hnT_evac, lg_full = sem("hnT_full"), sem("hnT_ready"), sem("logits_full")
    stat = sem("mixer_squares")
    plan, act_plan = sem("vector_plan_steps"), sem("scalar_plan_steps")
    route_in, route_out = sem("pair_counts_in"), sem("pair_counts_full")
    tab_in, tab_out = sem("table_operands"), sem("table_full")
    ones_set = sem("ones_set")
    ord_dve, ord_act = sem("vector_order4"), sem("scalar_order4")
    ones = M["misc"][:, 3072 - P:3072]

    with nc.Block() as block:
        @block.sync
        def _(sp):
            def load_x(c):
                if c >= 2:
                    sp.wait_ge(h_ready, c - 1)
                sp.dma_start(x_in[:, c % 2, :], A["x"][0, c * P:(c + 1) * P, :]).then_inc(s_x[c % 2], 16)

            load_x(0)
            load_x(1)
            sp.dma_start(rw[:, :, 0:4], A["router_g_w"][0].rearrange("(k p) n -> p k n", p=P)).then_inc(s_route, 16)
            sp.dma_start(rw[:, :, 4:NR], A["router_e_w"][0].rearrange("(k p) n -> p k n", p=P)).then_inc(s_route, 16)
            sp.dma_start(bias[:, 0:4], A["router_g_b"][0].partition_broadcast(P)).then_inc(s_route, 16)
            sp.dma_start(bias[:, 4:NR], A["router_e_b"][0].partition_broadcast(P)).then_inc(s_route, 16)
            sp.dma_start(edges, C["slot_edges"]).then_inc(s_route, 16)
            sp.dma_start(iota, C["iota"]).then_inc(s_route, 16)
            sp.dma_start(token, C["token"]).then_inc(s_route, 16)
            sp.dma_start(tri_strict, C["tri_strict"]).then_inc(s_route, 16)
            sp.dma_start(before_, C["before"].partition_broadcast(P)).then_inc(s_route, 16)
            load_expert(sp, M, A, 0, 0)
            for c in range(NT):
                if c + 2 < NT:
                    load_x(c + 2)
                sp.wait_ge(hn_ready, c + 1)
                sp.dma_start(M["hn_dram"][c * P:(c + 1) * P, :], hn[:, c % 2, :]).then_inc(s_hn[c % 2], 16)
            load_expert(sp, M, A, 1, 1)
            for b in range(2):
                sp.wait_ge(s_hn[b], 16 * NT // 2)

        @block.gpsimd
        def _(pool):
            nc.gpsimd.memset(ones, 1.0).then_inc(ones_set, 1)

        @block.tensor
        def _(pe):
            def cat_transposes(c):
                pe.wait_ge(cat_ready, 3 * (c + 1))
                if c >= 1:
                    pe.wait_ge(cat_evac, 2 * c)
                for k in range(KD):
                    src = o_att[:, c, k * P:(k + 1) * P] if k < 4 else o_ssm[:, c, (k - 4) * P:(k - 3) * P]
                    last = nc.tensor.transpose(ps[:, k // 4, (k % 4) * P:(k % 4 + 1) * P], src, ident[:, :])
                    if k % 4 == 3:
                        last.then_inc(cat_full, 1)

            def project_out(c):
                pe.wait_ge(cat_evac, 2 * (c + 1))
                if c >= 1:
                    pe.wait_ge(h_ready, c)
                for half in range(2):
                    for k in range(KD):
                        last = nc.tensor.matmul(ps[:, 2 + half, :], catT[:, c % 2, k, :],
                                                w_out[:, k, half * BANK:(half + 1) * BANK], start=(k == 0), stop=(k == KD - 1))
                last.then_inc(o_full, 1)

            def hn_transposes(c):
                pe.wait_ge(hn_ready, c + 1)
                if c >= 1:
                    pe.wait_ge(hnT_evac, 2 * c)
                for k in range(KD):
                    last = nc.tensor.transpose(ps[:, 4 + k // 4, (k % 4) * P:(k % 4 + 1) * P],
                                               hn[:, c % 2, k * P:(k + 1) * P], ident[:, :])
                    if k % 4 == 3:
                        last.then_inc(hnT_full, 1)

            def route(c):
                pe.wait_ge(hnT_evac, 2 * (c + 1))
                for k in range(KD):
                    last = nc.tensor.matmul(ps[:, 6, c * NR:(c + 1) * NR], hnT[:, k, :], rw[:, k, :],
                                            start=(k == 0), stop=(k == KD - 1))
                last.then_inc(lg_full, 1)

            pe.wait_ge(M["s_w_out"], 16 * KD)
            cat_transposes(0)
            for c in range(NT):
                project_out(c)
                if c == 1:
                    pe.wait_ge(s_route, 9 * 16)
                if c >= 2:
                    route(c - 2)
                if c >= 1:
                    hn_transposes(c - 1)
                if c + 1 < NT:
                    cat_transposes(c + 1)
            route(NT - 2)
            hn_transposes(NT - 1)
            route(NT - 1)
            pe.wait_ge(ones_set, 1)
            pe.wait_ge(route_in, 1)
            nc.tensor.matmul(ps[:, 7, 0:P], tri_strict, both, start=True, stop=True)
            nc.tensor.matmul(ps[:, 7, P:2 * P], ones, both, start=True, stop=True).then_inc(route_out, 1)
            pe.wait_ge(tab_in, 3)
            for i in range(2 * NT):
                last = nc.tensor.matmul(ps[:, 6, 0:2 * TABLE], place_hot[:, i, :], values[:, i, :],
                                        start=(i == 0), stop=(i == 2 * NT - 1))
            last.then_inc(tab_out, 1)

        @block.scalar
        def _(act):
            o = Order(act, ord_act)
            nc.scalar.preload_act_table_set("natural_log_exp_and_others")
            for c in range(NT):
                o.done(nc.scalar.activation(junk[:, 0:512], o_att[:, c, :], ACT.Square, accum_out=ss_att[:, c:c + 1]))
            o.mark(nc.scalar.activation(rs_att, ss_att, ACT.Ln, scale=1.0 / 512, bias=M["eps"][:, 0:1]))
            o.done(nc.scalar.activation(rs_ssm, M["ss_ssm"], ACT.Ln, scale=1.0 / 256, bias=M["eps"][:, 0:1]))
            o.mark(nc.scalar.activation(rs_att, rs_att, ACT.Exp, scale=-0.5))
            o.done(nc.scalar.activation(rs_ssm, rs_ssm, ACT.Exp, scale=-0.5))

            def scale_cat(c):
                nc.scalar.activation(o_att[:, c, :], o_att[:, c, :], ACT.Copy, scale=rs_att[:, c:c + 1]).then_inc(cat_ready, 1)
                for g in range(NG):
                    v = o_ssm[:, c, g * 256:(g + 1) * 256]
                    nc.scalar.activation(v, v, ACT.Copy, scale=rs_ssm[:, NG * c + g:NG * c + g + 1]).then_inc(cat_ready, 1)

            def h_stats(c):
                act.wait_ge(h_ready, c + 1)
                o.done(nc.scalar.activation(junk, h[:, c, :], ACT.Square, accum_out=ss_h[:, c:c + 1]))
                o.done(nc.scalar.activation(rs_h[:, c:c + 1], ss_h[:, c:c + 1], ACT.Ln, scale=1.0 / D, bias=M["eps"][:, 0:1]))
                nc.scalar.activation(rs_h[:, c:c + 1], rs_h[:, c:c + 1], ACT.Exp, scale=-0.5).then_inc(rs_ready, 1)

            scale_cat(0)
            for c in range(NT):
                if c + 1 < NT:
                    scale_cat(c + 1)
                h_stats(c)
            act.wait_ge(act_plan, 1)
            nc.scalar.activation(g4, g4, ACT.Exp).then_inc(act_plan, 1)
            act.wait_ge(act_plan, 3)
            nc.scalar.activation(d21, d21, ACT.Exp).then_inc(act_plan, 1)

        @block.vector
        def _(dve):
            o = Order(dve, ord_dve)
            tt, ts = nc.vector.tensor_tensor, nc.vector.tensor_scalar

            def cat_evacuate(c):
                for j in range(2):
                    dve.wait_ge(cat_full, 2 * c + j + 1)
                    tt(catT[:, c % 2, 4 * j:4 * j + 4, :], ps[:, j, :].rearrange("p (k t) -> p k t", k=4),
                       vecT[:, M["V_AON"] + 4 * j:M["V_AON"] + 4 * j + 4].unsqueeze(2).broadcast_to([P, 4, P]),
                       ALU.mult).then_inc(cat_evac, 1)

            def residual(c):
                dve.wait_ge(o_full, c + 1)
                dve.wait_ge(s_x[c % 2], 16 * (c // 2 + 1))
                tt(h[:, c, :], ps[:, 2:4, :].rearrange("p b n -> p (b n)"), x_in[:, c % 2, :], ALU.add).then_inc(h_ready, 1)

            def normalise(c):
                dve.wait_ge(rs_ready, c + 1)
                if c >= 2:
                    dve.wait_ge(s_hn[c % 2], 16 * (c // 2))
                    dve.wait_ge(hnT_full, 2 * (c - 1))
                ts(hn[:, c % 2, :], h[:, c, :], rs_h[:, c:c + 1], None, ALU.mult).then_inc(hn_ready, 1)

            def hn_evacuate(c):
                if c >= 1:
                    dve.wait_ge(lg_full, c)
                for j in range(2):
                    dve.wait_ge(hnT_full, 2 * c + j + 1)
                    tt(hnT[:, 4 * j:4 * j + 4, :], ps[:, 4 + j, :].rearrange("p (k t) -> p k t", k=4),
                       vecT[:, M["V_FFN"] + 4 * j:M["V_FFN"] + 4 * j + 4].unsqueeze(2).broadcast_to([P, 4, P]),
                       ALU.mult).then_inc(hnT_evac, 1)

            cat_evacuate(0)
            for c in range(NT):
                residual(c)
                normalise(c)
                if c >= 1:
                    hn_evacuate(c - 1)
                if c + 1 < NT:
                    cat_evacuate(c + 1)
            hn_evacuate(NT - 1)

            dve.wait_ge(lg_full, NT)
            dve.wait_ge(s_route, 9 * 16)
            o.done(tt(lg, ps[:, 6, 0:NT * NR].rearrange("p (c n) -> p c n", c=NT),
                      bias.unsqueeze(1).broadcast_to([P, NT, NR]), ALU.add))
            G = lg[:, :, 0:4]
            q4 = lambda v: v.rearrange("p (c j i) -> p c j i", c=NT, j=4)

            def rank(v, r):
                vi = v.unsqueeze(2).broadcast_to([P, NT, 4, 4])
                vj = v.unsqueeze(3).broadcast_to([P, NT, 4, 4])
                o.mark(tt(q4(c1), vi, vj, ALU.is_gt))
                o.done(tt(q4(c2), vi, vj, ALU.is_equal))
                o.done(tt(q4(c2), q4(c2), before[:, 0:4, 0:4].unsqueeze(1).broadcast_to([P, NT, 4, 4]), ALU.mult))
                o.done(tt(c1, c1, c2, ALU.add))
                o.done(nc.vector.tensor_reduce(r, q4(c1), AX.X, ALU.add))

            o.done(nc.vector.tensor_reduce(gmax, G, AX.X, ALU.max))
            tt(g4, G, gmax.unsqueeze(2).broadcast_to([P, NT, 4]), ALU.subtract).then_inc(act_plan, 1)
            rank(G, r4)
            o.done(ts(oh_g, r4, 0.0, None, ALU.is_equal))
            o.done(tt(q4(t4), lg[:, :, 4:NR].rearrange("p c (g e) -> p c g e", g=4),
                      oh_g.unsqueeze(3).broadcast_to([P, NT, 4, 4]), ALU.mult))
            o.done(nc.vector.tensor_reduce(e4, q4(t4).rearrange("p c g e -> p c e g"), AX.X, ALU.add))
            rank(e4, r4)
            o.mark(ts(oh1, r4, 0.0, None, ALU.is_equal))
            o.done(ts(oh2, r4, 1.0, None, ALU.is_equal))
            for k, oh in enumerate((oh1, oh2)):
                o.mark(tt(q4(H[k]), oh_g.unsqueeze(3).broadcast_to([P, NT, 4, 4]),
                          oh.unsqueeze(2).broadcast_to([P, NT, 4, 4]), ALU.mult))
            o.wait()
            tt(both, H[0], H[1], ALU.add).then_inc(route_in, 1)
            for oh, lv in ((oh1, l1), (oh2, l2)):
                o.done(tt(r4, e4, oh, ALU.mult))
                o.done(nc.vector.tensor_reduce(lv, r4, AX.X, ALU.add))
            dve.wait_ge(act_plan, 2)
            tt(d21, l2, l1, ALU.subtract).then_inc(act_plan, 1)
            o.done(nc.vector.tensor_reduce(gp, g4, AX.X, ALU.add))
            o.done(nc.vector.reciprocal(gp, gp))
            dve.wait_ge(act_plan, 4)
            o.done(ts(spare, d21, 1.0, None, ALU.add))
            o.done(nc.vector.reciprocal(spare, spare))
            o.done(tt(wk[:, 0:NT], spare, gp, ALU.mult))
            o.done(tt(wk[:, NT:2 * NT], wk[:, 0:NT], d21, ALU.mult))
            dve.wait_ge(route_out, 1)
            o.done(nc.vector.memset(base[:, 0:N_EXP], 0.0))
            for c in range(NT):
                o.done(tt(base[:, (c + 1) * N_EXP:(c + 2) * N_EXP], ps[:, 7, P + c * N_EXP:P + (c + 1) * N_EXP],
                          base[:, c * N_EXP:(c + 1) * N_EXP], ALU.add))
            n_e = base[:, NT * N_EXP:]
            o.done(tt(c1.rearrange("p (e k) -> p e k", k=NT), n_e.unsqueeze(2).broadcast_to([P, N_EXP, NT]),
                      edges[:, 0:NT].unsqueeze(1).broadcast_to([P, N_EXP, NT]), ALU.is_gt))
            o.done(nc.vector.tensor_reduce(tiles, c1.rearrange("p (e k) -> p e k", k=NT), AX.X, ALU.add))
            g16 = ge.rearrange("p i s -> p (i s)")[:, 0:256].rearrange("p (j i) -> p j i", j=N_EXP)
            o.done(tt(g16, before, tiles.unsqueeze(1).broadcast_to([P, N_EXP, N_EXP]), ALU.mult))
            o.done(nc.vector.tensor_reduce(start, g16, AX.X, ALU.add))
            o.mark(tt(end_, start, tiles, ALU.add))
            o.done(ts(st128, start, float(P), None, ALU.mult))
            pos3 = pos.rearrange("p (c e) -> p c e", c=NT)
            o.done(tt(pos, ps[:, 7, 0:P], base[:, 0:P], ALU.add))
            o.done(tt(pos3, pos3, st128.unsqueeze(1).broadcast_to([P, NT, N_EXP]), ALU.add))
            for k in range(2):
                o.done(tt(t4, H[k], pos, ALU.mult))
                o.done(nc.vector.tensor_reduce(posk[:, k * NT:(k + 1) * NT], t4.rearrange("p (c e) -> p c e", c=NT),
                                               AX.X, ALU.add))
            o.mark(nc.vector.tensor_copy(M["slot_pos"], posk))
            o.done(tt(ge, posk.unsqueeze(2).broadcast_to([P, 2 * NT, EDGES]),
                      edges.unsqueeze(1).broadcast_to([P, 2 * NT, EDGES]), ALU.is_ge))
            o.mark(tt(hot, ge[:, :, 0:TABLE], ge[:, :, 1:EDGES], ALU.subtract))
            o.done(nc.vector.tensor_reduce(slot, ge[:, :, 1:EDGES], AX.X, ALU.add))
            o.done(nc.vector.scalar_tensor_tensor(place, slot, -float(P), posk, ALU.mult, ALU.add))
            tt(place_hot, iota.unsqueeze(1).broadcast_to([P, 2 * NT, P]), place.unsqueeze(2).broadcast_to([P, 2 * NT, P]),
               ALU.is_equal).then_inc(tab_in, 1)
            v3 = values.rearrange("p (k c) n -> p k c n", k=2)
            tt(v3[:, :, :, 0:TABLE], hot.rearrange("p (k c) n -> p k c n", k=2),
               token.unsqueeze(1).unsqueeze(3).broadcast_to([P, 2, NT, TABLE]), ALU.mult).then_inc(tab_in, 1)
            tt(values[:, :, TABLE:], hot, wk.unsqueeze(2).broadcast_to([P, 2 * NT, TABLE]), ALU.mult).then_inc(tab_in, 1)
            o.done(ts(e_cmp.rearrange("p s e -> p (s e)")[:, 0:TABLE], edges[0:1, 0:TABLE], 1.0 / P, None, ALU.mult))
            o.done(nc.vector.tensor_copy(e_sum, e_cmp.rearrange("p s e -> p (s e)")[:, 0:TABLE]))
            o.done(tt(e_cmp, end_[0:1, :].unsqueeze(1).broadcast_to([1, TABLE, N_EXP]),
                      e_sum.unsqueeze(2).broadcast_to([1, TABLE, N_EXP]), ALU.is_le))
            o.done(nc.vector.tensor_reduce(e_sum, e_cmp, AX.X, ALU.add))
            o.mark(ts(M["slot_expert"], e_sum, float(N_EXP - 1), None, ALU.min))
            o.mark(nc.vector.tensor_copy(M["expert_end"], end_[0:1, :]))
            dve.wait_ge(tab_out, 1)
            o.mark(nc.vector.tensor_copy(M["tok_table"], ps[:, 6, 0:TABLE]))
            o.mark(nc.vector.tensor_copy(M["w_table"], ps[:, 6, TABLE:2 * TABLE]))


def experts(nc, N, M, A, C, out):
    sem = N.sem
    ps, ident, vecT = M["ps"], M["ident"], M["vecT"]
    w = M["big_w"]
    at = [0]

    def pair(n):
        at[0] += 2 * n
        return w[:, at[0] - 2 * n:at[0]].rearrange("p (b n) -> p b n", b=2)

    xg, xT_, y, hid, silu, hT_ = pair(D), pair(D), pair(D), pair(D_EXP), pair(D_EXP), pair(D_EXP)
    xT = xT_.rearrange("p b (k t) -> p b k t", k=KD)
    hT = hT_.rearrange("p b (f t) -> p b f t", f=D_EXP // P)
    ring_gu, ring_d = M["ring_gu"], M["ring_d"]
    NF = D_EXP // P

    s_rows = [sem("slot_rows0"), sem("slot_rows1")]
    s_y = [sem("slot_stored0"), sem("slot_stored1")]
    idx_ready, ready = sem("slot_index"), sem("experts_ready")
    gather_go = sem("gather_go")
    xt_full, xt_ready = sem("slot_xT_full"), sem("slot_xT_ready")
    gu_full, silu_ready, h_ready = sem("gate_up_full"), sem("silu_ready"), sem("hidden_ready")
    ht_full, ht_ready = sem("slot_hT_full"), sem("slot_hT_ready")
    y_full, y_ready = sem("slot_y_full"), sem("slot_y_ready")

    def over_slots(engine, step):
        for s in range(3):
            step(s, s % 2, s)
        with engine.Fori(0, (SLOTS - 5) // 2) as i:
            step(i * 2 + 3, 1, 3)
            step(i * 2 + 4, 0, 3)
        for s in range(SLOTS - 2, SLOTS):
            step(s, s % 2, s)

    with nc.Block() as block:
        @block.sync
        def _(sp):
            s_w = M["s_expert"]
            load_expert(sp, M, A, 2, 2)
            for e in range(2):
                sp.wait_ge(s_w[e], 48)
                sp.sem_inc(ready, 1)

            def next_expert(e, r, turn):
                end = sp.value_load(M["expert_end"][0:1, bass.ds(e - RING, 1)], min_val=0, max_val=SLOTS)
                sp.wait_ge(y_full, end)
                load_expert(sp, M, A, e, r)
                sp.wait_ge(s_w[(r + RING - 1) % RING], 48 * turn if r == 0 else 48 * (turn + 1))
                sp.sem_inc(ready, 1)

            with sp.Fori(0, 4) as i:
                for r in range(RING):
                    next_expert(i * RING + RING + r, r, i + 1)
            next_expert(N_EXP - 1, 0, 5)
            sp.wait_ge(s_w[0], 48 * 6)
            sp.sem_inc(ready, 1)

        @block.gpsimd
        def _(pool):
            def gather(s, b, first):
                if first >= 2:
                    pool.wait_ge(xt_full, (s - 1) * 2)
                nc.gpsimd.tensor_copy(M["tok_idx"][:, b:b + 1], M["tok_table"][:, bass.ds(s, 1)]).then_inc(idx_ready, 1)
                pool.wait_ge(idx_ready, s + 1)
                pool.sem_inc(gather_go, 1)
                nc.gpsimd.indirect_dma_start(xg[:, b, :], None, M["hn_dram"],
                                             bass.IndirectOffsetOnAxis(ap=M["tok_idx"][:, b:b + 1], axis=0))\
                    .then_inc(s_rows[b], 16)

            over_slots(pool, gather)

        @block.tensor
        def _(pe):
            def transposes(s, b, first):
                pe.wait_ge(s_rows[b], (s // 2 + 1) * 16 if isinstance(s, int) else (s + (2 - b)) * 8)
                if first >= 1:
                    pe.wait_ge(xt_ready, s * 2)
                for k in range(KD):
                    last = nc.tensor.transpose(ps[:, k // 4, (k % 4) * P:(k % 4 + 1) * P], xg[:, b, k * P:(k + 1) * P],
                                               ident[:, :])
                    if k % 4 == 3:
                        last.then_inc(xt_full, 1)

            def place_of(s):
                return pe.value_load(M["slot_expert"][0:1, bass.ds(s, 1)], min_val=0, max_val=N_EXP - 1)

            def gate_up(s, b, first):
                e = place_of(s)
                pe.wait_ge(ready, e + 1)
                pe.wait_ge(xt_ready, s * 2 + 2)
                if first >= 2:
                    pe.wait_ge(h_ready, s - 1)
                at = (e % RING) * GU_COLS
                for k in range(KD):
                    last = nc.tensor.matmul(ps[:, 2 + b, :], xT[:, b, k, :], ring_gu[:, bass.ds(at + k * 2 * D_EXP, BANK)],
                                            start=(k == 0), stop=(k == KD - 1))
                last.then_inc(gu_full, 1)

            def down(s, b, first):
                pe.wait_ge(h_ready, s + 1)
                if first >= 1:
                    pe.wait_ge(ht_ready, s)
                for f in range(NF):
                    last = nc.tensor.transpose(ps[:, 4, f * P:(f + 1) * P], hid[:, b, f * P:(f + 1) * P], ident[:, :])
                last.then_inc(ht_full, 1)
                e = place_of(s)
                pe.wait_ge(ht_ready, s + 1)
                if first >= 1:
                    pe.wait_ge(y_ready, s)
                at = (e % RING) * D_COLS
                for half in range(2):
                    for f in range(NF):
                        last = nc.tensor.matmul(ps[:, 5 + half, :], hT[:, b, f, :],
                                                ring_d[:, bass.ds(at + f * D + half * BANK, BANK)],
                                                start=(f == 0), stop=(f == NF - 1))
                last.then_inc(y_full, 1)

            transposes(0, 0, 0)

            def step(s, b, first):
                gate_up(s, b, first)
                if first >= 1:
                    down(s - 1, 1 - b, first - 1)
                if not isinstance(s, int) or s + 1 < SLOTS:
                    transposes(s + 1, 1 - b, first + 1)

            over_slots(pe, step)
            down(SLOTS - 1, (SLOTS - 1) % 2, SLOTS - 1)

        @block.scalar
        def _(act):
            nc.scalar.preload_act_table(ACT.Silu)

            def activate(s, b, first):
                act.wait_ge(gu_full, s + 1)
                if first >= 2:
                    act.wait_ge(h_ready, s - 1)
                nc.scalar.activation(silu[:, b, :], ps[:, 2 + b, 0:D_EXP], ACT.Silu).then_inc(silu_ready, 1)

            def put_out(s, b, first):
                act.wait_ge(y_full, s + 1)
                if first >= 2:
                    act.wait_ge(s_y[b], (s // 2) * 16 if isinstance(s, int) else (s - b) * 8)
                nc.scalar.activation(y[:, b, :], ps[:, 5:7, :].rearrange("p a n -> p (a n)"), ACT.Copy).then_inc(y_ready, 1)
                act.wait_ge(y_ready, s + 1)
                act.dma_start(M["y_dram"][bass.ds(s * P, P), :], y[:, b, :]).then_inc(s_y[b], 16)

            def step(s, b, first):
                activate(s, b, first)
                if first >= 1:
                    put_out(s - 1, 1 - b, first - 1)

            over_slots(act, step)
            put_out(SLOTS - 1, (SLOTS - 1) % 2, SLOTS - 1)
            act.wait_ge(s_y[0], 16 * ((SLOTS + 1) // 2))
            act.wait_ge(s_y[1], 16 * (SLOTS // 2))

        @block.vector
        def _(dve):
            def evacuate_x(s, b, first):
                if first >= 2:
                    dve.wait_ge(gu_full, s - 1)
                for j in range(2):
                    dve.wait_ge(xt_full, s * 2 + j + 1)
                    nc.vector.tensor_tensor(xT[:, b, 4 * j:4 * j + 4, :], ps[:, j, :].rearrange("p (k t) -> p k t", k=4),
                                            vecT[:, M["V_FFN"] + 4 * j:M["V_FFN"] + 4 * j + 4].unsqueeze(2)
                                            .broadcast_to([P, 4, P]), ALU.mult).then_inc(xt_ready, 1)

            def hidden(s, b, first):
                dve.wait_ge(silu_ready, s + 1)
                if first >= 2:
                    dve.wait_ge(ht_full, s - 1)
                nc.vector.scalar_tensor_tensor(hid[:, b, :], silu[:, b, :], M["w_table"][:, bass.ds(s, 1)],
                                               ps[:, 2 + b, D_EXP:2 * D_EXP], ALU.mult, ALU.mult).then_inc(h_ready, 1)

            def evacuate_h(s, b, first):
                dve.wait_ge(ht_full, s + 1)
                if first >= 2:
                    dve.wait_ge(y_full, s - 1)
                nc.vector.tensor_copy(hT_[:, b, :], ps[:, 4, 0:D_EXP]).then_inc(ht_ready, 1)

            evacuate_x(0, 0, 0)

            def step(s, b, first):
                if first >= 1:
                    evacuate_h(s - 1, 1 - b, first - 1)
                hidden_first = isinstance(s, int) and s + 1 >= SLOTS
                if not hidden_first:
                    evacuate_x(s + 1, 1 - b, first + 1)
                hidden(s, b, first)

            over_slots(dve, step)
            evacuate_h(SLOTS - 1, (SLOTS - 1) % 2, SLOTS - 1)


def combine(nc, N, M, A, C, out):
    sem = N.sem
    s_in = [sem(f"pair_rows{i}") for i in range(4)]
    done, s_out = sem("tile_summed"), sem("out_stored")
    ord_dve = sem("vector_order6")
    h = M["conv"][:, :, 0:D]

    def rows(c, k):
        i = 2 * c + k
        return M["ring_gu"][:, i * D:(i + 1) * D] if i < 12 else M["big_w"][:, (i - 12) * D:(i - 11) * D]

    with nc.Block() as block:
        @block.gpsimd
        def _(pool):
            for c in range(NT):
                if c >= 4:
                    pool.wait_ge(s_in[c % 4], 32)
                for k in range(2):
                    pool.indirect_dma_start(rows(c, k), None, M["y_dram"],
                                            bass.IndirectOffsetOnAxis(ap=M["slot_pos"][:, k * NT + c:k * NT + c + 1], axis=0))\
                        .then_inc(s_in[c % 4], 16)

        @block.vector
        def _(dve):
            o = Order(dve, ord_dve)
            for c in range(NT):
                dve.wait_ge(s_in[c % 4], 32 * (c // 4 + 1))
                o.done(nc.vector.tensor_tensor(h[:, c, :], h[:, c, :], rows(c, 0), ALU.add))
                nc.vector.tensor_tensor(h[:, c, :], h[:, c, :], rows(c, 1), ALU.add).then_inc(done, 1)

        @block.sync
        def _(sp):
            for c in range(NT):
                sp.wait_ge(done, c + 1)
                sp.dma_start(out[0, c * P:(c + 1) * P, :], h[:, c, :]).then_inc(s_out, 16)
            sp.wait_ge(s_out, 16 * NT)


def kernel(**inputs):
    import numpy as np
    import concourse.bacc as bacc
    from concourse.bass_utils import run_bass_kernel_spmd

    nc = bacc.Bacc("TRN2", target_bir_lowering=False, num_devices=1)
    arrays, A, C = {}, {}, {}
    for name, a in inputs.items():
        a = np.ascontiguousarray(a)
        arrays[f"in_{name}"] = a
        A[name] = nc.dram_tensor(f"in_{name}", a.shape, mybir.dt.from_np(a.dtype), kind="ExternalInput").ap()
    for name, a in shape_constants().items():
        a = np.ascontiguousarray(a)
        arrays[f"const_{name}"] = a
        C[name] = nc.dram_tensor(f"const_{name}", a.shape, mybir.dt.from_np(a.dtype), kind="ExternalInput").ap()
    out = nc.dram_tensor("out", (1, S, D), F32, kind="ExternalOutput").ap()
    build(nc, A, C, out)
    return run_bass_kernel_spmd(nc, [arrays], core_ids=[0]).results[0]["out"]
```

```python
from contextlib import ExitStack

import concourse.bass as bass
from concourse import mybir

F32 = mybir.dt.float32
BF16 = mybir.dt.bfloat16
I32 = mybir.dt.int32
ACT = mybir.ActivationFunctionType
ALU = mybir.AluOpType
AX = mybir.AxisListType

P = 128
D = 1024
S = 1024
NT = S // P
KD = D // P
HD = 64
NH = 8
NG = 2
GQ = NH // NG
BANK = 512
N_CMP = 63
N_BLK = 16
L_CMP = 32
CSTR = 16
TOP_N = 8
D_SSM = 512
D_CONV = 1024
N_STATE = 128
SH = 8
EPS = 1e-6
NEG = -1.0e30
KR = 64 + 2 * N_BLK + GQ + 1
ROW_SEL, ROW_ALIBI, ROW_MAX, ROW_SLOPE = 64, 80, 96, 100
N_EXP = 16
D_EXP = 256
PAIRS = 2 * S
SLOTS = PAIRS // P + N_EXP - 1
SLOTS_HEAD = 3
SLOTS_SURE = PAIRS // P + 1
LOOP_PAIRS = (SLOTS - SLOTS_HEAD) // 2
NGATE = 24
TABLE = 32
EDGES = TABLE + 1
RING = 3
GU_COLS, D_COLS = KD * 2 * D_EXP, (D_EXP // P) * D

COL_Q = 0
COL_KV = 512
COL_GATE = COL_KV + 6 * 128
COL_Z = COL_GATE + NGATE
COL_X = COL_Z + D_SSM
COL_DT = COL_X + D_CONV
D_IN = COL_DT + SH
KVB = 256 + NGATE + SH


def shape_constants():
    import numpy as np

    t = np.arange(S)
    loc = np.arange(P)
    slopes = np.exp2(-8.0 * (np.arange(NH) + 1) / NH).astype(np.float32)
    c = {}
    c["ident"] = np.eye(P, dtype=np.float32)
    def key_rows(pos, live):
        hot = (pos[None] // HD == np.arange(N_BLK)[:, None]).astype(np.float32)
        sel = hot * live
        return np.concatenate([sel, hot, np.ones((GQ, len(pos))), (pos % HD)[None]]).astype(np.float32)
    c["key_rows_sel"] = key_rows(t, 1.0)
    c["key_rows_win"] = key_rows(t, 0.0)
    c["key_rows_cmp"] = key_rows(np.arange(N_CMP) * CSTR + L_CMP - 1, 0.0)
    q = np.zeros((NT, N_BLK, NH, P), np.float32)
    for n in range(NT):
        d = (n * P + loc)[None, :] - HD * np.arange(N_BLK)[:, None]
        q[n] = -slopes[None, :, None] * d[:, None, :]
    c["alibi_rows"] = q
    c["slope_row"] = np.repeat(slopes, P)[None].astype(np.float32)
    c["head_delta"] = np.repeat(np.eye(GQ, dtype=np.float32), P, axis=1)
    m = np.zeros((4, P, P), np.float32)
    m[0] = np.where(loc[None, :] > loc[:, None], NEG, 0)
    m[1] = m[0].T
    m[2] = np.where(loc[None, :] <= loc[:, None], NEG, 0)
    m[3] = m[2].T
    c["masks"] = m.transpose(1, 0, 2).copy()
    end = np.arange(N_CMP) * CSTR + L_CMP - 1
    mc = np.where(end[None, :] > t[:, None], NEG, 0).astype(np.float32).reshape(NT, P, N_CMP)
    c["mask_cmp"] = mc.transpose(1, 0, 2).copy()
    c["mask_cmpT"] = mc.transpose(2, 0, 1).copy()
    s0 = np.arange(N_BLK) * HD
    st = np.arange(N_CMP) * CSTR
    ov = np.clip(np.minimum(st[:, None] + L_CMP, s0[None] + HD) - np.maximum(st[:, None], s0[None]), 0, None)
    c["v_cmp_tail"] = np.concatenate([np.ones((N_CMP, 1)), ov / L_CMP], axis=1).astype(np.float32)
    j = np.arange(N_BLK)[None, :]
    cur = (t // HD)[:, None]
    forced = (j == 0) | (j == cur) | (j == cur - 1)
    valid = j <= cur
    rows = np.stack([valid & ~forced, np.where(forced, 1.0e4, np.where(valid, 0.0, -1.0))]).astype(np.float32)
    c["score_rows"] = rows.reshape(2, NT, P, N_BLK).transpose(2, 0, 1, 3).copy()
    i = np.arange(N_BLK)
    c["before"] = (i[None, :] < i[:, None]).astype(np.float32).reshape(-1)
    c["tri"] = np.triu(np.ones((P, P), np.float32))
    c["tri_strict"] = np.triu(np.ones((P, P), np.float32), 1)
    c["iota"] = np.tile(np.arange(P, dtype=np.float32), (P, 1))
    c["token"] = (np.arange(NT)[None, :] * P + loc[:, None]).astype(np.float32)
    c["slot_edges"] = np.tile(np.arange(EDGES, dtype=np.float32) * P, (P, 1))
    return c


class Names:

    def __init__(self, nc, stack):
        self.nc, self.stack = nc, stack

    def sb(self, name, shape, dt=F32):
        return self.stack.enter_context(self.nc.sbuf_tensor(name, shape, dt))

    def ps(self, name, shape, dt=F32):
        return self.stack.enter_context(self.nc.psum_tensor(name, shape, dt))

    def sem(self, name):
        return self.stack.enter_context(self.nc.semaphore(name))


class Order:

    def __init__(self, engine, sem):
        self.engine, self.sem, self.n = engine, sem, 0

    def mark(self, ins):
        self.n += 1
        ins.then_inc(self.sem, 1)

    def wait(self):
        self.engine.wait_ge(self.sem, self.n)

    def done(self, ins):
        self.mark(ins)
        self.wait()


def build(nc, A, C, out, last="combine"):
    stack = ExitStack()
    with stack:
        N = Names(nc, stack)
        M = {}
        setup_memory(nc, N, M, A, C)
        stages = [("project", project), ("attend", attend), ("ssd", ssd), ("merge", merge),
                  ("experts", experts), ("combine", combine)]
        for name, stage in stages:
            stage(nc, N, M, A, C, out)
            if name == last:
                break


def setup_memory(nc, N, M, A, C):
    sb = N.sb
    M["ident"] = sb("ident", [P, P])
    M["identb"] = sb("identb", [P, P], BF16)
    M["masksb"] = sb("masksb", [P, 4, P], BF16)
    M["vec_rows"] = sb("vec_rows", [64, P])
    M["vecT"] = sb("vecT", [P, 64])
    M["qk_rows"] = sb("qk_rows", [4, HD])
    M["qkT"] = sb("qkT", [HD, 4])
    M["small"] = sb("small", [P, 512])
    M["eps"] = sb("eps", [P, 1])
    M["head_rows"] = sb("head_rows", [P, 3, SH])
    M["tri"] = sb("tri", [P, P])
    M["gate_dt"] = sb("gate_dt", [P, NT, 32])
    M["big_u"] = sb("big_u", [P, KD * S])
    M["big_w"] = sb("big_w", [P, 2 * KD * BANK])
    M["conv"] = sb("conv", [P, NT, S + 3])
    ring = sb("ring_gate_up", [P, 3 * 4096])
    M["ring_gu"] = ring
    M["z"] = ring[:, 0:4096].rearrange("p (c n) -> p c n", c=NT)
    M["kvcT"] = ring[:, 4096:8192].rearrange("p (j n) -> p j n", j=4)
    M["qn"] = ring[:, 8192:12288].rearrange("p (c n) -> p c n", c=NT)
    M["o_att"] = sb("o_att", [P, NT, 512])
    ring = sb("ring_down", [P, 2 * NG * S + 2 * NT * NG * (HD + 1)])
    M["ring_d"] = ring
    M["k_sel"] = ring[:, 0:2048].rearrange("p (g n) -> p g n", g=NG)
    M["k_win"] = ring[:, 2048:4096].rearrange("p (g n) -> p g n", g=NG)
    M["v_sel"] = ring[:, 4096:5136].rearrange("p (c g n) -> p c g n", c=NT, g=NG)
    M["v_win"] = ring[:, 5136:6176].rearrange("p (c g n) -> p c g n", c=NT, g=NG)
    M["misc"] = sb("misc", [P, 3 * 1024])
    M["ps"] = N.ps("ps", [P, 8, BANK])
    M["s_w_out"] = N.sem("w_out_loaded")
    M["zeros"] = sb("zeros", [P, 256])
    M["s_zero_slots"] = N.sem("empty_slots_zeroed")
    M["dt_steps"] = N.sem("dt_steps")
    M["idx_ready"] = N.sem("slot_index")
    M["s_rows"] = [N.sem("slot_rows0"), N.sem("slot_rows1")]
    M["w_out_scaled"] = N.sem("w_out_scaled")
    M["y_stored"] = N.sem("y_stored")
    M["s_expert"] = [N.sem(f"expert_loaded{r}") for r in range(RING)]
    M["hn_dram"] = nc.dram_tensor("hn_dram", (S, D), F32, kind="Internal").ap()
    M["y_dram"] = nc.dram_tensor("y_dram", (SLOTS * P, D), F32, kind="Internal").ap()
    plan = M["misc"][:, 2048:3072]
    M["tok_table"] = plan[:, 0:TABLE].bitcast(I32)
    M["w_table"] = plan[:, 32:64]
    M["slot_pos"] = plan[:, 64:80].bitcast(I32)
    M["expert_end"] = plan[0:1, 112:128].bitcast(I32)
    M["tok_idx"] = plan[:, 128:130].bitcast(I32)
    M["slot_places"] = plan[0:1, 132:132 + 4 * TABLE].bitcast(I32).rearrange("p (s n) -> p s n", n=4)
    M["last_slot"] = plan[0:1, 260:261].bitcast(I32)
    M["Q"] = M["misc"][:, :].rearrange("p (r g n) -> p r g n", r=3, g=NG)
    M["s_alibi"] = [N.sem("alibi_loaded0"), N.sem("alibi_loaded1")]
    w = M["big_w"]
    at = [0]

    def part(name, n, dt=F32, p=P):
        cols = n if dt == F32 else (n + 1) // 2
        view = w[0:p, at[0]:at[0] + cols]
        at[0] += cols
        M[name] = view if dt == F32 else view.bitcast(dt)

    part("k_cmp", NG * 64)
    part("v_cmp", NG * 82)
    part("score_rows", 2 * NT * N_BLK)
    part("before", N_BLK * N_BLK)
    part("sg", NT * NGATE)
    part("mask_cmp", NT * 64, BF16)
    part("mask_cmpT", NT * P, BF16)
    part("hid", 2 * NG * 64)
    part("peT", 32)
    part("cmp_w2", 2 * HD)
    part("pe_rows", P)
    part("pe_bias", 2)
    part("head_delta", GQ * P)
    part("o_tmp", GQ * HD)
    part("sel_tmp", 896)
    part("sel01", N_BLK, BF16)
    part("att_small", 64)
    assert at[0] <= KD * BANK
    stage = M["o_att"][:, :, :].rearrange("p c n -> p (c n)")
    M["cmp_w1"] = stage[:, 0:2048].rearrange("p (v l e) -> p v l e", v=2, l=16)
    M["stage_masks"] = stage[:, 2048:2560]
    M["stage_cmp"] = stage[:, 2560:2560 + NT * N_CMP]
    M["stage_cmpT"] = stage[0:N_CMP, 3072:4096]
    M["V_ATT"], M["V_CONVW"], M["V_CONVB"], M["V_AON"] = 0, 8, 40, 48


def small_part(M, i):
    return M["small"][:, 64 * i:64 * i + 64]


def load_alibi(sp, M, C, u):
    c, g = u // NG, u % NG
    for br in range(3):
        sp.dma_start(M["Q"][ROW_ALIBI:ROW_MAX, br, g, :],
                     C["alibi_rows"][c, :, g * GQ:(g + 1) * GQ, :].rearrange("j h q -> j (h q)")).then_inc(M["s_alibi"][g], 16)


def project(nc, N, M, A, C, out):
    sem = N.sem
    x_in = M["misc"][:, 0:2048].rearrange("p (b n) -> p b n", b=2)
    xn1 = M["misc"][:, 2048:3072]
    uT = M["big_u"][:, :].rearrange("p (k t) -> p k t", k=KD)
    wbuf = M["big_w"][:, :].rearrange("p (b k n) -> p b k n", b=2, k=KD)
    conv, z, qn = M["conv"], M["z"], M["qn"]
    square = conv[:, 6, 3:3 + BANK]
    junk = conv[:, 7, 3:3 + D]
    kc_nat = M["o_att"]
    ks_nat = conv[:, 5, 3:3 + 256]
    acc = M["misc"][:, 0:2048].rearrange("p (b n) -> p b n", b=2)
    small = M["small"]
    ss_x, rs_x = small[:, 0:8], small[:, 8:16]
    ss_q, rs_q = small[:, 16:80], small[:, 80:144]
    ss_k, rs_k = small[:, 144:176], small[:, 176:208]
    ps, ident, vecT, qkT = M["ps"], M["ident"], M["vecT"], M["qkT"]

    s_const, s_rows = sem("const_loaded"), sem("rows_loaded")
    s_x = [sem("x_loaded0"), sem("x_loaded1")]
    s_w = [sem("w_loaded0"), sem("w_loaded1")]
    s_krows = sem("key_rows_loaded")
    x_stat = sem("x_rstd_ready")
    xn_ready = sem("xn_ready")
    t_full = sem("transposes_full")
    t_free = sem("transposes_evacuated")
    m_full = sem("product_full")
    q_ready = sem("q_normed")
    m_free_act = sem("product_copied")
    vec_full, vec_done = sem("vectors_transposed"), sem("vectors_copied")
    sq_ready, ss_ready, rs_ready = sem("squares_ready"), sem("square_sums_ready"), sem("rstd_ready")
    kn_ready = sem("k_normed")
    conv_out, conv_silu = sem("conv_sum_ready"), sem("conv_silu_done")
    ord_act, ord_dve = sem("scalar_order1"), sem("vector_order1")
    pads = sem("pads_set")
    q_zeroed, s_slopes = sem("query_rows_zeroed"), sem("slopes_loaded")
    s_cmp, s_stage, s_small = sem("cmp_w1_loaded"), sem("masks_loaded"), sem("small_loaded")
    c_full, c_read, c_hid = sem("compress_full"), sem("compress_read"), sem("compress_hidden_ready")
    c_sq, c_ss, c_rs, c_kn = sem("cmp_squares"), sem("cmp_sums"), sem("cmp_rstd"), sem("cmp_k_normed")
    kvcT = M["kvcT"]
    hid = M["hid"][0:HD, :].rearrange("p (v g n) -> p v g n", v=2, g=NG)
    w2 = M["cmp_w2"][0:HD, :].rearrange("p (v e) -> p v e", v=2)
    k_nat = M["sel_tmp"][0:N_CMP, 0:P].rearrange("p (g d) -> p g d", g=NG)
    k_sq = M["sel_tmp"][0:N_CMP, P:2 * P]
    ss_c, rs_c = small[0:N_CMP, 208:210], small[0:N_CMP, 210:212]
    w_in = A["w_in"][0].rearrange("(k p) n -> p k n", p=P)
    NCH = 6
    Q_, KVA, KVB, X0, X1, Z_ = range(NCH)
    T_X = 2 * NT

    with nc.Block() as block:
        @block.sync
        def _(sp):
            def load_x(c):
                if c >= 2:
                    sp.wait_ge(xn_ready, c - 1)
                sp.dma_start(x_in[:, c % 2, :], A["x"][0, c * P:(c + 1) * P, :]).then_inc(s_x[c % 2], 16)

            def load_w(n):
                b = n % 2
                if n >= 2:
                    sp.wait_ge(m_full, NT * (n - 1))
                if n == KVB:
                    sp.dma_start(wbuf[:, b, :, 0:280],
                                 w_in[:, :, COL_KV + 512:COL_Z]).then_inc(s_w[b], 16)
                    sp.dma_start(wbuf[:, b, :, 280:288], w_in[:, :, COL_DT:D_IN]).then_inc(s_w[b], 16)
                    return
                col = {Q_: COL_Q, KVA: COL_KV, X0: COL_X, X1: COL_X + BANK, Z_: COL_Z}[n]
                for h in range(2):
                    sp.dma_start(wbuf[:, b, 4 * h:4 * h + 4, :],
                                 w_in[:, 4 * h:4 * h + 4, col:col + BANK]).then_inc(s_w[b], 16)

            load_x(0)
            sp.dma_start(ident[:, :], C["ident"]).then_inc(s_const, 16)
            r = M["vec_rows"]
            sp.dma_start(r[0:8, :], A["attn_norm_w"].rearrange("a (m p) -> (a m) p", p=P)).then_inc(s_rows, 16)
            sp.dma_start(r[8:40, :], A["conv_w"][0].rearrange("i (m p) -> (i m) p", p=P)).then_inc(s_rows, 16)
            sp.dma_start(r[40:48, :], A["conv_b"].rearrange("a (m p) -> (a m) p", p=P)).then_inc(s_rows, 16)
            sp.dma_start(r[48:52, :], A["attn_out_norm_w"].rearrange("a (m p) -> (a m) p", p=P)).then_inc(s_rows, 16)
            sp.dma_start(r[52:56, :], A["ssm_norm_w"].rearrange("a (m p) -> (a m) p", p=P)).then_inc(s_rows, 16)
            sp.dma_start(r[56:64, :], A["ffn_norm_w"].rearrange("a (m p) -> (a m) p", p=P)).then_inc(s_rows, 16)
            sp.dma_start(M["qk_rows"][0:1, :], A["q_norm_w"]).then_inc(s_rows, 16)
            sp.dma_start(M["qk_rows"][1:4, :], A["k_norm_w"][0]).then_inc(s_rows, 16)
            load_x(1)
            load_w(Q_)
            load_w(KVA)
            for c in range(2, NT):
                load_x(c)
            for i, name in enumerate(("dt_bias", "A_log", "D_skip")):
                sp.dma_start(M["head_rows"][:, i, :], A[name][0].partition_broadcast(P)).then_inc(s_krows, 16)
            sp.dma_start(M["tri"][:, :], C["tri"]).then_inc(s_krows, 16)
            for g in range(NG):
                sp.dma_start(M["k_sel"][64:KR, g, :], C["key_rows_sel"]).then_inc(s_krows, 16)
                sp.dma_start(M["k_win"][64:KR, g, :], C["key_rows_win"]).then_inc(s_krows, 16)
            load_w(KVB)
            load_w(X0)
            sp.wait_ge(t_free, T_X + 2 * NT)
            for v in range(2):
                sp.dma_start(M["cmp_w1"][:, v], A["cmp_w1"][0, v].rearrange("(l p) e -> p l e", p=P)).then_inc(s_cmp, 16)
            sp.dma_start(M["stage_masks"], C["masks"].rearrange("p a b -> p (a b)")).then_inc(s_stage, 16)
            sp.dma_start(M["stage_cmp"], C["mask_cmp"].rearrange("p a b -> p (a b)")).then_inc(s_stage, 16)
            sp.dma_start(M["stage_cmpT"], C["mask_cmpT"].rearrange("p a b -> p (a b)")).then_inc(s_stage, 16)
            sp.dma_start(M["kvcT"][64:P, :, 0:S - 1], M["kvcT"][0:HD, :, 1:S]).then_inc(s_cmp, 16)
            load_w(X1)
            load_w(Z_)
            sp.wait_ge(m_full, NT * Z_)
            sp.dma_start(M["cmp_w2"][0:HD, :].rearrange("p (v e) -> p v e", v=2),
                         A["cmp_w2"][0].rearrange("v d e -> d v e")).then_inc(s_small, 16)
            sp.dma_start(M["pe_rows"][0:32, :], A["cmp_pe"][0].rearrange("v (l i) d -> (v l) (i d)", i=2)).then_inc(s_small, 16)
            vc = M["v_cmp"].rearrange("p (g n) -> p g n", g=NG)
            for g in range(NG):
                sp.dma_start(M["k_cmp"].rearrange("p (g n) -> p g n", g=NG)[64:KR, g, 0:N_CMP],
                             C["key_rows_cmp"]).then_inc(s_small, 16)
                sp.dma_start(vc[0:N_CMP, g, HD:HD + 17], C["v_cmp_tail"]).then_inc(s_small, 16)
            sp.dma_start(M["score_rows"], C["score_rows"].rearrange("p a b c -> p (a b c)")).then_inc(s_small, 16)
            sp.dma_start(M["before"], C["before"].partition_broadcast(P)).then_inc(s_small, 16)
            sp.dma_start(M["head_delta"][0:GQ, :], C["head_delta"]).then_inc(s_small, 16)
            sp.wait_ge(q_zeroed, 1)
            for g in range(NG):
                for br in range(3):
                    sp.dma_start(M["Q"][ROW_SLOPE:ROW_SLOPE + 1, br, g, :],
                                 C["slope_row"][:, g * BANK:(g + 1) * BANK]).then_inc(s_slopes, 16)
                load_alibi(sp, M, C, g)
            sp.wait_ge(s_slopes, 96)
            sp.wait_ge(s_krows, 128)
            sp.wait_ge(s_stage, 48)
            sp.wait_ge(s_small, 9 * 16)

        @block.tensor
        def _(pe):
            state = {"t": 0, "m": 0}

            def t_bank(n_ops):
                t = state["t"]
                if t >= 4:
                    pe.wait_ge(t_free, t - 3)
                state["t"] += 1
                return t % 4

            def m_bank():
                m = state["m"]
                if m >= 4 + 3 * NT:
                    pe.wait_ge(m_free_act, m - 3 - 3 * NT)
                elif m >= 4 + NT:
                    pe.wait_ge(kn_ready, m - 3 - NT)
                elif m >= 4:
                    pe.wait_ge(q_ready, m - 3)
                state["m"] += 1
                return 4 + m % 4

            def transpose_x(c):
                pe.wait_ge(xn_ready, c + 1)
                for j in range(2):
                    b = t_bank(4)
                    for i in range(4):
                        k = 4 * j + i
                        last = nc.tensor.transpose(ps[:, b, i * P:(i + 1) * P], xn1[:, k * P:(k + 1) * P], ident[:, :])
                    last.then_inc(t_full, 1)

            def chunk_loaded(n):
                pe.wait_ge(s_w[n % 2], 32 * (n // 2 + 1))

            def product_natural(n, c, width):
                b = m_bank()
                for k in range(KD):
                    last = nc.tensor.matmul(ps[:, b, 0:width], uT[:, k, c * P:(c + 1) * P], wbuf[:, n % 2, k, 0:width],
                                            start=(k == 0), stop=(k == KD - 1))
                last.then_inc(m_full, 1)
                return last

            def product_channels(n, m, half):
                b = m_bank()
                for k in range(KD):
                    last = nc.tensor.matmul(ps[:, b, :], wbuf[:, n % 2, k, m * P:(m + 1) * P],
                                            uT[:, k, half * BANK:(half + 1) * BANK], start=(k == 0), stop=(k == KD - 1))
                last.then_inc(m_full, 1)

            pe.wait_ge(s_const, 16)
            pe.wait_ge(s_rows, 8 * 16)
            nc.tensor.transpose(ps[:, 4, 0:64], M["vec_rows"][:, :], ident[0:64, 0:64])
            nc.tensor.transpose(ps[0:HD, 4, 64:68], M["qk_rows"][:, :], ident[0:4, 0:4]).then_inc(vec_full, 1)
            transpose_x(0)
            pe.wait_ge(vec_done, 1)
            chunk_loaded(Q_)
            for c in range(NT):
                if c + 1 < NT:
                    transpose_x(c + 1)
                pe.wait_ge(t_free, 2 * (c + 1))
                product_natural(Q_, c, BANK)
            def transpose_kv(i):
                c = i % NT
                pe.wait_ge(kn_ready, i + 1)
                if i < NT:
                    b = t_bank(4)
                    for j in range(4):
                        last = nc.tensor.transpose(ps[0:HD, b, j * P:(j + 1) * P],
                                                   kc_nat[:, i, j * HD:(j + 1) * HD], ident[:, :])
                    last.then_inc(t_full, 1)
                b = t_bank(2)
                for g in range(NG):
                    last = nc.tensor.transpose(ps[0:HD, b, g * P:(g + 1) * P],
                                               ks_nat[:, (i % 2) * P + g * HD:(i % 2) * P + (g + 1) * HD], ident[:, :])
                last.then_inc(t_full, 1)

            for i in range(2 * NT):
                n = KVA if i < NT else KVB
                if i % NT == 0:
                    chunk_loaded(n)
                product_natural(n, i % NT, BANK if n == KVA else 288)
                if i >= 1:
                    transpose_kv(i - 1)
            for n in (X0, X1):
                chunk_loaded(n)
                for m in range(4):
                    for half in range(2):
                        product_channels(n, m, half)
                        if n == X0 and m == 0 and half == 0:
                            transpose_kv(2 * NT - 1)
            chunk_loaded(Z_)
            for c in range(NT):
                product_natural(Z_, c, BANK)
                if c == 0:
                    pe.wait_ge(t_free, T_X + 3 * NT)
                    pe.wait_ge(s_small, 9 * 16)
                    nc.tensor.transpose(ps[:, 0, 0:32], M["pe_rows"][0:32, :], ident[0:32, 0:32]).then_inc(c_full, 1)
                if c == 1:
                    pe.wait_ge(s_cmp, 48)
                    pe.wait_ge(c_read, 1)
                    for v in range(2):
                        for l in range(16):
                            nc.tensor.matmul(ps[0:HD, 1, v * P:v * P + NG * N_CMP].rearrange("e (g n) -> e g n", g=NG),
                                             M["cmp_w1"][:, v, l, :],
                                             kvcT[:, 2 * v:2 * v + 2, 2 * l:2 * l + CSTR * (N_CMP - 1) + 1:CSTR],
                                             start=(l == 0), stop=(l == 15))
                    for v in range(2):
                        for l in range(16):
                            last = nc.tensor.matmul(ps[0:HD, 2, v:v + 1], M["cmp_w1"][:, v, l, :],
                                                    M["peT"][:, v * 16 + l:v * 16 + l + 1], start=(l == 0), stop=(l == 15))
                    last.then_inc(c_full, 1)
                if c == 3:
                    pe.wait_ge(c_hid, 2)
                    for v in range(2):
                        for g in range(NG):
                            last = nc.tensor.matmul(ps[0:N_CMP, 0, (2 * v + g) * HD:(2 * v + g + 1) * HD],
                                                    hid[:, v, g, 0:N_CMP], w2[:, v, :], start=True, stop=True)
                    last.then_inc(c_full, 1)
                if c == 5:
                    pe.wait_ge(c_kn, 1)
                    for g in range(NG):
                        last = nc.tensor.transpose(ps[0:HD, 1, g * 64:g * 64 + N_CMP], k_nat[:, g, :],
                                                   ident[0:N_CMP, 0:N_CMP])
                    last.then_inc(c_full, 1)

        @block.scalar
        def _(act):
            o = Order(act, ord_act)
            nc.scalar.preload_act_table_set("natural_log_exp_and_others")

            def rstd(ss, rs, n):
                o.done(nc.scalar.activation(rs, ss, ACT.Ln, scale=1.0 / n, bias=M["eps"][:, 0:1]))
                return nc.scalar.activation(rs, rs, ACT.Exp, scale=-0.5)

            def x_stats(c):
                act.wait_ge(s_x[c % 2], 16 * (c // 2 + 1))
                o.done(nc.scalar.activation(junk, x_in[:, c % 2, :], ACT.Square, accum_out=ss_x[:, c:c + 1]))
                rstd(ss_x[:, c:c + 1], rs_x[:, c:c + 1], D).then_inc(x_stat, 1)

            def q_stats(c):
                act.wait_ge(m_full, c + 1)
                nc.scalar.activation(square, ps[:, 4 + c % 4, :], ACT.Square).then_inc(sq_ready, 1)
                act.wait_ge(ss_ready, c + 1)
                rstd(ss_q[:, 8 * c:8 * c + 8], rs_q[:, 8 * c:8 * c + 8], HD).then_inc(rs_ready, 1)

            def kv_part(i):
                c, b = i % NT, 4 + i % 4
                act.wait_ge(m_full, NT + i + 1)
                if i < NT:
                    nc.scalar.activation(square[:, 0:P], ps[:, b, 256:384], ACT.Square).then_inc(sq_ready, 1)
                    o.mark(nc.scalar.activation(kc_nat[:, c, 0:256], ps[:, b, 0:256], ACT.Copy))
                    o.mark(nc.scalar.activation(M["v_sel"][:, c, :, 0:HD],
                                                ps[:, b, 384:512].rearrange("p (g d) -> p g d", g=NG), ACT.Copy))
                else:
                    nc.scalar.activation(square[:, 0:P], ps[:, b, 0:P], ACT.Square).then_inc(sq_ready, 1)
                    o.mark(nc.scalar.activation(M["v_win"][:, c, :, 0:HD],
                                                ps[:, b, P:2 * P].rearrange("p (g d) -> p g d", g=NG), ACT.Copy))
                    o.mark(nc.scalar.activation(M["gate_dt"][:, c, :], ps[:, b, 256:288], ACT.Copy))
                act.wait_ge(ss_ready, NT + i + 1)
                rstd(ss_k[:, 2 * i:2 * i + 2], rs_k[:, 2 * i:2 * i + 2], HD).then_inc(rs_ready, 1)

            act.wait_ge(pads, 1)
            x_stats(0)
            x_stats(1)
            for c in range(NT):
                if c + 2 < NT:
                    x_stats(c + 2)
                q_stats(c)
            for i in range(2 * NT):
                kv_part(i)
            nc.scalar.preload_act_table(ACT.Silu)

            def silu(m):
                act.wait_ge(conv_out, m + 1)
                nc.scalar.activation(conv[:, m, 3:3 + S], acc[:, m % 2, :], ACT.Silu).then_inc(conv_silu, 1)

            for m in range(KD):
                for half in range(2):
                    j = 2 * m + half
                    act.wait_ge(m_full, 3 * NT + j + 1)
                    if j == 0:
                        act.wait_ge(kn_ready, 2 * NT)
                    if m == 5 and half == 0:
                        act.wait_ge(t_free, T_X + 2 * NT + NT)
                    a = nc.scalar.activation(conv[:, m, 3 + half * BANK:3 + (half + 1) * BANK], ps[:, 4 + j % 4, :],
                                             ACT.Copy)
                    a.then_inc(m_free_act, 1)
                if m >= 1:
                    silu(m - 1)
            silu(KD - 1)
            for c in range(NT):
                act.wait_ge(m_full, 5 * NT + c + 1)
                nc.scalar.activation(z[:, c, :], ps[:, 4 + c % 4, :], ACT.Silu).then_inc(m_free_act, 1)
                if c == 1:
                    act.wait_ge(c_read, 2)
                    for v in range(2):
                        nc.scalar.activation(hid[:, v, :, 0:N_CMP],
                                             ps[0:HD, 1, v * P:v * P + NG * N_CMP].rearrange("e (g n) -> e g n", g=NG),
                                             ACT.Silu, bias=M["pe_bias"][0:HD, v:v + 1]).then_inc(c_hid, 1)
                if c == 3:
                    act.wait_ge(c_read, 3)
                    nc.scalar.activation(k_sq, ps[0:N_CMP, 0, 0:P], ACT.Square).then_inc(c_sq, 1)
                    act.wait_ge(c_ss, 1)
                    o.done(nc.scalar.activation(rs_c, ss_c, ACT.Ln, scale=1.0 / HD, bias=M["eps"][0:N_CMP, 0:1]))
                    nc.scalar.activation(rs_c, rs_c, ACT.Exp, scale=-0.5).then_inc(c_rs, 1)

        @block.gpsimd
        def _(pool):
            nc.gpsimd.memset(M["eps"][:, :], EPS).then_inc(pads, 1)
            nc.gpsimd.memset(conv[:, :, 0:3], 0.0).then_inc(pads, 1)
            nc.gpsimd.memset(M["v_sel"][:, :, :, HD:HD + 1], 1.0).then_inc(pads, 1)
            nc.gpsimd.memset(M["v_win"][:, :, :, HD:HD + 1], 1.0).then_inc(pads, 1)
            pool.wait_ge(conv_silu, KD)
            nc.gpsimd.memset(M["misc"][64:P, :], 0.0).then_inc(q_zeroed, 1)

        @block.vector
        def _(dve):
            o = Order(dve, ord_dve)
            V_ATT, V_CONVW, V_CONVB = M["V_ATT"], M["V_CONVW"], M["V_CONVB"]
            state = {"t": 0}

            def normalise_x(c):
                dve.wait_ge(x_stat, c + 1)
                if c >= 1:
                    dve.wait_ge(t_full, 2 * c)
                nc.vector.tensor_scalar(xn1, x_in[:, c % 2, :], rs_x[:, c:c + 1], None, ALU.mult).then_inc(xn_ready, 1)

            def next_t():
                state["t"] += 1
                dve.wait_ge(t_full, state["t"])
                return (state["t"] - 1) % 4

            def evacuate_u(c):
                for j in range(2):
                    b = next_t()
                    nc.vector.tensor_tensor(uT[:, 4 * j:4 * j + 4, c * P:(c + 1) * P],
                                            ps[:, b, :].rearrange("p (k t) -> p k t", k=4),
                                            vecT[:, V_ATT + 4 * j:V_ATT + 4 * j + 4].unsqueeze(2).broadcast_to([P, 4, P]),
                                            ALU.mult).then_inc(t_free, 1)

            def q_norm(c):
                dve.wait_ge(sq_ready, c + 1)
                nc.vector.tensor_reduce(ss_q[:, 8 * c:8 * c + 8], square.rearrange("p (h d) -> p h d", h=NH),
                                        AX.X, ALU.add).then_inc(ss_ready, 1)
                dve.wait_ge(rs_ready, c + 1)
                nc.vector.tensor_tensor(qn[:, c, :].rearrange("p (h d) -> p h d", h=NH),
                                        ps[:, 4 + c % 4, :].rearrange("p (h d) -> p h d", h=NH),
                                        rs_q[:, 8 * c:8 * c + 8].unsqueeze(2).broadcast_to([P, NH, HD]),
                                        ALU.mult).then_inc(q_ready, 1)

            dve.wait_ge(vec_full, 1)
            o.mark(nc.vector.tensor_copy(vecT[:, :], ps[:, 4, 0:64]))
            o.done(nc.vector.tensor_copy(qkT[:, :], ps[0:HD, 4, 64:68]))
            o.done(nc.vector.tensor_scalar(qkT[:, 0:1], qkT[:, 0:1], HD ** -0.5, None, ALU.mult))
            nc.vector.tensor_scalar(qkT[:, 1:4], qkT[:, 1:4], qkT[:, 0:1], None, ALU.mult).then_inc(vec_done, 1)
            dve.wait_ge(vec_done, 1)
            normalise_x(0)
            for c in range(NT):
                if c + 1 < NT:
                    normalise_x(c + 1)
                evacuate_u(c)
                if c >= 1:
                    q_norm(c - 1)
            q_norm(NT - 1)

            def k_norm(i):
                b = 4 + i % 4
                dve.wait_ge(sq_ready, NT + i + 1)
                nc.vector.tensor_reduce(ss_k[:, 2 * i:2 * i + 2], square[:, 0:P].rearrange("p (h d) -> p h d", h=NG),
                                        AX.X, ALU.add).then_inc(ss_ready, 1)
                dve.wait_ge(rs_ready, NT + i + 1)
                col = 256 if i < NT else 0
                if i >= 2:
                    dve.wait_ge(t_full, T_X + (2 * (i - 1) if i - 1 <= NT else 2 * NT + (i - 1 - NT)))
                nc.vector.tensor_tensor(ks_nat[:, (i % 2) * P:(i % 2) * P + P].rearrange("p (h d) -> p h d", h=NG),
                                        ps[:, b, col:col + P].rearrange("p (h d) -> p h d", h=NG),
                                        rs_k[:, 2 * i:2 * i + 2].unsqueeze(2).broadcast_to([P, NG, HD]),
                                        ALU.mult).then_inc(kn_ready, 1)

            def evacuate_kv(i):
                c = i % NT
                if i < NT:
                    b = next_t()
                    nc.vector.tensor_copy(M["kvcT"][0:HD, :, c * P:(c + 1) * P],
                                          ps[0:HD, b, :].rearrange("p (j t) -> p j t", j=4)).then_inc(t_free, 1)
                b = next_t()
                dst, w = (M["k_sel"], 2) if i < NT else (M["k_win"], 3)
                nc.vector.tensor_scalar(dst[0:HD, :, c * P:(c + 1) * P],
                                        ps[0:HD, b, 0:2 * P].rearrange("p (g t) -> p g t", g=NG),
                                        qkT[:, w:w + 1], None, ALU.mult).then_inc(t_free, 1)

            for i in range(2 * NT):
                k_norm(i)
                if i >= 1:
                    evacuate_kv(i - 1)
            evacuate_kv(2 * NT - 1)
            dve.wait_ge(pads, 4)
            for m in range(KD):
                dve.wait_ge(m_free_act, 2 * m + 2)
                if m >= 2:
                    dve.wait_ge(conv_silu, m - 1)
                a = acc[:, m % 2, :]
                w = lambda i: vecT[:, V_CONVW + 8 * i + m:V_CONVW + 8 * i + m + 1]
                o.done(nc.vector.tensor_scalar(a, conv[:, m, 3:3 + S], w(3), vecT[:, V_CONVB + m:V_CONVB + m + 1],
                                               ALU.mult, ALU.add))
                for i in (2, 1):
                    o.done(nc.vector.scalar_tensor_tensor(a, conv[:, m, i:i + S], w(i), a, ALU.mult, ALU.add))
                nc.vector.scalar_tensor_tensor(a, conv[:, m, 0:S], w(0), a, ALU.mult, ALU.add).then_inc(conv_out, 1)
            dve.wait_ge(c_full, 1)
            nc.vector.tensor_copy(M["peT"], ps[:, 0, 0:32]).then_inc(c_read, 1)
            dve.wait_ge(c_full, 2)
            nc.vector.tensor_copy(M["pe_bias"][0:HD, :], ps[0:HD, 2, 0:2]).then_inc(c_read, 1)
            dve.wait_ge(c_full, 3)
            nc.vector.tensor_copy(M["v_cmp"][0:N_CMP, :].rearrange("p (g n) -> p g n", g=NG)[:, :, 0:HD],
                                  ps[0:N_CMP, 0, P:2 * P].rearrange("p (g d) -> p g d", g=NG)).then_inc(c_read, 1)
            dve.wait_ge(c_sq, 1)
            nc.vector.tensor_reduce(ss_c, k_sq.rearrange("p (g d) -> p g d", g=NG), AX.X, ALU.add).then_inc(c_ss, 1)
            dve.wait_ge(c_rs, 1)
            nc.vector.tensor_tensor(k_nat, ps[0:N_CMP, 0, 0:P].rearrange("p (g d) -> p g d", g=NG),
                                    rs_c.unsqueeze(2).broadcast_to([N_CMP, NG, HD]), ALU.mult).then_inc(c_kn, 1)
            dve.wait_ge(c_full, 4)
            nc.vector.tensor_scalar(M["k_cmp"].rearrange("p (g n) -> p g n", g=NG)[0:HD, :, 0:N_CMP],
                                    ps[0:HD, 1, 0:P].rearrange("p (g n) -> p g n", g=NG)[:, :, 0:N_CMP],
                                    qkT[:, 1:2], None, ALU.mult)


CMP, WIN, SEL = range(3)


def attend_order():
    steps = [("queriesT", CMP, 0), ("queries", WIN, 0)]
    for u in range(-1, NT * NG):
        new, old = u + 1 < NT * NG, u >= 0
        if old:
            steps += [("scores", SEL, u)]
        if old:
            steps += [("values", WIN, u), ("maxT", SEL, u)]
        if new:
            steps += [("scores", CMP, u + 1), ("scores", WIN, u + 1), ("maxT", CMP, u + 1)]
        if old:
            steps += [("scoresT", SEL, u)]
        if new:
            steps += [("maxT", WIN, u + 1)]
            if u + 2 < NT * NG:
                steps += [("queriesT", CMP, u + 2)]
            steps += [("scoresT", CMP, u + 1), ("scoresT", WIN, u + 1)]
            if u + 2 < NT * NG:
                steps += [("queries", WIN, u + 2)]
            steps += [("values", CMP, u + 1)]
            if (u + 1) // NG >= NT // 2:
                steps += [("selT", SEL, u + 1)]
        if old:
            steps += [("values", SEL, u)]
    return steps


def cmp_keys(c):
    return (c * P + P - L_CMP) // CSTR + 1


def key_blocks(br, c):
    return {CMP: [0], WIN: list(range(max(0, c - 2), c + 1)), SEL: list(range(c + 1))}[br]


def score_slots(br, c):
    return {CMP: [[0, 1, 2, 3]], WIN: [[0, 1], [2, 3]],
            SEL: [[0, 1], [2, 3]] if c < NT // 2 else [[0], [1], [2], [3]]}[br]


def attend(nc, N, M, A, C, out):
    sem = N.sem
    ps, ident, identb, Q, qn = M["ps"], M["ident"], M["identb"], M["Q"], M["qn"]
    masksb = M["masksb"]
    mask_cmp = M["mask_cmp"].rearrange("p (c n) -> p c n", c=NT)
    mask_cmpT = M["mask_cmpT"].rearrange("p (c n) -> p c n", c=NT)
    k_cmp = M["k_cmp"].rearrange("p (g n) -> p g n", g=NG)
    v_cmp = M["v_cmp"].rearrange("p (g n) -> p g n", g=NG)
    keys = {WIN: M["k_win"], SEL: M["k_sel"]}
    vals = {WIN: M["v_win"], SEL: M["v_sel"]}
    pT = {CMP: M["kvcT"][:, 0, 0:BANK].unsqueeze(1),
          WIN: M["kvcT"][:, 1:3, :].rearrange("p a n -> p (a n)")[:, 0:3 * BANK].rearrange("p (b n) -> p b n", b=3),
          SEL: M["big_u"][:, 0:NT * BANK].rearrange("p (b n) -> p b n", b=NT)}
    sg = M["sg"].rearrange("p (c h r) -> p c h r", c=NT, h=NH)
    o_att = M["o_att"]
    o_tmp = M["o_tmp"].rearrange("p (h d) -> p h d", h=GQ)
    t = M["sel_tmp"]
    imp_h, imp, score = t[:, 0:64], t[:, 64:80], t[:, 80:96]
    gt, eq, rank = t[:, 96:352], t[:, 352:608], t[:, 608:624]
    before = M["before"].rearrange("p (j i) -> p j i", j=N_BLK)
    score_rows = M["score_rows"].rearrange("p (a c j) -> p a c j", a=2, c=NT)
    neg = M["att_small"][:, 0:12].rearrange("p (r h) -> p r h", r=3)
    den, coef = M["att_small"][:, 12:24].rearrange("p (r h) -> p r h", r=3), M["att_small"][:, 24:36].rearrange("p (r h) -> p r h", r=3)
    head_delta = M["head_delta"][0:GQ, :]

    consts = sem("masks_cast")
    q_cmp_rows, q_rows = sem("query_rows_cmp"), sem("query_rows_both")
    slot_full, slot_read = sem("scores_full"), sem("scores_read")
    max_ready, max_full, max_rows = sem("maxima_ready"), sem("maxima_transposed"), sem("maxima_rows")
    st_full, exp_done = sem("scoresT_full"), sem("exp_done")
    o_full, o_read = sem("values_full"), sem("values_read")
    sel_ready, sel_full, sel_rows = sem("selection_ready"), sem("selection_transposed"), sem("selection_rows")
    zeroed, zeros_set = sem("maxima_rows_zeroed"), sem("zeros_set")
    ord_dve, ord_act = sem("vector_order2"), sem("scalar_order2")
    gates_exp = sem("gates_exp")
    dt_sem, head_rows = M["dt_steps"], M["head_rows"]
    flat = lambda i: small_part(M, i)
    part = lambda i: flat(i).rearrange("p (c h) -> p c h", c=NT)

    steps = attend_order()
    slots_before, st_before, o_before, max_before, sel_before = {}, {}, {}, {}, {}
    a = b = v = m = z = 0
    for kind, br, u in steps:
        c = u // NG
        if kind == "scores":
            slots_before[br, u] = a
            a += len(score_slots(br, c))
        elif kind == "scoresT":
            st_before[br, u] = b
            b += len(key_blocks(br, c))
        elif kind == "values":
            o_before[br, u] = v
            v += 1
        elif kind == "maxT":
            max_before[br, u] = m
            m += 1
        elif kind == "selT":
            sel_before[u] = z
            z += 1

    with nc.Block() as block:
        @block.sync
        def _(sp):
            for u in range(NT * NG - NG):
                sp.wait_ge(st_full, st_before[SEL, u] + u // NG + 1)
                load_alibi(sp, M, C, u + NG)
                if u == 0:
                    sp.wait_ge(zeros_set, 1)
                if SLOTS_SURE + u < SLOTS:
                    sp.dma_start(M["y_dram"][(SLOTS_SURE + u) * P:(SLOTS_SURE + u + 1) * P, :].rearrange("p (a n) -> p a n", n=256),
                                 M["zeros"][:, :].unsqueeze(1).broadcast_to([P, D // 256, 256])).then_inc(M["s_zero_slots"], 16)

        @block.gpsimd
        def _(pool):
            nc.gpsimd.memset(M["zeros"][:, :], 0.0).then_inc(zeros_set, 1)
            pool.wait_ge(zeros_set, 1)
            for u in range(NT * NG - NG):
                pool.wait_ge(st_full, st_before[SEL, u] + u // NG + 1)
                nc.gpsimd.memset(Q[ROW_MAX:ROW_MAX + GQ, :, u % NG, :], 0.0).then_inc(zeroed, 1)

        @block.tensor
        def _(pe):
            state = {"maxT": 0, "selT": 0, "cmp": 0, "bank6": 0, "late": None}

            def bank7_free():
                for n, read in ((state["maxT"], max_rows), (state["selT"], sel_rows), (state["cmp"], o_read)):
                    if n:
                        pe.wait_ge(read, n)

            def scores(br, u):
                c, g = u // NG, u % NG
                if br == CMP:
                    pe.wait_ge(q_cmp_rows, u + 1)
                    pe.wait_ge(M["s_alibi"][g], 48 * (c + 1))
                    if u >= NG:
                        pe.wait_ge(zeroed, u - 1)
                elif br == WIN:
                    pe.wait_ge(q_rows, u + 1)
                elif c >= NT // 2:
                    pe.wait_ge(sel_rows, sel_before[u] + 1)
                for i, heads in enumerate(score_slots(br, c)):
                    k = slots_before[br, u] + i
                    if k >= 2:
                        pe.wait_ge(slot_read, k - 1)
                    for j, h in enumerate(heads):
                        lhsT = Q[0:KR, br, g, h * P:(h + 1) * P]
                        if br == CMP:
                            n = cmp_keys(c)
                            o = ps[:, 2 * (k % 2), h * 64:h * 64 + n]
                            nc.tensor.matmul(o, lhsT, k_cmp[0:KR, g, 0:n], start=True, stop=False)
                            last = nc.tensor.matmul(o, identb[:, :], mask_cmp[:, c, 0:n], start=False, stop=True)
                            continue
                        blocks = key_blocks(br, c)
                        k0 = blocks[0] * P
                        for part in range(0, len(blocks), 4):
                            inner = blocks[part:part + 4]
                            bank = 2 * (k % 2) + (j if len(heads) > 1 else part // 4)
                            n = len(inner) * P
                            diag = inner[-1] == c
                            far = br == WIN and inner[0] == c - 2
                            s0 = k0 + part * P
                            last = nc.tensor.matmul(ps[:, bank, 0:n], lhsT, keys[br][0:KR, g, s0:s0 + n],
                                                    start=True, stop=not (diag or far))
                            if far:
                                nc.tensor.matmul(ps[:, bank, 0:P], identb[:, :], masksb[:, 2, :], start=False, stop=False)
                            if diag:
                                last = nc.tensor.matmul(ps[:, bank, n - P:n], identb[:, :], masksb[:, 0, :],
                                                        start=False, stop=True)
                    last.then_inc(slot_full, 1)

            def maxT(br, u):
                n = max_before[br, u]
                pe.wait_ge(max_ready, n + 1)
                bank7_free()
                nc.tensor.transpose(ps[0:GQ, 7, 0:P], neg[:, br, :], ident[:, :]).then_inc(max_full, 1)
                state["maxT"] = n + 1

            def selT(u):
                n = sel_before[u]
                pe.wait_ge(sel_ready, n + 1)
                bank7_free()
                nc.tensor.matmul(ps[64:64 + N_BLK, 7, 0:P], M["sel01"], identb[:, :], start=True, stop=True)\
                    .then_inc(sel_full, 1)
                state["selT"] = n + 1

            def scoresT(br, u):
                c, g = u // NG, u % NG
                pe.wait_ge(max_rows, max_before[br, u] + 1)
                for i, b in enumerate(key_blocks(br, c)):
                    k = st_before[br, u] + i
                    if k >= 2:
                        pe.wait_ge(exp_done, k - 1)
                    rhs = Q[0:KR, br, g, :]
                    if br == CMP:
                        n = cmp_keys(c)
                        o = ps[0:n, 4 + k % 2, :]
                        nc.tensor.matmul(o, k_cmp[0:KR, g, 0:n], rhs, start=True, stop=False)
                        last = nc.tensor.matmul(o, identb[0:N_CMP, 0:n],
                                                mask_cmpT[0:N_CMP, c, :].unsqueeze(1).broadcast_to([N_CMP, GQ, P]),
                                                start=False, stop=True)
                    else:
                        o = ps[:, 4 + k % 2, :]
                        mask = 1 if b == c else 3 if br == WIN and b == c - 2 else None
                        last = nc.tensor.matmul(o, keys[br][0:KR, g, b * P:(b + 1) * P], rhs,
                                                start=True, stop=mask is None)
                        if mask is not None:
                            last = nc.tensor.matmul(o, identb[:, :],
                                                    masksb[:, mask, :].unsqueeze(1).broadcast_to([P, GQ, P]),
                                                    start=False, stop=True)
                    last.then_inc(st_full, 1)

            def values(br, u):
                c, g = u // NG, u % NG
                n = o_before[br, u]
                blocks = key_blocks(br, c)
                bank = 7 if br == CMP else 6
                if br == CMP:
                    bank7_free()
                    state["cmp"] = n + 1
                else:
                    if state["bank6"]:
                        pe.wait_ge(o_read, state["bank6"])
                    state["bank6"] = n + 1
                pe.wait_ge(exp_done, st_before[br, u] + len(blocks))
                w = HD + 17 if br == CMP else HD + 1
                for h in range(GQ):
                    if h == GQ - 1 and state["late"] is not None:
                        selT(state["late"])
                        state["late"] = None
                    o = ps[:, bank, h * w:(h + 1) * w]
                    for i, b in enumerate(blocks):
                        if br == CMP:
                            kk = cmp_keys(c)
                            last = nc.tensor.matmul(o, pT[CMP][0:kk, 0, h * P:(h + 1) * P], v_cmp[0:kk, g, 0:w],
                                                    start=True, stop=True)
                        else:
                            last = nc.tensor.matmul(o, pT[br][:, i, h * P:(h + 1) * P], vals[br][:, b, g, :],
                                                    start=(i == 0), stop=(i == len(blocks) - 1))
                last.then_inc(o_full, 1)

            pe.wait_ge(consts, 4)
            for kind, br, u in steps:
                if kind == "scores":
                    scores(br, u)
                elif kind == "maxT":
                    maxT(br, u)
                elif kind == "selT":
                    state["late"] = u
                elif kind == "scoresT":
                    scoresT(br, u)
                elif kind == "values":
                    values(br, u)

        @block.scalar
        def _(act):
            o = Order(act, ord_act)
            nc.scalar.preload_act_table_set("natural_log_exp_and_others")
            nc.scalar.activation(M["sg"].rearrange("p (c n) -> p c n", c=NT), M["gate_dt"][:, :, 0:NGATE], ACT.Exp,
                                 scale=-1.0).then_inc(gates_exp, 1)
            for kind, br, u in steps:
                c, g = u // NG, u % NG
                if kind == "queries":
                    act.wait_ge(q_cmp_rows, u + 1)
                    nc.scalar.activation(Q[0:HD, 1:3, g, :], Q[0:HD, CMP, g, :].unsqueeze(1).broadcast_to([HD, 2, BANK]),
                                         ACT.Copy).then_inc(q_rows, 1)
                elif kind == "scoresT":
                    for i, b in enumerate(key_blocks(br, c)):
                        k = st_before[br, u] + i
                        n = cmp_keys(c) if br == CMP else P
                        act.wait_ge(st_full, k + 1)
                        nc.scalar.activation(pT[br][0:n, i, :], ps[0:n, 4 + k % 2, :], ACT.Exp).then_inc(exp_done, 1)
                    if (br, u) == (SEL, 3):
                        act.wait_ge(dt_sem, 2)
                        o.mark(nc.scalar.activation(head_rows[:, 1, :], head_rows[:, 1, :], ACT.Exp))
                        o.done(nc.scalar.activation(flat(0), flat(6), ACT.Exp, scale=-1.0))
                        nc.scalar.activation(flat(0), flat(0), ACT.Ln, bias=1.0).then_inc(dt_sem, 1)

        @block.vector
        def _(dve):
            o = Order(dve, ord_dve)
            nc.vector.tensor_copy(masksb[:, :, :].rearrange("p a b -> p (a b)"), M["stage_masks"]).then_inc(consts, 1)
            nc.vector.tensor_copy(mask_cmp[:, :, 0:N_CMP],
                                  M["stage_cmp"].rearrange("p (c n) -> p c n", c=NT)).then_inc(consts, 1)
            nc.vector.tensor_copy(mask_cmpT[0:N_CMP, :, :].rearrange("p c n -> p (c n)"), M["stage_cmpT"]).then_inc(consts, 1)
            nc.vector.tensor_copy(identb[:, :], ident[:, :]).then_inc(consts, 1)
            dve.wait_ge(consts, 4)

            def gates():
                dve.wait_ge(gates_exp, 1)
                o.done(nc.vector.tensor_scalar(M["sg"], M["sg"], 1.0, None, ALU.add))
                o.done(nc.vector.reciprocal(M["sg"], M["sg"]))

            def maxima(br, u):
                c = u // NG
                for i, heads in enumerate(score_slots(br, c)):
                    k = slots_before[br, u] + i
                    dve.wait_ge(slot_full, k + 1)
                    h0, b0 = heads[0], 2 * (k % 2)
                    if br == CMP:
                        src = ps[:, b0, 0:4 * 64].rearrange("p (h n) -> p h n", h=GQ)[:, :, 0:cmp_keys(c)]
                    elif len(heads) == 2:
                        src = ps[:, b0:b0 + 2, 0:len(key_blocks(br, c)) * P]
                    else:
                        src = ps[:, b0:b0 + 2, :].rearrange("p b n -> p (b n)")[:, 0:(c + 1) * P].unsqueeze(1)
                    ins = nc.vector.tensor_reduce(neg[:, br, h0:h0 + len(heads)], src, AX.X, ALU.max, negate=True)
                    ins.then_inc(slot_read, 1)
                dve.wait_ge(slot_read, k + 1)
                nc.vector.tensor_scalar(neg[:, br, :], neg[:, br, :], 1.0e20, None, ALU.min).then_inc(max_ready, 1)

            def maxima_to_rows(br, u):
                dve.wait_ge(max_full, max_before[br, u] + 1)
                nc.vector.tensor_tensor(Q[ROW_MAX:ROW_MAX + GQ, br, u % NG, :].rearrange("p (h q) -> p h q", h=GQ),
                                        ps[0:GQ, 7, 0:P].unsqueeze(1).broadcast_to([GQ, GQ, P]),
                                        head_delta.rearrange("p (h q) -> p h q", h=GQ), ALU.mult).then_inc(max_rows, 1)

            def read_values(br, u):
                c, g = u // NG, u % NG
                dve.wait_ge(o_full, o_before[br, u] + 1)
                w = HD + 17 if br == CMP else HD + 1
                O = ps[:, 7 if br == CMP else 6, 0:GQ * w].rearrange("p (h n) -> p h n", h=GQ)
                dst = o_att[:, c, g * GQ * HD:(g + 1) * GQ * HD].rearrange("p (h d) -> p h d", h=GQ)
                gate_at = {CMP: 0, SEL: 1, WIN: 2}[br]
                d, f = den[:, br, :], coef[:, br, :]
                o.done(nc.vector.tensor_scalar(d, O[:, :, HD], 1.0e-30, None, ALU.max))
                o.done(nc.vector.reciprocal(d, d))
                o.done(nc.vector.tensor_tensor(f, d, sg[:, c, g * GQ:(g + 1) * GQ, gate_at], ALU.mult))
                fb = f.unsqueeze(2).broadcast_to([P, GQ, HD])
                if br == CMP:
                    if c >= NT // 2:
                        o.mark(nc.vector.tensor_tensor(imp_h.rearrange("p (h j) -> p h j", h=GQ), O[:, :, HD + 1:w],
                                                       d.unsqueeze(2).broadcast_to([P, GQ, N_BLK]), ALU.mult))
                    o.mark(nc.vector.tensor_tensor(dst, O[:, :, 0:HD], fb, ALU.mult))
                    o.wait()
                    dve.sem_inc(o_read, 1)
                else:
                    nc.vector.tensor_tensor(o_tmp, O[:, :, 0:HD], fb, ALU.mult).then_inc(o_read, 1)
                    dve.wait_ge(o_read, o_before[br, u] + 1)
                    o.done(nc.vector.tensor_tensor(dst, dst, o_tmp, ALU.add))

            def select(u):
                c = u // NG
                o.done(nc.vector.tensor_reduce(imp, imp_h.rearrange("p (h j) -> p j h", h=GQ), AX.X, ALU.add))
                o.done(nc.vector.tensor_tensor(score, imp, score_rows[:, 0, c, :], ALU.mult))
                o.done(nc.vector.tensor_tensor(score, score, score_rows[:, 1, c, :], ALU.add))
                si = score.unsqueeze(1).broadcast_to([P, N_BLK, N_BLK])
                sj = score.unsqueeze(2).broadcast_to([P, N_BLK, N_BLK])
                g3, e3 = gt.rearrange("p (j i) -> p j i", j=N_BLK), eq.rearrange("p (j i) -> p j i", j=N_BLK)
                o.mark(nc.vector.tensor_tensor(g3, si, sj, ALU.is_gt))
                o.done(nc.vector.tensor_tensor(e3, si, sj, ALU.is_equal))
                o.done(nc.vector.tensor_tensor(e3, e3, before, ALU.mult))
                o.done(nc.vector.tensor_tensor(g3, g3, e3, ALU.add))
                o.done(nc.vector.tensor_reduce(rank, g3, AX.X, ALU.add))
                nc.vector.tensor_scalar(M["sel01"], rank, float(TOP_N) - 0.5, None, ALU.is_lt).then_inc(sel_ready, 1)

            def selection_to_rows(u):
                dve.wait_ge(sel_full, sel_before[u] + 1)
                nc.vector.tensor_scalar(Q[ROW_SEL:ROW_SEL + N_BLK, SEL, u % NG, :].rearrange("p (h q) -> p h q", h=GQ),
                                        ps[64:64 + N_BLK, 7, 0:P].unsqueeze(1).broadcast_to([N_BLK, GQ, P]),
                                        -1.0, -NEG, ALU.add, ALU.mult).then_inc(sel_rows, 1)

            for kind, br, u in steps:
                c, g = u // NG, u % NG
                if kind == "queriesT":
                    dst = Q[0:HD, CMP, g, :].rearrange("p (h q) -> p h q", h=GQ)
                    src = qn[:, c, g * GQ * HD:(g + 1) * GQ * HD].rearrange("p (h d) -> p h d", h=GQ)
                    for i in range(P // 32):
                        for j in range(HD // 32):
                            last = nc.vector.transpose(dst[j * 32:(j + 1) * 32, :, i * 32:(i + 1) * 32],
                                                       src[i * 32:(i + 1) * 32, :, j * 32:(j + 1) * 32])
                    last.then_inc(q_cmp_rows, 1)
                    if u == 1:
                        gates()
                elif kind == "scores":
                    maxima(br, u)
                elif kind == "maxT":
                    maxima_to_rows(br, u)
                elif kind == "selT":
                    selection_to_rows(u)
                elif kind == "values":
                    read_values(br, u)
                    if br == CMP and c >= NT // 2:
                        select(u)
                    if (br, u) == (SEL, 2):
                        o.done(nc.vector.tensor_tensor(part(0), M["gate_dt"][:, :, NGATE:],
                                                       head_rows[:, 0, :].unsqueeze(1).broadcast_to([P, NT, SH]), ALU.add))
                        nc.vector.tensor_scalar(flat(1), flat(0), 0.0, None, ALU.max).then_inc(dt_sem, 1)
                        dve.wait_ge(dt_sem, 1)
                        nc.vector.scalar_tensor_tensor(flat(6), flat(1), 2.0, flat(0), ALU.mult, ALU.subtract)\
                            .then_inc(dt_sem, 1)
                    if (br, u) == (SEL, 4):
                        dve.wait_ge(dt_sem, 3)
                        nc.vector.tensor_tensor(flat(0), flat(0), flat(1), ALU.add).then_inc(dt_sem, 1)
                        dve.wait_ge(dt_sem, 4)
                        nc.vector.tensor_scalar(flat(6), flat(0), -1.0, None, ALU.mult).then_inc(dt_sem, 1)
                        dve.wait_ge(dt_sem, 5)
                        nc.vector.tensor_tensor(part(1), part(6), head_rows[:, 1, :].unsqueeze(1).broadcast_to([P, NT, SH]),
                                                ALU.mult).then_inc(dt_sem, 1)


def ssd(nc, N, M, A, C, out):
    sem = N.sem
    ps, ident, identb, conv, z, tri = M["ps"], M["ident"], M["identb"], M["conv"], M["z"], M["tri"]
    u = M["big_u"]
    x_dt = u[:, 0:1024].rearrange("p (b h d) -> p b h d", b=2, h=SH)
    x_decay = u[:, 1024:2048].rearrange("p (b h d) -> p b h d", b=2, h=SH)
    x_skip = u[:, 2048:3072].rearrange("p (b h d) -> p b h d", b=2, h=SH)
    mT = u[:, 3072:5120].rearrange("p (b h l) -> p b h l", b=2, h=SH)
    decT = u[:, 5120:7168].rearrange("p (b h l) -> p b h l", b=2, h=SH)
    b_nat = u[:, 7168:7680].rearrange("p (b g n) -> p b g n", b=2, g=NG)
    state = u[:, 7680:8192].rearrange("p (h d) -> p h d", h=SH)
    y = M["misc"][:, 0:1024].rearrange("p (b h d) -> p b h d", b=2, h=SH)
    ones = M["misc"][:, 1024:1024 + P]
    junk = M["misc"][:, 2048:2048 + 256]
    sm = M["small"]
    part = lambda i: small_part(M, i).rearrange("p (c h) -> p c h", c=NT)
    flat = lambda i: small_part(M, i)
    dt, a, neg_cs, decay, e_cs, e_tot = (part(i) for i in range(6))
    M["ss_ssm"], M["ss_att"], M["rs_att"] = sm[:, 448:464], sm[:, 464:472], sm[:, 472:480]
    o_ssm = M["qn"]
    GW = 4 * HD

    prep_full, prep_done = sem("ssd_constants_full"), sem("ssd_constants_ready")
    dt_sem = M["dt_steps"]
    pre_full = sem("chunk_operands_full")
    x_read, b_read, cb_read, dec_read = sem("x_natural_read"), sem("b_natural_read"), sem("cb_read"), sem("decay_read")
    y_full, y_read = sem("y_full"), sem("y_read")
    st_full, st_ready = sem("new_states_full"), sem("state_ready")
    y_ready = sem("y_ready")
    ord_dve, ord_act = sem("vector_order3"), sem("scalar_order3")
    set_up = sem("ssd_set_up")
    X_BANK, CB_BANK, DEC_BANK, YD_BANK, YO_BANK, ST_BANK = 0, 1, 2, 4, 5, 6

    with nc.Block() as block:
        @block.sync
        def _(sp):
            for k in range(KD):
                sp.dma_start(M["big_w"][:, k * D:(k + 1) * D], A["w_out"][0, k * P:(k + 1) * P, :]).then_inc(M["s_w_out"], 16)

        @block.gpsimd
        def _(pool):
            nc.gpsimd.memset(ones, 1.0).then_inc(set_up, 1)
            nc.gpsimd.memset(u[:, 7680:8192], 0.0).then_inc(set_up, 1)
            pool.wait_ge(M["s_w_out"], 16 * KD)
            for k in range(KD):
                wk = M["big_w"][:, k * D:(k + 1) * D]
                nc.gpsimd.tensor_scalar(wk, wk, M["vecT"][:, M["V_AON"] + k:M["V_AON"] + k + 1], None, ALU.mult)\
                    .then_inc(M["w_out_scaled"], 1)

        @block.tensor
        def _(pe):
            pe.wait_ge(set_up, 2)
            pe.wait_ge(dt_sem, 6)
            nc.tensor.matmul(ps[:, 7, 0:64], tri[:, :], flat(1), start=True, stop=True)
            nc.tensor.matmul(ps[:, 7, 64:128], ones, flat(1), start=True, stop=True).then_inc(prep_full, 1)

            def operands(c):
                tok = slice(3 + c * P, 3 + (c + 1) * P)
                if c >= 1:
                    pe.wait_ge(x_read, c)
                for m in range(4):
                    nc.tensor.transpose(ps[:, X_BANK, m * P:(m + 1) * P], conv[:, m, tok], ident[:, :])
                if c >= 1:
                    pe.wait_ge(b_read, c)
                    pe.wait_ge(cb_read, NG * c)
                for g in range(NG):
                    nc.tensor.transpose(ps[:, CB_BANK, g * P:(g + 1) * P], conv[:, 4 + g, tok], ident[:, :])
                for g in range(NG):
                    nc.tensor.matmul(ps[:, CB_BANK, (2 + g) * P:(3 + g) * P], conv[:, 4 + g, tok], conv[:, 6 + g, tok],
                                     start=True, stop=True)
                if c >= 1:
                    pe.wait_ge(dec_read, NG * c)
                for g in range(NG):
                    o = ps[:, DEC_BANK + g, :]
                    nc.tensor.matmul(o, identb[:, :], M["masksb"][:, 1, :].unsqueeze(1).broadcast_to([P, GQ, P]),
                                     start=True, stop=True, skip_group_check=True)
                    for r in range(GQ):
                        last = nc.tensor.matmul(o[:, r * P:(r + 1) * P],
                                                a[:, c, g * GQ + r:g * GQ + r + 1].broadcast_to([P, P]), tri[:, :],
                                                start=False, stop=True, skip_group_check=True)
                last.then_inc(pre_full, 1)

            operands(0)
            for c in range(NT):
                tok = slice(3 + c * P, 3 + (c + 1) * P)
                if c + 1 < NT:
                    operands(c + 1)
                if c >= 1:
                    pe.wait_ge(y_read, c)
                    pe.wait_ge(st_ready, c)
                    for g in range(NG):
                        nc.tensor.matmul(ps[:, YO_BANK, g * GW:(g + 1) * GW], conv[:, 6 + g, tok],
                                         state[:, g * GQ:(g + 1) * GQ, :], start=True, stop=True)
                pe.wait_ge(b_read, c + 1)
                pe.wait_ge(cb_read, NG * (c + 1))
                for h in range(SH):
                    last = nc.tensor.matmul(ps[:, YD_BANK, h * HD:(h + 1) * HD], mT[:, c % 2, h, :], x_dt[:, c % 2, h, :],
                                            start=True, stop=True)
                last.then_inc(y_full, 1)
                if c + 1 < NT:
                    for g in range(NG):
                        last = nc.tensor.matmul(ps[:, ST_BANK, g * GW:(g + 1) * GW], b_nat[:, c % 2, g, :],
                                                x_decay[:, c % 2, g * GQ:(g + 1) * GQ, :], start=True, stop=True)
                    last.then_inc(st_full, 1)

        @block.scalar
        def _(act):
            o = Order(act, ord_act)
            act.wait_ge(dt_sem, 8)
            for i in (3, 4, 5):
                nc.scalar.activation(flat(i), flat(i), ACT.Exp).then_inc(prep_done, 1)

            def square(c):
                act.wait_ge(y_ready, c + 1)
                for g in range(NG):
                    o.done(nc.scalar.activation(junk, o_ssm[:, c, g * GW:(g + 1) * GW], ACT.Square,
                                                accum_out=M["ss_ssm"][:, NG * c + g:NG * c + g + 1]))

            for c in range(NT):
                act.wait_ge(pre_full, c + 1)
                if c >= 2:
                    act.wait_ge(y_full, c - 1)
                    act.wait_ge(st_full, c - 1)
                nc.scalar.activation(b_nat[:, c % 2, :, :], ps[:, CB_BANK, 0:2 * P].rearrange("p (g n) -> p g n", g=NG),
                                     ACT.Copy).then_inc(b_read, 1)
                for g in range(NG):
                    for r in range(GQ):
                        h = g * GQ + r
                        last = nc.scalar.activation(decT[:, c % 2, h, :], ps[:, DEC_BANK + g, r * P:(r + 1) * P], ACT.Exp,
                                                    bias=neg_cs[:, c, h:h + 1])
                    last.then_inc(dec_read, 1)
                if c >= 2:
                    square(c - 2)
            square(NT - 2)
            ss_att, rs_att = M["ss_att"], M["rs_att"]
            for c in range(NT):
                o.done(nc.scalar.activation(M["ring_gu"][:, 4096:4608], M["o_att"][:, c, :], ACT.Square,
                                            accum_out=ss_att[:, c:c + 1]))
            o.done(nc.scalar.activation(rs_att, ss_att, ACT.Ln, scale=1.0 / 512, bias=M["eps"][:, 0:1]))
            o.mark(nc.scalar.activation(rs_att, rs_att, ACT.Exp, scale=-0.5))
            square(NT - 1)

        @block.vector
        def _(dve):
            o = Order(dve, ord_dve)
            rows = M["head_rows"]
            dve.wait_ge(prep_full, 1)
            o.mark(nc.vector.tensor_scalar(flat(2), ps[:, 7, 0:64], -1.0, None, ALU.mult))
            o.mark(nc.vector.tensor_copy(flat(4), ps[:, 7, 0:64]))
            o.done(nc.vector.tensor_copy(flat(5), ps[:, 7, 64:128]))
            nc.vector.tensor_tensor(flat(3), flat(5), flat(4), ALU.subtract).then_inc(dt_sem, 1)
            dve.wait_ge(dt_sem, 7)
            nc.vector.tensor_copy(flat(6)[:, 0:1], flat(3)[:, 0:1]).then_inc(dt_sem, 1)

            def heads(v):
                return v.unsqueeze(2).broadcast_to([P, v.shape[1], HD])

            def chunk_in(c):
                dve.wait_ge(pre_full, c + 1)
                b = c % 2
                if c >= 2:
                    dve.wait_ge(y_full, c - 1)
                    dve.wait_ge(st_full, c - 1)
                xs = ps[:, X_BANK, :].rearrange("p (h d) -> p h d", h=SH)
                o.mark(nc.vector.tensor_tensor(x_dt[:, b], xs, heads(dt[:, c, :]), ALU.mult))
                nc.vector.tensor_tensor(x_skip[:, b], xs, heads(rows[:, 2, :]), ALU.mult).then_inc(x_read, 1)
                o.wait()
                o.done(nc.vector.tensor_tensor(x_decay[:, b], x_dt[:, b], heads(decay[:, c, :]), ALU.mult))
                dve.wait_ge(b_read, c + 1)
                for g in range(NG):
                    dve.wait_ge(dec_read, NG * c + g + 1)
                    nc.vector.tensor_tensor(mT[:, b, g * GQ:(g + 1) * GQ, :], decT[:, b, g * GQ:(g + 1) * GQ, :],
                                            ps[:, CB_BANK, (2 + g) * P:(3 + g) * P].unsqueeze(1).broadcast_to([P, GQ, P]),
                                            ALU.mult).then_inc(cb_read, 1)

            def chunk_out(c):
                b = c % 2
                yb = y[:, b]
                dve.wait_ge(y_full, c + 1)
                dve.wait_ge(x_read, c + 1)
                o.done(nc.vector.tensor_tensor(yb, ps[:, YD_BANK, :].rearrange("p (h d) -> p h d", h=SH), x_skip[:, b],
                                               ALU.add))
                if c >= 1:
                    o.done(nc.vector.tensor_tensor(x_skip[:, b], ps[:, YO_BANK, :].rearrange("p (h d) -> p h d", h=SH),
                                                   heads(e_cs[:, c, :]), ALU.mult))
                dve.sem_inc(y_read, 1)
                if c + 1 < NT:
                    o.done(nc.vector.tensor_tensor(state, state, heads(e_tot[:, c, :]), ALU.mult))
                    dve.wait_ge(st_full, c + 1)
                    nc.vector.tensor_tensor(state, state, ps[:, ST_BANK, :].rearrange("p (h d) -> p h d", h=SH),
                                            ALU.add).then_inc(st_ready, 1)
                if c >= 1:
                    o.done(nc.vector.tensor_tensor(yb, yb, x_skip[:, b], ALU.add))
                nc.vector.tensor_tensor(o_ssm[:, c, :].rearrange("p (h d) -> p h d", h=SH), yb,
                                        z[:, c, :].rearrange("p (h d) -> p h d", h=SH), ALU.mult).then_inc(y_ready, 1)

            dve.wait_ge(prep_done, 3)
            dve.wait_ge(set_up, 2)
            chunk_in(0)
            for c in range(NT):
                if c + 1 < NT:
                    chunk_in(c + 1)
                chunk_out(c)


def transpose_chunks(nc, dst, src):
    for i in range(P // 32):
        for j in range(P // 32):
            last = nc.vector.transpose(dst[j * 32:(j + 1) * 32, :, i * 32:(i + 1) * 32],
                                       src[i * 32:(i + 1) * 32, :, j * 32:(j + 1) * 32])
    return last


def load_expert(sp, M, A, e, r):
    ws = bass.ds(e, 1)
    gu = M["ring_gu"][:, r * GU_COLS:(r + 1) * GU_COLS].rearrange("p (k n) -> p k n", k=KD)
    dn = M["ring_d"][:, r * D_COLS:(r + 1) * D_COLS].rearrange("p (f n) -> p f n", f=D_EXP // P)
    for i, name in enumerate(("w_gate", "w_up")):
        sp.dma_start(gu[:, :, i * D_EXP:(i + 1) * D_EXP],
                     A[name][0, ws].rearrange("e (k p) n -> p (e k) n", p=P)).then_inc(M["s_expert"][r], 16)
    sp.dma_start(dn, A["w_down"][0, ws].rearrange("e (f p) n -> p (e f) n", p=P)).then_inc(M["s_expert"][r], 16)


def merge(nc, N, M, A, C, out):
    sem = N.sem
    ps, ident = M["ps"], M["ident"]
    u = M["big_u"]
    catT = u[:, 0:2048].rearrange("p (b k t) -> p b k t", b=2, k=KD)
    hnT = u[:, 2048:3072].rearrange("p (k t) -> p k t", k=KD)
    hn = u[:, 3072:5120].rearrange("p (b n) -> p b n", b=2)
    at = [5120]

    def cols(n, base=u, at=at):
        at[0] += n
        return base[:, at[0] - n:at[0]]

    NR = 4 + N_EXP
    rw = cols(KD * NR).rearrange("p (k n) -> p k n", k=KD)
    edges, iota, token, tri_strict, before_, bias = cols(EDGES), cols(P), cols(NT), cols(P), cols(256), cols(NR)
    before = before_.rearrange("p (j i) -> p j i", j=N_BLK)
    lg = cols(NT * NR).rearrange("p (c n) -> p c n", c=NT)
    ge = cols(2 * NT * EDGES).rearrange("p (i s) -> p i s", s=EDGES)
    c1, c2, t4 = cols(NT * 16), cols(NT * 16), cols(NT * 16)
    H = [cols(P), cols(P)]
    both, pos, base = cols(P), cols(P), cols((NT + 1) * N_EXP)
    gmax, gp, l1, l2, d21, spare = (cols(NT) for _ in range(6))
    g4, e4, r4, oh_g, oh1, oh2 = (cols(NT * 4).rearrange("p (c n) -> p c n", c=NT) for _ in range(6))
    tiles, start, end_, st128 = (cols(N_EXP) for _ in range(4))
    posk, slot, place, wk = (cols(2 * NT) for _ in range(4))
    assert at[0] <= KD * S
    x_in = M["misc"][:, 0:2048].rearrange("p (b n) -> p b n", b=2)
    hot = M["misc"][:, 0:1024].rearrange("p (i s) -> p i s", s=64)[:, :, 0:TABLE]
    e_cmp = M["misc"][0:1, 1024:1536].rearrange("p (s e) -> p s e", e=N_EXP)
    e_sum = M["misc"][0:1, 1536:1536 + TABLE]
    e_ring = M["misc"][0:1, 1568:1568 + TABLE]
    place_hot = u[:, 0:2048].rearrange("p (i n) -> p i n", n=P)
    values = u[:, 2048:3072].rearrange("p (i n) -> p i n", n=2 * TABLE)
    w_out = M["big_w"][:, :].rearrange("p (k n) -> p k n", k=KD)
    h = M["conv"][:, :, 0:D]
    o_att, o_ssm = M["o_att"], M["qn"]
    junk, ffn_rows = M["ring_gu"][:, 4096:4096 + D], M["ring_gu"][:, 4096 + D:4096 + 2 * D]
    rs = M["small"]
    rs_att, rs_ssm, ss_h, rs_h = M["rs_att"], rs[:, 480:496], rs[:, 496:504], rs[:, 504:512]

    s_x = [sem("x_again_loaded0"), sem("x_again_loaded1")]
    s_route, s_ffn = sem("router_loaded"), sem("ffn_norm_loaded")
    s_hn = [sem("hn_stored0"), sem("hn_stored1")]
    cat_ready, cat_full, cat_transposed = sem("cat_scaled"), sem("first_catT_full"), sem("catT_ready")
    o_full, h_ready, rs_ready, hn_ready = sem("out_full"), sem("h_ready"), sem("h_rstd_ready"), sem("hn_ready")
    hnT_full, hnT_evac, lg_full = sem("hnT_full"), sem("hnT_ready"), sem("logits_full")
    act_plan = sem("scalar_plan_steps")
    route_in, route_out = sem("pair_counts_in"), sem("pair_counts_full")
    tab_in, tab_out = sem("table_operands"), sem("table_full")
    ones_set, tab_copied = sem("ones_set"), sem("token_table_ready")
    ord_dve, ord_act = sem("vector_order4"), sem("scalar_order4")
    ones = M["misc"][:, 3072 - P:3072]

    with nc.Block() as block:
        @block.sync
        def _(sp):
            def load_x(c):
                if c >= 2:
                    sp.wait_ge(h_ready, 2 * (c - 1))
                sp.dma_start(x_in[:, c % 2, :], A["x"][0, c * P:(c + 1) * P, :]).then_inc(s_x[c % 2], 16)

            load_x(0)
            load_x(1)
            sp.dma_start(ffn_rows, A["ffn_norm_w"][0].partition_broadcast(P)).then_inc(s_ffn, 16)
            sp.dma_start(rw[:, :, 0:4], A["router_g_w"][0].rearrange("(k p) n -> p k n", p=P)).then_inc(s_route, 16)
            sp.dma_start(rw[:, :, 4:NR], A["router_e_w"][0].rearrange("(k p) n -> p k n", p=P)).then_inc(s_route, 16)
            sp.dma_start(bias[:, 0:4], A["router_g_b"][0].partition_broadcast(P)).then_inc(s_route, 16)
            sp.dma_start(bias[:, 4:NR], A["router_e_b"][0].partition_broadcast(P)).then_inc(s_route, 16)
            sp.dma_start(edges, C["slot_edges"]).then_inc(s_route, 16)
            sp.dma_start(iota, C["iota"]).then_inc(s_route, 16)
            sp.dma_start(token, C["token"]).then_inc(s_route, 16)
            sp.dma_start(tri_strict, C["tri_strict"]).then_inc(s_route, 16)
            sp.dma_start(before_, C["before"].partition_broadcast(P)).then_inc(s_route, 16)
            load_expert(sp, M, A, 0, 0)
            for c in range(NT):
                if c + 2 < NT:
                    load_x(c + 2)
                sp.wait_ge(hn_ready, c + 1)
                sp.dma_start(M["hn_dram"][c * P:(c + 1) * P, :], hn[:, c % 2, :]).then_inc(s_hn[c % 2], 16)
            load_expert(sp, M, A, 1, 1)
            load_expert(sp, M, A, 2, 2)

        @block.gpsimd
        def _(pool):
            nc.gpsimd.memset(ones, 1.0).then_inc(ones_set, 1)
            pool.wait_ge(tab_copied, 1)
            nc.gpsimd.tensor_copy(M["tok_idx"][:, 0:1], M["tok_table"][:, 0:1]).then_inc(M["idx_ready"], 1)
            for b in range(2):
                pool.wait_ge(s_hn[b], 16 * NT // 2)
            pool.wait_ge(M["idx_ready"], 1)
            nc.gpsimd.indirect_dma_start(M["big_w"][:, 0:D], None, M["hn_dram"],
                                         bass.IndirectOffsetOnAxis(ap=M["tok_idx"][:, 0:1], axis=0))\
                .then_inc(M["s_rows"][0], 16)

        @block.tensor
        def _(pe):
            def first_cat_transposes():
                pe.wait_ge(cat_ready, 3)
                for k in range(KD):
                    src = o_att[:, 0, k * P:(k + 1) * P] if k < 4 else o_ssm[:, 0, (k - 4) * P:(k - 3) * P]
                    last = nc.tensor.transpose(ps[:, k // 4, (k % 4) * P:(k % 4 + 1) * P], src, ident[:, :])
                    if k % 4 == 3:
                        last.then_inc(cat_full, 1)

            def project_out(c):
                pe.wait_ge(cat_transposed, c + 1)
                for half in range(2):
                    if c >= 1:
                        pe.wait_ge(h_ready, 2 * (c - 1) + half + 1)
                    for k in range(KD):
                        last = nc.tensor.matmul(ps[:, 2 + half, :], catT[:, c % 2, k, :],
                                                w_out[:, k, half * BANK:(half + 1) * BANK], start=(k == 0), stop=(k == KD - 1))
                    last.then_inc(o_full, 1)
                    if half == 0 and c >= 2:
                        if c == 2:
                            pe.wait_ge(s_route, 9 * 16)
                        route(c - 2)

            def hn_transposes(c):
                pe.wait_ge(hn_ready, c + 1)
                if c >= 1:
                    pe.wait_ge(hnT_evac, 2 * c)
                for k in range(KD):
                    last = nc.tensor.transpose(ps[:, 4 + k // 4, (k % 4) * P:(k % 4 + 1) * P],
                                               hn[:, c % 2, k * P:(k + 1) * P], ident[:, :])
                    if k % 4 == 3:
                        last.then_inc(hnT_full, 1)

            def route(c):
                pe.wait_ge(hnT_evac, 2 * (c + 1))
                for k in range(KD):
                    last = nc.tensor.matmul(ps[:, 6, c * NR:(c + 1) * NR], hnT[:, k, :], rw[:, k, :],
                                            start=(k == 0), stop=(k == KD - 1))
                last.then_inc(lg_full, 1)

            first_cat_transposes()
            pe.wait_ge(M["w_out_scaled"], KD)
            for c in range(NT):
                project_out(c)
                if c >= 1:
                    hn_transposes(c - 1)
            route(NT - 2)
            hn_transposes(NT - 1)
            route(NT - 1)
            pe.wait_ge(ones_set, 1)
            pe.wait_ge(route_in, 1)
            nc.tensor.matmul(ps[:, 7, 0:P], tri_strict, both, start=True, stop=True)
            nc.tensor.matmul(ps[:, 7, P:2 * P], ones, both, start=True, stop=True).then_inc(route_out, 1)
            pe.wait_ge(tab_in, 3)
            for i in range(2 * NT):
                last = nc.tensor.matmul(ps[:, 6, 0:2 * TABLE], place_hot[:, i, :], values[:, i, :],
                                        start=(i == 0), stop=(i == 2 * NT - 1))
            last.then_inc(tab_out, 1)

        @block.scalar
        def _(act):
            o = Order(act, ord_act)
            nc.scalar.preload_act_table_set("natural_log_exp_and_others")
            o.done(nc.scalar.activation(rs_ssm, M["ss_ssm"], ACT.Ln, scale=1.0 / 256, bias=M["eps"][:, 0:1]))
            o.done(nc.scalar.activation(rs_ssm, rs_ssm, ACT.Exp, scale=-0.5))

            def scale_cat(c):
                nc.scalar.activation(o_att[:, c, :], o_att[:, c, :], ACT.Copy, scale=rs_att[:, c:c + 1]).then_inc(cat_ready, 1)
                for g in range(NG):
                    v = o_ssm[:, c, g * 256:(g + 1) * 256]
                    nc.scalar.activation(v, v, ACT.Copy, scale=rs_ssm[:, NG * c + g:NG * c + g + 1]).then_inc(cat_ready, 1)

            def h_stats(c):
                act.wait_ge(h_ready, 2 * (c + 1))
                o.done(nc.scalar.activation(junk, h[:, c, :], ACT.Square, accum_out=ss_h[:, c:c + 1]))
                o.done(nc.scalar.activation(rs_h[:, c:c + 1], ss_h[:, c:c + 1], ACT.Ln, scale=1.0 / D, bias=M["eps"][:, 0:1]))
                nc.scalar.activation(rs_h[:, c:c + 1], rs_h[:, c:c + 1], ACT.Exp, scale=-0.5).then_inc(rs_ready, 1)

            scale_cat(0)
            scale_cat(1)
            for c in range(NT):
                if c + 2 < NT:
                    scale_cat(c + 2)
                h_stats(c)
            act.wait_ge(act_plan, 1)
            nc.scalar.activation(g4, g4, ACT.Exp).then_inc(act_plan, 1)
            act.wait_ge(act_plan, 3)
            nc.scalar.activation(d21, d21, ACT.Exp).then_inc(act_plan, 1)

        @block.vector
        def _(dve):
            o = Order(dve, ord_dve)
            tt, ts = nc.vector.tensor_tensor, nc.vector.tensor_scalar

            def cat_transpose(c):
                if c == 0:
                    for j in range(2):
                        dve.wait_ge(cat_full, j + 1)
                        last = nc.vector.tensor_copy(catT[:, 0, 4 * j:4 * j + 4, :],
                                                     ps[:, j, :].rearrange("p (k t) -> p k t", k=4))
                    last.then_inc(cat_transposed, 1)
                    return
                dve.wait_ge(cat_ready, 3 * (c + 1))
                for j, mixer in enumerate((o_att, o_ssm)):
                    last = transpose_chunks(nc, catT[:, c % 2, 4 * j:4 * j + 4, :],
                                            mixer[:, c, :].rearrange("p (k n) -> p k n", k=4))
                last.then_inc(cat_transposed, 1)

            def residual(c):
                dve.wait_ge(s_x[c % 2], 16 * (c // 2 + 1))
                for half in range(2):
                    dve.wait_ge(o_full, 2 * c + half + 1)
                    n = slice(half * BANK, (half + 1) * BANK)
                    tt(h[:, c, n], ps[:, 2 + half, :], x_in[:, c % 2, n], ALU.add).then_inc(h_ready, 1)

            def normalise(c):
                dve.wait_ge(rs_ready, c + 1)
                if c >= 2:
                    dve.wait_ge(s_hn[c % 2], 16 * (c // 2))
                    dve.wait_ge(hnT_full, 2 * (c - 1))
                if c == 0:
                    dve.wait_ge(s_ffn, 16)
                nc.vector.scalar_tensor_tensor(hn[:, c % 2, :], h[:, c, :], rs_h[:, c:c + 1], ffn_rows, ALU.mult, ALU.mult)\
                    .then_inc(hn_ready, 1)

            def hn_evacuate(c):
                if c >= 1:
                    dve.wait_ge(lg_full, c)
                for j in range(2):
                    dve.wait_ge(hnT_full, 2 * c + j + 1)
                    nc.vector.tensor_copy(hnT[:, 4 * j:4 * j + 4, :], ps[:, 4 + j, :].rearrange("p (k t) -> p k t", k=4))\
                        .then_inc(hnT_evac, 1)

            cat_transpose(0)
            cat_transpose(1)
            for c in range(NT):
                residual(c)
                if c >= 1:
                    hn_evacuate(c - 1)
                normalise(c)
                if c + 2 < NT:
                    cat_transpose(c + 2)
            hn_evacuate(NT - 1)

            dve.wait_ge(lg_full, NT)
            dve.wait_ge(s_route, 9 * 16)
            o.done(tt(lg, ps[:, 6, 0:NT * NR].rearrange("p (c n) -> p c n", c=NT),
                      bias.unsqueeze(1).broadcast_to([P, NT, NR]), ALU.add))
            G = lg[:, :, 0:4]
            q4 = lambda v: v.rearrange("p (c j i) -> p c j i", c=NT, j=4)

            def rank(v, r):
                vi = v.unsqueeze(2).broadcast_to([P, NT, 4, 4])
                vj = v.unsqueeze(3).broadcast_to([P, NT, 4, 4])
                o.mark(tt(q4(c1), vi, vj, ALU.is_gt))
                o.done(tt(q4(c2), vi, vj, ALU.is_equal))
                o.done(tt(q4(c2), q4(c2), before[:, 0:4, 0:4].unsqueeze(1).broadcast_to([P, NT, 4, 4]), ALU.mult))
                o.done(tt(c1, c1, c2, ALU.add))
                o.done(nc.vector.tensor_reduce(r, q4(c1), AX.X, ALU.add))

            o.done(nc.vector.tensor_reduce(gmax, G, AX.X, ALU.max))
            tt(g4, G, gmax.unsqueeze(2).broadcast_to([P, NT, 4]), ALU.subtract).then_inc(act_plan, 1)
            rank(G, r4)
            o.done(ts(oh_g, r4, 0.0, None, ALU.is_equal))
            o.done(tt(q4(t4), lg[:, :, 4:NR].rearrange("p c (g e) -> p c g e", g=4),
                      oh_g.unsqueeze(3).broadcast_to([P, NT, 4, 4]), ALU.mult))
            o.done(nc.vector.tensor_reduce(e4, q4(t4).rearrange("p c g e -> p c e g"), AX.X, ALU.add))
            rank(e4, r4)
            o.mark(ts(oh1, r4, 0.0, None, ALU.is_equal))
            o.done(ts(oh2, r4, 1.0, None, ALU.is_equal))
            for k, oh in enumerate((oh1, oh2)):
                o.mark(tt(q4(H[k]), oh_g.unsqueeze(3).broadcast_to([P, NT, 4, 4]),
                          oh.unsqueeze(2).broadcast_to([P, NT, 4, 4]), ALU.mult))
            o.wait()
            tt(both, H[0], H[1], ALU.add).then_inc(route_in, 1)
            for oh, lv in ((oh1, l1), (oh2, l2)):
                o.done(tt(r4, e4, oh, ALU.mult))
                o.done(nc.vector.tensor_reduce(lv, r4, AX.X, ALU.add))
            dve.wait_ge(act_plan, 2)
            tt(d21, l2, l1, ALU.subtract).then_inc(act_plan, 1)
            o.done(nc.vector.tensor_reduce(gp, g4, AX.X, ALU.add))
            o.done(nc.vector.reciprocal(gp, gp))
            dve.wait_ge(act_plan, 4)
            o.done(ts(spare, d21, 1.0, None, ALU.add))
            o.done(nc.vector.reciprocal(spare, spare))
            o.done(tt(wk[:, 0:NT], spare, gp, ALU.mult))
            o.done(tt(wk[:, NT:2 * NT], wk[:, 0:NT], d21, ALU.mult))
            dve.wait_ge(route_out, 1)
            o.done(nc.vector.memset(base[:, 0:N_EXP], 0.0))
            for c in range(NT):
                o.done(tt(base[:, (c + 1) * N_EXP:(c + 2) * N_EXP], ps[:, 7, P + c * N_EXP:P + (c + 1) * N_EXP],
                          base[:, c * N_EXP:(c + 1) * N_EXP], ALU.add))
            n_e = base[:, NT * N_EXP:]
            o.done(tt(c1.rearrange("p (e k) -> p e k", k=NT), n_e.unsqueeze(2).broadcast_to([P, N_EXP, NT]),
                      edges[:, 0:NT].unsqueeze(1).broadcast_to([P, N_EXP, NT]), ALU.is_gt))
            o.done(nc.vector.tensor_reduce(tiles, c1.rearrange("p (e k) -> p e k", k=NT), AX.X, ALU.add))
            g16 = ge.rearrange("p i s -> p (i s)")[:, 0:256].rearrange("p (j i) -> p j i", j=N_EXP)
            o.done(tt(g16, before, tiles.unsqueeze(1).broadcast_to([P, N_EXP, N_EXP]), ALU.mult))
            o.done(nc.vector.tensor_reduce(start, g16, AX.X, ALU.add))
            o.mark(tt(end_, start, tiles, ALU.add))
            o.done(ts(st128, start, float(P), None, ALU.mult))
            pos3 = pos.rearrange("p (c e) -> p c e", c=NT)
            o.done(tt(pos, ps[:, 7, 0:P], base[:, 0:P], ALU.add))
            o.done(tt(pos3, pos3, st128.unsqueeze(1).broadcast_to([P, NT, N_EXP]), ALU.add))
            for k in range(2):
                o.done(tt(t4, H[k], pos, ALU.mult))
                o.done(nc.vector.tensor_reduce(posk[:, k * NT:(k + 1) * NT], t4.rearrange("p (c e) -> p c e", c=NT),
                                               AX.X, ALU.add))
            o.mark(nc.vector.tensor_copy(M["slot_pos"], posk))
            o.done(tt(ge, posk.unsqueeze(2).broadcast_to([P, 2 * NT, EDGES]),
                      edges.unsqueeze(1).broadcast_to([P, 2 * NT, EDGES]), ALU.is_ge))
            o.mark(tt(hot, ge[:, :, 0:TABLE], ge[:, :, 1:EDGES], ALU.subtract))
            o.done(nc.vector.tensor_reduce(slot, ge[:, :, 1:EDGES], AX.X, ALU.add))
            o.done(nc.vector.scalar_tensor_tensor(place, slot, -float(P), posk, ALU.mult, ALU.add))
            tt(place_hot, iota.unsqueeze(1).broadcast_to([P, 2 * NT, P]), place.unsqueeze(2).broadcast_to([P, 2 * NT, P]),
               ALU.is_equal).then_inc(tab_in, 1)
            v3 = values.rearrange("p (k c) n -> p k c n", k=2)
            tt(v3[:, :, :, 0:TABLE], hot.rearrange("p (k c) n -> p k c n", k=2),
               token.unsqueeze(1).unsqueeze(3).broadcast_to([P, 2, NT, TABLE]), ALU.mult).then_inc(tab_in, 1)
            tt(values[:, :, TABLE:], hot, wk.unsqueeze(2).broadcast_to([P, 2 * NT, TABLE]), ALU.mult).then_inc(tab_in, 1)
            o.done(ts(e_cmp.rearrange("p s e -> p (s e)")[:, 0:TABLE], edges[0:1, 0:TABLE], 1.0 / P, None, ALU.mult))
            o.done(nc.vector.tensor_copy(e_sum, e_cmp.rearrange("p s e -> p (s e)")[:, 0:TABLE]))
            o.done(tt(e_cmp, end_[0:1, :].unsqueeze(1).broadcast_to([1, TABLE, N_EXP]),
                      e_sum.unsqueeze(2).broadcast_to([1, TABLE, N_EXP]), ALU.is_le))
            o.done(nc.vector.tensor_reduce(e_sum, e_cmp, AX.X, ALU.add))
            o.done(ts(e_sum, e_sum, float(N_EXP - 1), None, ALU.min))
            places = M["slot_places"]
            o.mark(ts(places[:, :, 0], e_sum, 1.0, None, ALU.add))
            o.done(ts(e_ring, e_sum, float(RING), None, ALU.is_ge))
            for j in range(2 * RING, N_EXP, RING):
                o.done(nc.vector.scalar_tensor_tensor(e_ring, e_sum, float(j), e_ring, ALU.is_ge, ALU.add))
            o.done(nc.vector.scalar_tensor_tensor(e_ring, e_ring, -float(RING), e_sum, ALU.mult, ALU.add))
            o.mark(ts(places[:, :, 1], e_ring, float(GU_COLS), None, ALU.mult))
            o.done(ts(places[:, 1:TABLE, 2], e_ring[:, 0:TABLE - 1], float(D_COLS), None, ALU.mult))
            o.mark(nc.vector.memset(places[:, 0:1, 2], 0))
            o.mark(nc.vector.tensor_copy(M["expert_end"], end_[0:1, :]))
            o.done(ts(e_ring[:, 0:LOOP_PAIRS], edges[0:1, 0:LOOP_PAIRS], 2.0 / P, float(SLOTS_HEAD), ALU.mult, ALU.add))
            o.done(tt(e_ring[:, 0:LOOP_PAIRS], e_ring[:, 0:LOOP_PAIRS],
                      end_[0:1, N_EXP - 1:N_EXP].broadcast_to([1, LOOP_PAIRS]), ALU.is_lt))
            o.done(nc.vector.tensor_reduce(e_ring[:, LOOP_PAIRS:LOOP_PAIRS + 1], e_ring[:, 0:LOOP_PAIRS], AX.X, ALU.add))
            o.mark(ts(M["last_slot"], e_ring[:, LOOP_PAIRS:LOOP_PAIRS + 1], 2.0, float(SLOTS_HEAD - 1), ALU.mult, ALU.add))
            dve.wait_ge(tab_out, 1)
            nc.vector.tensor_copy(M["tok_table"], ps[:, 6, 0:TABLE]).then_inc(tab_copied, 1)
            o.mark(nc.vector.tensor_copy(M["w_table"], ps[:, 6, TABLE:2 * TABLE]))


def experts(nc, N, M, A, C, out):
    sem = N.sem
    ps = M["ps"]
    w = M["big_w"]
    at = [0]

    def pair(n):
        at[0] += 2 * n
        return w[:, at[0] - 2 * n:at[0]].rearrange("p (b n) -> p b n", b=2)

    xg, xT_, y, hid, silu, hT_ = pair(D), pair(D), pair(D), pair(D_EXP), pair(D_EXP), pair(D_EXP)
    xT = xT_.rearrange("p b (k t) -> p b k t", k=KD)
    hT = hT_.rearrange("p b (f t) -> p b f t", f=D_EXP // P)
    ring_gu, ring_d = M["ring_gu"], M["ring_d"]
    NF = D_EXP // P

    s_rows = M["s_rows"]
    s_y = [sem("slot_stored0"), sem("slot_stored1")]
    idx_ready, ready = M["idx_ready"], sem("experts_ready")
    gather_go = sem("gather_go")
    xt_ready = sem("slot_xT_ready")
    gu_full, silu_ready, h_ready = sem("gate_up_full"), sem("silu_ready"), sem("hidden_ready")
    ht_ready = sem("slot_hT_ready")
    y_full, y_ready = sem("slot_y_full"), sem("slot_y_ready")

    def over_slots(engine, step):
        last = engine.value_load(M["last_slot"], min_val=PAIRS // P, max_val=SLOTS - 1)
        for s in range(SLOTS_HEAD):
            step(s, s % 2, s)
        with engine.Fori(0, LOOP_PAIRS) as i:
            with engine.If(i * 2 + SLOTS_HEAD < last):
                step(i * 2 + SLOTS_HEAD, 1, SLOTS_HEAD)
                step(i * 2 + SLOTS_HEAD + 1, 0, SLOTS_HEAD)
        return last

    with nc.Block() as block:
        @block.sync
        def _(sp):
            s_w = M["s_expert"]
            sp.sem_inc(y_full, 1)
            for e in range(2):
                sp.wait_ge(s_w[e], 48)
                sp.sem_inc(ready, 1)

            def next_expert(e, r, turn):
                end = sp.value_load(M["expert_end"][0:1, bass.ds(e - RING, 1)], min_val=0, max_val=SLOTS)
                sp.wait_ge(s_w[(r + RING - 1) % RING], 48 * turn if r == 0 else 48 * (turn + 1))
                sp.sem_inc(ready, 1)
                sp.wait_ge(y_full, end + 1)
                load_expert(sp, M, A, e, r)

            with sp.Fori(0, 4) as i:
                for r in range(RING):
                    next_expert(i * RING + RING + r, r, i + 1)
            next_expert(N_EXP - 1, 0, 5)
            sp.wait_ge(s_w[0], 48 * 6)
            sp.sem_inc(ready, 1)

        @block.gpsimd
        def _(pool):
            def gather(s, b, first):
                if first >= 2:
                    pool.wait_ge(xt_ready, s - 1)
                nc.gpsimd.tensor_copy(M["tok_idx"][:, b:b + 1], M["tok_table"][:, bass.ds(s, 1)]).then_inc(idx_ready, 1)
                pool.wait_ge(idx_ready, s + 1)
                pool.sem_inc(gather_go, 1)
                nc.gpsimd.indirect_dma_start(xg[:, b, :], None, M["hn_dram"],
                                             bass.IndirectOffsetOnAxis(ap=M["tok_idx"][:, b:b + 1], axis=0))\
                    .then_inc(s_rows[b], 16)

            over_slots(pool, lambda s, b, first: gather(s + 1, 1 - b, first + 1))

        @block.tensor
        def _(pe):
            def place_of(s, n, top):
                return pe.value_load(M["slot_places"][0:1, bass.ds(s, 1), n:n + 1], min_val=0, max_val=top)

            def gate_up(s, b, first, turn, at):
                pe.wait_ge(ready, turn)
                pe.wait_ge(xt_ready, s + 1)
                if first >= 2:
                    pe.wait_ge(h_ready, s - 1)
                for k in range(KD):
                    last = nc.tensor.matmul(ps[:, 2 + b, :], xT[:, b, k, :], ring_gu[:, bass.ds(at + k * 2 * D_EXP, BANK)],
                                            start=(k == 0), stop=(k == KD - 1))
                last.then_inc(gu_full, 1)

            def down(s, b, first, at):
                pe.wait_ge(ht_ready, s + 1)
                if first >= 1:
                    pe.wait_ge(y_ready, s)
                for half in range(2):
                    for f in range(NF):
                        last = nc.tensor.matmul(ps[:, 5 + half, :], hT[:, b, f, :],
                                                ring_d[:, bass.ds(at + f * D + half * BANK, BANK)],
                                                start=(f == 0), stop=(f == NF - 1))
                last.then_inc(y_full, 1)

            def step(s, b, first):
                turn = place_of(s, 0, N_EXP)
                gu_at = place_of(s, 1, (RING - 1) * GU_COLS)
                down_at = place_of(s, 2, (RING - 1) * D_COLS)
                gate_up(s, b, first, turn, gu_at)
                if first >= 1:
                    down(s - 1, 1 - b, first - 1, down_at)

            last_slot = over_slots(pe, step)
            down(last_slot, 0, SLOTS_HEAD, place_of(last_slot + 1, 2, (RING - 1) * D_COLS))

        @block.scalar
        def _(act):
            nc.scalar.preload_act_table(ACT.Silu)

            act.wait_ge(M["s_zero_slots"], 16 * (SLOTS - SLOTS_SURE))

            def activate(s, b, first):
                act.wait_ge(gu_full, s + 1)
                if first >= 2:
                    act.wait_ge(h_ready, s - 1)
                nc.scalar.activation(silu[:, b, :], ps[:, 2 + b, 0:D_EXP], ACT.Silu).then_inc(silu_ready, 1)

            def put_out(s, b, first):
                act.wait_ge(y_full, s + 2)
                if first >= 2:
                    act.wait_ge(s_y[b], (s - b) * 8)
                nc.scalar.activation(y[:, b, :], ps[:, 5:7, :].rearrange("p a n -> p (a n)"), ACT.Copy).then_inc(y_ready, 1)
                act.wait_ge(y_ready, s + 1)
                act.dma_start(M["y_dram"][bass.ds(s * P, P), :], y[:, b, :]).then_inc(s_y[b], 16)

            def step(s, b, first):
                activate(s, b, first)
                if first >= 1:
                    put_out(s - 1, 1 - b, first - 1)

            last_slot = over_slots(act, step)
            put_out(last_slot, 0, SLOTS_HEAD)
            act.wait_ge(s_y[0], (last_slot + 2) * 8)
            act.wait_ge(s_y[1], last_slot * 8)
            act.sem_inc(M["y_stored"], 1)

        @block.vector
        def _(dve):
            def transpose_x(s, b, first):
                dve.wait_ge(s_rows[b], (s + (2 - b)) * 8)
                if first >= 2:
                    dve.wait_ge(gu_full, s - 1)
                transpose_chunks(nc, xT[:, b], xg[:, b, :].rearrange("p (k n) -> p k n", k=KD)).then_inc(xt_ready, 1)

            def hidden(s, b, first):
                dve.wait_ge(silu_ready, s + 1)
                if first >= 2:
                    dve.wait_ge(ht_ready, s - 1)
                nc.vector.scalar_tensor_tensor(hid[:, b, :], silu[:, b, :], M["w_table"][:, bass.ds(s, 1)],
                                               ps[:, 2 + b, D_EXP:2 * D_EXP], ALU.mult, ALU.mult).then_inc(h_ready, 1)

            def transpose_h(s, b, first):
                dve.wait_ge(h_ready, s + 1)
                if first >= 2:
                    dve.wait_ge(y_full, s)
                transpose_chunks(nc, hT[:, b], hid[:, b, :].rearrange("p (f n) -> p f n", f=NF)).then_inc(ht_ready, 1)

            transpose_x(0, 0, 0)

            def step(s, b, first):
                transpose_x(s + 1, 1 - b, first + 1)
                hidden(s, b, first)
                transpose_h(s, b, first)

            over_slots(dve, step)


def combine(nc, N, M, A, C, out):
    sem = N.sem
    s_in = [sem(f"pair_rows{i}") for i in range(4)]
    done, s_out = sem("tile_summed"), sem("out_stored")
    ord_dve = sem("vector_order6")
    h = M["conv"][:, :, 0:D]

    def rows(c, k):
        i = 2 * c + k
        return M["ring_gu"][:, i * D:(i + 1) * D] if i < 12 else M["big_w"][:, (i - 12) * D:(i - 11) * D]

    with nc.Block() as block:
        @block.gpsimd
        def _(pool):
            pool.wait_ge(M["y_stored"], 1)
            for c in range(NT):
                if c >= 4:
                    pool.wait_ge(s_in[c % 4], 32)
                for k in range(2):
                    pool.indirect_dma_start(rows(c, k), None, M["y_dram"],
                                            bass.IndirectOffsetOnAxis(ap=M["slot_pos"][:, k * NT + c:k * NT + c + 1], axis=0))\
                        .then_inc(s_in[c % 4], 16)

        @block.vector
        def _(dve):
            o = Order(dve, ord_dve)
            for c in range(NT):
                dve.wait_ge(s_in[c % 4], 32 * (c // 4 + 1))
                o.done(nc.vector.tensor_tensor(h[:, c, :], h[:, c, :], rows(c, 0), ALU.add))
                nc.vector.tensor_tensor(h[:, c, :], h[:, c, :], rows(c, 1), ALU.add).then_inc(done, 1)

        @block.sync
        def _(sp):
            for c in range(NT):
                sp.wait_ge(done, c + 1)
                sp.dma_start(out[0, c * P:(c + 1) * P, :], h[:, c, :]).then_inc(s_out, 16)
            sp.wait_ge(s_out, 16 * NT)


def kernel(**inputs):
    import numpy as np
    import concourse.bacc as bacc
    from concourse.bass_utils import run_bass_kernel_spmd

    nc = bacc.Bacc("TRN2", target_bir_lowering=False, num_devices=1)
    arrays, A, C = {}, {}, {}
    for name, a in inputs.items():
        a = np.ascontiguousarray(a)
        arrays[f"in_{name}"] = a
        A[name] = nc.dram_tensor(f"in_{name}", a.shape, mybir.dt.from_np(a.dtype), kind="ExternalInput").ap()
    for name, a in shape_constants().items():
        a = np.ascontiguousarray(a)
        arrays[f"const_{name}"] = a
        C[name] = nc.dram_tensor(f"const_{name}", a.shape, mybir.dt.from_np(a.dtype), kind="ExternalInput").ap()
    out = nc.dram_tensor("out", (1, S, D), F32, kind="ExternalOutput").ap()
    build(nc, A, C, out)
    return run_bass_kernel_spmd(nc, [arrays], core_ids=[0]).results[0]["out"]
```
